# Optimizing a Trainium2 kernel written in Bass

```python
import jax, jax.numpy as jnp
from jax import lax
import numpy as np

D_MODEL = 1024
BATCH = 1
SEQ = 256
DEPTH = 4

N_MIXERS = 3
SWA_HEADS = 16
SWA_KV_HEADS = 4
SWA_HEAD_DIM = 64
SWA_WINDOW = 128
SWA_QKV_DIM = (SWA_HEADS + 2 * SWA_KV_HEADS) * SWA_HEAD_DIM
HGRN_HEADS = 8
HGRN_EXPAND = 128
HGRN_HEAD_DIM = D_MODEL // HGRN_HEADS
HGRN_CHUNK = 64
HGRN_IN_DIM = 2 * HGRN_HEADS * HGRN_EXPAND + 2 * HGRN_HEADS * HGRN_HEAD_DIM
FOX_HEADS = 16
FOX_HEAD_DIM = 64
FOX_BLOCK = 128
FOX_IN_DIM = 3 * FOX_HEADS * FOX_HEAD_DIM + FOX_HEADS
FOX_FORGET_BIAS_INIT = 2.0
D_FF = 4 * D_MODEL
EPS = 1e-6

N_A = (DEPTH + 2) // 3
N_B = (DEPTH + 1) // 3
N_C = DEPTH // 3

kernel_name = "hybrid_swa_hgrn2_fox_trunk"

def rms_norm(x, g):
    xf = x.astype(jnp.float32)
    y = xf * lax.rsqrt(jnp.mean(xf * xf, axis=-1, keepdims=True) + EPS)
    return (y * g.astype(jnp.float32)).astype(x.dtype)

def swa_sink_attention(h, w_qkv, b_qkv, sinks, w_o):
    B, T, _ = h.shape
    W, KV, dh = SWA_WINDOW, SWA_KV_HEADS, SWA_HEAD_DIM
    G = SWA_HEADS // KV
    nb = T // W
    qkv = h @ w_qkv + b_qkv
    q, k, v = jnp.split(qkv, [SWA_HEADS * dh, (SWA_HEADS + KV) * dh], axis=-1)
    q = q.reshape(B, nb, W, KV, G, dh) * (dh ** -0.5)
    k = k.reshape(B, nb, W, KV, dh)
    v = v.reshape(B, nb, W, KV, dh)
    k_band = jnp.concatenate([jnp.pad(k[:, :-1], ((0, 0), (1, 0), (0, 0), (0, 0), (0, 0))), k], axis=2)
    v_band = jnp.concatenate([jnp.pad(v[:, :-1], ((0, 0), (1, 0), (0, 0), (0, 0), (0, 0))), v], axis=2)
    s = jnp.einsum('bnqhgd,bnkhd->bnhgqk', q, k_band).astype(jnp.float32)
    qi = jnp.arange(W)[:, None]
    kk = jnp.arange(2 * W)[None, :]
    rel = qi + W - kk
    in_window = (rel >= 0) & (rel < W)
    blk = jnp.arange(nb)[:, None, None]
    mask = in_window[None] & ((blk > 0) | (kk[None] >= W))
    s = jnp.where(mask[None, :, None, None], s, -jnp.inf)
    sink = sinks.astype(jnp.float32).reshape(KV, G)[None, None, :, :, None, None]
    sink = jnp.broadcast_to(sink, s.shape[:-1] + (1,))
    p = jax.nn.softmax(jnp.concatenate([s, sink], axis=-1), axis=-1)[..., :-1]
    o = jnp.einsum('bnhgqk,bnkhd->bnqhgd', p.astype(v.dtype), v_band)
    return o.reshape(B, T, SWA_HEADS * dh) @ w_o

def hgrn2_mixer(h, w_in, lb, g_norm, w_o):
    B, T, _ = h.shape
    H, K, V, C = HGRN_HEADS, HGRN_EXPAND, HGRN_HEAD_DIM, HGRN_CHUNK
    nc = T // C
    proj = h @ w_in
    q, f_logit, i_in, g = jnp.split(proj, [H * K, 2 * H * K, 2 * H * K + H * V], axis=-1)
    f = lb + (1.0 - lb) * jax.nn.sigmoid(f_logit.astype(jnp.float32))
    log_f = jnp.log(f)
    k = 1.0 - f

    def to_chunks(a, d):
        return a.astype(jnp.float32).reshape(B, nc, C, H, d).transpose(1, 0, 3, 2, 4)

    xs = (to_chunks(jax.nn.silu(q), K), to_chunks(k, K), to_chunks(i_in, V), to_chunks(log_f, K))
    causal = jnp.tril(jnp.ones((C, C), dtype=bool))[:, :, None]

    def step(S, inp):
        qc, kc, vc, gc = inp
        bcum = jnp.cumsum(gc, axis=2)
        diff = jnp.where(causal, bcum[:, :, :, None, :] - bcum[:, :, None, :, :], -jnp.inf)
        A = jnp.einsum('bhtk,bhsk,bhtsk->bhts', qc, kc, jnp.exp(diff))
        o = jnp.einsum('bhts,bhsv->bhtv', A, vc) + jnp.einsum('bhtk,bhkv->bhtv', qc * jnp.exp(bcum), S)
        b_last = bcum[:, :, -1]
        S_new = jnp.exp(b_last)[..., None] * S + jnp.einsum(
            'bhsk,bhsv->bhkv', kc * jnp.exp(b_last[:, :, None, :] - bcum), vc)
        return S_new, o

    S0 = jnp.zeros((B, H, K, V), jnp.float32)
    _, o = lax.scan(step, S0, xs)
    o = o.transpose(1, 0, 3, 2, 4).reshape(B, T, H, V)
    o = o * lax.rsqrt(jnp.mean(o * o, axis=-1, keepdims=True) + EPS)
    o = o.reshape(B, T, H * V) * g_norm.astype(jnp.float32) * jax.nn.silu(g.astype(jnp.float32))
    return o.astype(h.dtype) @ w_o

def fox_attention(h, w_in, b_in, w_o):
    B, T, _ = h.shape
    H, dh, Q = FOX_HEADS, FOX_HEAD_DIM, FOX_BLOCK
    nb = T // Q
    proj = h @ w_in + b_in
    q, k, v, f_logit = jnp.split(proj, [H * dh, 2 * H * dh, 3 * H * dh], axis=-1)
    log_f = jax.nn.log_sigmoid(f_logit.astype(jnp.float32))
    c = jnp.cumsum(log_f, axis=1).transpose(0, 2, 1)
    q = q.reshape(B, T, H, dh) * (dh ** -0.5)
    k = k.reshape(B, T, H, dh)
    v = v.reshape(B, T, H, dh)
    q_blocks = q.reshape(B, nb, Q, H, dh).transpose(1, 0, 2, 3, 4)
    c_blocks = c.reshape(B, H, nb, Q).transpose(2, 0, 1, 3)
    pos_blocks = jnp.arange(T).reshape(nb, Q)
    kpos = jnp.arange(T)

    def block(args):
        qb, cb, pb = args
        s = jnp.einsum('bqhd,bkhd->bhqk', qb, k).astype(jnp.float32)
        s = s + (cb[..., :, None] - c[..., None, :])
        s = jnp.where((pb[:, None] >= kpos[None, :])[None, None], s, -jnp.inf)
        p = jax.nn.softmax(s, axis=-1)
        return jnp.einsum('bhqk,bkhd->bqhd', p.astype(v.dtype), v)

    o = lax.map(block, (q_blocks, c_blocks, pos_blocks))
    o = o.transpose(1, 0, 2, 3, 4).reshape(B, T, H * dh)
    return o @ w_o

def setup_inputs(seed: int = 0) -> dict:
    key = jax.random.key(seed)
    ks = jax.random.split(key, 18)
    f32 = jnp.float32

    def nrm(k, shape, fan_in):
        return jax.random.normal(k, shape, f32) * (fan_in ** -0.5)

    def gain(k, shape):
        return 1.0 + 0.02 * jax.random.normal(k, shape, f32)

    fox_b_in = 0.02 * jax.random.normal(ks[16], (N_C, FOX_IN_DIM), f32)
    fox_b_in = fox_b_in.at[:, 3 * FOX_HEADS * FOX_HEAD_DIM:].add(FOX_FORGET_BIAS_INIT)
    return {
        "x": jax.random.normal(ks[0], (BATCH, SEQ, D_MODEL), f32),
        "norm_mix": gain(ks[1], (DEPTH, D_MODEL)),
        "norm_mlp": gain(ks[2], (DEPTH, D_MODEL)),
        "norm_final": gain(ks[3], (D_MODEL,)),
        "w_up": nrm(ks[4], (DEPTH, D_MODEL, D_FF), D_MODEL),
        "w_down": nrm(ks[5], (DEPTH, D_FF, D_MODEL), D_FF),
        "swa_w_qkv": nrm(ks[6], (N_A, D_MODEL, SWA_QKV_DIM), D_MODEL),
        "swa_b_qkv": 0.02 * jax.random.normal(ks[7], (N_A, SWA_QKV_DIM), f32),
        "swa_sinks": 0.5 * jax.random.normal(ks[8], (N_A, SWA_HEADS), f32),
        "swa_w_o": nrm(ks[9], (N_A, SWA_HEADS * SWA_HEAD_DIM, D_MODEL), SWA_HEADS * SWA_HEAD_DIM),
        "hgrn_w_in": nrm(ks[10], (N_B, D_MODEL, HGRN_IN_DIM), D_MODEL),
        "hgrn_lb_logits": 0.1 * jax.random.normal(ks[11], (DEPTH, HGRN_HEADS * HGRN_EXPAND), f32),
        "hgrn_g_norm": gain(ks[12], (N_B, HGRN_HEADS * HGRN_HEAD_DIM)),
        "hgrn_w_o": nrm(ks[13], (N_B, HGRN_HEADS * HGRN_HEAD_DIM, D_MODEL), HGRN_HEADS * HGRN_HEAD_DIM),
        "fox_w_in": nrm(ks[14], (N_C, D_MODEL, FOX_IN_DIM), D_MODEL),
        "fox_b_in": fox_b_in,
        "fox_w_o": nrm(ks[15], (N_C, FOX_HEADS * FOX_HEAD_DIM, D_MODEL), FOX_HEADS * FOX_HEAD_DIM),
    }

def reference(x, norm_mix, norm_mlp, norm_final, w_up, w_down,
              swa_w_qkv, swa_b_qkv, swa_sinks, swa_w_o,
              hgrn_w_in, hgrn_lb_logits, hgrn_g_norm, hgrn_w_o,
              fox_w_in, fox_b_in, fox_w_o):
    lb_soft = jax.nn.softmax(hgrn_lb_logits.astype(jnp.float32), axis=0)
    lower_bounds = jnp.cumsum(lb_soft, axis=0) - lb_soft[0]
    for i in range(DEPTH):
        h = rms_norm(x, norm_mix[i])
        m, j = i % N_MIXERS, i // N_MIXERS
        if m == 0:
            y = swa_sink_attention(h, swa_w_qkv[j], swa_b_qkv[j], swa_sinks[j], swa_w_o[j])
        elif m == 1:
            y = hgrn2_mixer(h, hgrn_w_in[j], lower_bounds[i], hgrn_g_norm[j], hgrn_w_o[j])
        else:
            y = fox_attention(h, fox_w_in[j], fox_b_in[j], fox_w_o[j])
        x = x + y
        h = rms_norm(x, norm_mlp[i])
        x = x + jnp.square(jax.nn.relu(h @ w_up[i])) @ w_down[i]
    return rms_norm(x, norm_final)


_drawn_inputs = setup_inputs


def setup_inputs(seed=0):
    import zlib

    import numpy as np

    out = dict(_drawn_inputs(seed))
    spreads = {}
    factors = {'norm_mix': 3.417,
     'norm_final': 3.018,
     'swa_sinks': 3.784,
     'hgrn_lb_logits': 8.0,
     'hgrn_g_norm': 7.35}
    for name, (base, spread) in spreads.items():
        noise = np.random.default_rng([zlib.crc32(name.encode()), seed]).standard_normal(out[name].shape)
        drawn = base * np.exp(spread * noise) if base else spread * noise
        out[name] = __import__('jax').numpy.asarray(drawn.astype(out[name].dtype))
    for name, factor in factors.items():
        out[name] = (out[name] * factor).astype(out[name].dtype)
    return out
```

```python
import concourse.bass as bass
from concourse import mybir
from contextlib import ExitStack

F32 = mybir.dt.float32
F32R = mybir.dt.float32r
BF16 = mybir.dt.bfloat16
I16 = mybir.dt.int16
ALU = mybir.AluOpType
ACT = mybir.ActivationFunctionType
AX = mybir.AxisListType

P = 128
D = 1024
T = 256
DEPTH = 4
TT = T // P
KT = D // P
FF = 4 * D
EPS = 1e-6
HALF = 512
UNIT = 2048
RING = 4
RAWS = 2
PAIRS = FF // (2 * HALF)
MASKED = -1.0e30

HEADS = 16
KV_HEADS = 4
DH = 64
GROUP = 4
GROUPS = HEADS // GROUP
Q_SCALE = DH ** -0.5
HG_HEADS = 8
LEVELS = 8

MIXERS = ["swa", "hgrn", "fox"]
KIND = [MIXERS[i % 3] for i in range(DEPTH)]
MIX_UNITS = {"swa": 6, "hgrn": 16, "fox": 12}
OUT_UNITS = 4
MLP_UNITS = 8 * PAIRS


def unit_bases():
    at, mix, out, mlp = 0, [], [], []
    for kind in KIND:
        mix.append(at)
        out.append(at + MIX_UNITS[kind])
        mlp.append(at + MIX_UNITS[kind] + OUT_UNITS)
        at = mlp[-1] + MLP_UNITS
    return mix, out, mlp, at


MIX0, OUT0, MLP0, ALL_UNITS = unit_bases()

CHUNKS = {"swa": [2, 0, 1], "hgrn": [0, 2, 1, 3, 4, 5, 6, 7], "fox": [2, 0, 4, 3, 1, 5]}

STEPS = {
    "swa": ([("feat", "k", j) for j in range(2)] + [("tok", "v", 0, t) for t in range(TT)] + [("use", 0)]
            + [("feat", "q", j) for j in range(4)] + [("use", 1), ("score", 0)]
            + [("feat", "q", 4), ("feat", "q", 5), ("score", 1), ("feat", "q", 6), ("feat", "q", 7), ("use", 2)]
            + [("turn", 0), ("score", 2), ("value", 0), ("turn", 1), ("score", 3), ("value", 1)]
            + [("turn", 2), ("value", 2), ("turn", 3), ("value", 3)]),
    "fox": ([("gate",)] + [("feat", "k", j) for j in range(4)] + [("use", 0)]
            + [("feat", "q", j) for j in range(4)] + [("use", 1)]
            + [("tok", "v", 0, t) for t in range(TT)] + [("use", 2), ("score", 0)]
            + [("feat", "k", 4), ("feat", "k", 5), ("score", 1), ("feat", "k", 6), ("feat", "k", 7), ("use", 3)]
            + [("turn", 0), ("feat", "q", 4), ("feat", "q", 5), ("value", 0)]
            + [("feat", "q", 6), ("feat", "q", 7), ("use", 4), ("turn", 1), ("score", 2), ("tok", "v", 1, 0), ("value", 1)]
            + [("score", 3), ("tok", "v", 1, 1), ("use", 5), ("turn", 2), ("value", 2), ("turn", 3), ("value", 3)]),
    "hgrn": ([("feat", "q", j) for j in range(4)] + [("use", 0)]
             + [("feat", "f", j) for j in range(4)] + [("use", 1)]
             + [s for j in range(4) for s in (("feat", "q", 4 + j), ("level", 0, j))] + [("use", 2)]
             + [s for j in range(4) for s in (("feat", "f", 4 + j), ("level", 0, 4 + j))] + [("use", 3)]
             + [("cross", 0)]
             + [("tok", "i", 0, 0), ("level", 1, 0), ("tok", "i", 0, 1), ("level", 1, 1), ("use", 4)]
             + [("tok", "i", 1, 0), ("level", 1, 2), ("tok", "i", 1, 1), ("level", 1, 3), ("use", 5)]
             + [("tok", "g", 0, 0), ("level", 1, 4), ("tok", "g", 0, 1), ("level", 1, 5), ("use", 6)]
             + [("mix", 0, 0), ("mix", 0, 1)]
             + [("tok", "g", 1, 0), ("level", 1, 6), ("tok", "g", 1, 1), ("level", 1, 7), ("use", 7)]
             + [("cross", 1), ("mix", 1, 0), ("mix", 1, 1)]),
}
CHUNK_OF = {
    "swa": lambda s: 0 if s[1] in "kv" else 1 + s[2] // 4,
    "fox": lambda s: {"k": (0, 3), "q": (1, 4)}[s[1]][s[2] // 4] if s[0] == "feat" else (2, 5)[s[2]],
    "hgrn": lambda s: {"q": (0, 2), "f": (1, 3)}[s[1]][s[2] // 4] if s[0] == "feat" else {"i": 4, "g": 6}[s[1]] + s[2],
}


class Plan:

    def __init__(self):
        self.full, self.free, self.before = {}, {}, {}
        self.order = {}
        self.fills, self.last, self.counts, self.turn = [0] * 8, [None] * 8, {}, 0
        self.walk()

    def take(self, key, bank, signal, times=1, count=1):
        self.before[key] = self.last[bank]
        self.last[bank] = key
        self.fills[bank] += 1
        self.full[key] = (bank, self.fills[bank])
        self.fills[bank] += times - 1
        self.counts[signal] = self.counts.get(signal, 0) + count
        self.free[key] = (signal, self.counts[signal])

    def note(self, key, signal, count=1):
        self.counts[signal] = self.counts.get(signal, 0) + count
        self.order[signal, key] = self.counts[signal]

    def work(self, key, signal):
        self.take(key, 4 + self.turn % 4, signal)
        self.turn += 1

    def walk(self):
        for c in range(2):
            self.work(("param", c), "cols_copied")
        for l, kind in enumerate(KIND):
            for b in range(4):
                self.take(("normT", 2 * l, b), 4 + b, "actT_lo")
            self.turn = 0
            for s in STEPS[kind]:
                if s[0] == "feat":
                    self.work((l, *s), "feat_ready")
                    self.note((l, *s), "half_ready")
                    if kind == "hgrn":
                        self.note((l, *s), "wide_ready")
                        self.note((l, *s), "sig_ready")
                if s[0] == "tok":
                    self.work((l, *s), "gate_ready" if s[1] == "g" else "v_ready")
                    if s[1] == "g":
                        self.note((l, *s), "sig_ready")
                if s[0] == "gate":
                    self.work((l, *s), "gate_rows_ready")
                    self.work((l, "gateT"), "gateT_ready")
                if s[0] == "score":
                    for b in range(3):
                        self.take((l, *s, b), b, "exp_ready")
                if s[0] == "turn":
                    for b in range(3):
                        self.take((l, *s, b), 4 + b, "turned_v" if b == 1 else "turned_a")
                if s[0] == "value":
                    self.take((l, *s), 7, "o_ready")
                if s[0] == "level":
                    for t in range(TT):
                        self.take((l, *s, t), 2 * (s[2] % 2) + t, "level_out")
                    self.note((l, *s), "level_ready")
                if s[0] == "cross":
                    self.take((l, *s), 0, "mixT_ready")
                if s[0] == "mix":
                    self.take((l, *s), 2 + s[2], "hg_scaled")
            for b in range(4):
                self.take(("outT", l, b), 4 + b, "actT_lo")
            for b in range(4):
                self.take(("mixed", l, b), b, "x_ready", count=b % 2)
            for b in (0, 2):
                self.free[("mixed", l, b)] = self.free[("mixed", l, b + 1)]
            for b in range(4):
                self.take(("normT", 2 * l + 1, b), 4 + b, "actT_lo")
            for b in range(4):
                self.take(("up", l, b), 4 + b, "up_sum", 2 * PAIRS)
            self.counts["up_sum"] += 8 * PAIRS - 4
            for signal in ("half_ready", "wide_ready"):
                self.note((l, "mlp"), signal, 0)
                self.counts[signal] += 8 * PAIRS
            for b in range(4):
                self.free[("up", l, b)] = ("up_sum", self.counts["up_sum"] + 4)
            for b in range(4):
                self.take(("down", l, b), b, "x_ready", 0, b % 2)
            for b in (0, 2):
                self.free[("down", l, b)] = self.free[("down", l, b + 1)]


ROW_MIX, ROW_MLP, ROW_LB, ROW_GN, ROW_SWA = 0, 32, 64, 96, 104
SWA_ROWS = 10
HG_LAYER = 1
SWA_LAYERS = [l for l in range(DEPTH) if KIND[l] == "swa"]
SMALLS, BCASTS = 7, 7


def build_trunk(nc, x_in, norm_mix, norm_mlp, norm_final, w_up, w_down, swa_w_qkv, swa_b_qkv, swa_sinks, swa_w_o,
                hgrn_w_in, hgrn_lb_logits, hgrn_g_norm, hgrn_w_o, fox_w_in, fox_b_in, fox_w_o, out):
    plan = Plan()
    ctx = ExitStack()
    with ctx:
        def sb(name, shape, dt=F32):
            return ctx.enter_context(nc.sbuf_tensor(name, shape, dt))

        def sem(name):
            return ctx.enter_context(nc.semaphore(name))

        raw = sb("raw", [P, RAWS, UNIT])
        w_hi = sb("w_hi", [P, RING, UNIT], F32R)
        w_lo = sb("w_lo", [P, RING, UNIT], F32R)
        x = sb("x", [P, TT, D])
        rows = sb("rows", [P, TT, D])
        actT = sb("actT", [P, KT, 2, T], F32R)
        hidden = sb("hidden", [P, 2, 4, 2, T], F32R)
        half = sb("half", [P, 4, T])
        wide = sb("wide", [P, 4, T])
        qT = sb("qT", [P, 8, T])
        kT = sb("kT", [P, 8, T])
        v = sb("v", [P, TT, D])
        scratch = sb("scratch", [P, 6144])
        probs = scratch[:, 0:3072].rearrange("p (g h s) -> p g h s", g=2, h=GROUP)
        probsT = scratch[:, 3072:6144].rearrange("p (g b h s) -> p g b h s", g=2, b=3, h=GROUP)
        mixT = scratch[:, 0:2048].rearrange("p (h t) -> p h t", h=HG_HEADS)
        crossT = scratch[:, 2048:3072].rearrange("p (h t) -> p h t", h=HG_HEADS)
        gate = scratch[:, 3072:5120].rearrange("p (t n) -> p t n", t=TT)
        keep = scratch[:, 5120:6144].rearrange("p (h t) -> p h t", h=GROUP)
        span = sb("span", [P, GROUP * 254])
        level_mask = sb("level_mask", [P, LEVELS, P], BF16)
        ident = sb("ident", [P, P])
        ident_h = sb("ident_h", [P, P], BF16)
        masks = sb("masks", [P, 5, P], BF16)
        pick = sb("pick", [HEADS, HEADS, P], BF16)
        decay = sb("decay", [HEADS, 3, T], BF16)
        cols = sb("cols", [P, P])
        foxcols = sb("foxcols", [P, 16])
        q_bias = sb("q_bias", [P, 3, 8])
        v_bias = sb("v_bias", [P, D])
        swa_v_bias = sb("swa_v_bias", [P, 2, 256])
        sinks = sb("sinks", [P, 2, HEADS])
        neg_sinks = sb("neg_sinks", [P, 2, HEADS])
        gate_bias = sb("gate_bias", [P, HEADS])
        gate_w = sb("gate_w", [P, KT, HEADS])
        gate_whi = sb("gate_whi", [P, KT, HEADS], F32R)
        gate_wlo = sb("gate_wlo", [P, KT, HEADS], F32R)
        sumsq = sb("sumsq", [P, TT])
        mean = sb("mean", [P, GROUP])
        rnorm = sb("rnorm", [P, TT])
        hg_sumsq = sb("hg_sumsq", [P, GROUP])
        hg_rnorm = sb("hg_rnorm", [P, GROUP])
        minus_half = sb("minus_half", [P, GROUP])
        neg_max = sb("neg_max", [P, 2, 2 * GROUP])
        sink_shift = sb("sink_shift", [P, 2, 2 * GROUP])
        sink_exp = sb("sink_exp", [P, 2, 2 * GROUP])
        denom = sb("denom", [P, 2, 2 * GROUP])
        inv_denom = sb("inv_denom", [P, 2, 2 * GROUP])
        lb = sb("lb", [P, DEPTH + 3, HG_HEADS])
        lower = sb("lower", [P, 2, HG_HEADS])

        params = qT[:, 0, 0:P]
        params2 = qT[:, 0, P:2 * P]
        gate_rows = wide[:, 0:2, 0:P]
        fox_tmp = wide[0:HEADS, :, :]
        final_gain = v[:, 0, :]

        psum = ctx.enter_context(nc.psum_tensor("psum", [P, 8, HALF], F32))

        raw_full = [sem(f"raw_full{i}") for i in range(RAWS)]
        hi_done = sem("hi_done")
        lo_done = sem("lo_done")
        out_used = sem("out_used")
        down_used = sem("down_used")
        down_tile0 = sem("down_tile0")
        bank_full = [sem(f"bank_full{b}") for b in range(8)]
        x_in_full = sem("x_in_full")
        small_full = sem("small_full")
        bcast_full = sem("bcast_full")
        gain_full = sem("gain_full")
        zeroed = sem("zeroed")
        consts = sem("consts")
        pool_step = sem("pool_step")
        cols_copied = sem("cols_copied")
        bias_ready = sem("bias_ready")
        lb_shifted = sem("lb_shifted")
        lb_exp = sem("lb_exp")
        x_ready = sem("x_ready")
        sq_ready = sem("sq_ready")
        rnorm_ready = sem("rnorm_ready")
        rows_ready = sem("rows_ready")
        actT_hi = sem("actT_hi")
        actT_lo = sem("actT_lo")
        half_ready = sem("half_ready")
        wide_ready = sem("wide_ready")
        sig_ready = sem("sig_ready")
        up_sum = sem("up_sum")
        hid_hi = sem("hid_hi")
        hid_lo = sem("hid_lo")
        feat_ready = sem("feat_ready")
        v_ready = sem("v_ready")
        gate_ready = sem("gate_ready")
        max_ready = sem("max_ready")
        exp_ready = sem("exp_ready")
        sink_ready = sem("sink_ready")
        turned_a = sem("turned_a")
        turned_v = sem("turned_v")
        o_ready = sem("o_ready")
        level_ready = sem("level_ready")
        level_out = sem("level_out")
        mixT_ready = sem("mixT_ready")
        hg_sq = sem("hg_sq")
        hg_sum = sem("hg_sum")
        hg_rn = sem("hg_rn")
        hg_scaled = sem("hg_scaled")
        hg_rows = sem("hg_rows")
        gate_split = sem("gate_split")
        gate_hi_done = sem("gate_hi_done")
        gate_rows_ready = sem("gate_rows_ready")
        gateT_ready = sem("gateT_ready")
        gate_log = sem("gate_log")
        decay_ready = sem("decay_ready")
        dve_step = sem("dve_step")
        act_step = sem("act_step")
        out_done = sem("out_done")
        signals = {"cols_copied": cols_copied, "actT_lo": actT_lo, "feat_ready": feat_ready, "v_ready": v_ready,
                   "gate_ready": gate_ready, "gate_rows_ready": gate_rows_ready, "gateT_ready": gateT_ready,
                   "exp_ready": exp_ready, "turned_a": turned_a, "turned_v": turned_v, "o_ready": o_ready,
                   "level_out": level_out, "mixT_ready": mixT_ready, "hg_scaled": hg_scaled, "x_ready": x_ready,
                   "up_sum": up_sum}

        block = ctx.enter_context(nc.Block())

        def bank(key, width=HALF, start=0):
            return psum[:, plan.full[key][0], start:start + width]

        def bank_of(key):
            return plan.full[key][0]

        def wait_full(engine, key):
            b, n = plan.full[key]
            engine.wait_ge(bank_full[b], n)

        def wait_free(engine, key):
            signal, n = plan.free[key]
            engine.wait_ge(signals[signal], n)

        def group_number(l, g):
            return GROUPS * sum(KIND[m] != "hgrn" for m in range(l)) + g

        def turned_number(l, turned, b):
            return 4 * (3 * l + turned) + b + 1

        UP_TILES = 8 * PAIRS
        GATES = [l for l in range(DEPTH) if KIND[l] == "hgrn"]

        def wait_unit_used(engine, n):
            l = max(m for m in range(DEPTH) if MIX0[m] <= n)
            if n < OUT0[l]:
                place = (n - MIX0[l]) // 2
                tiles = [s for s in STEPS[KIND[l]] if s[0] in ("feat", "tok") and CHUNK_OF[KIND[l]](s) == place]
                wait_full(engine, (l, *tiles[-1]))
            elif n < OUT0[l] + OUT_UNITS - 1:
                engine.wait_ge(out_used, (OUT_UNITS - 1) * l + n - OUT0[l] + 1)
            elif n == OUT0[l] + OUT_UNITS - 1:
                wait_full(engine, ("mixed", l, 3))

        @block.sync
        def _(sp):
            def load(n, src, columns):
                slot = n % RAWS
                if n >= RAWS:
                    sp.wait_ge(lo_done, n - RAWS + 1)
                dst = raw[:, slot, :].rearrange("p (k n) -> p k n", n=columns)
                sp.dma_start(dst, src).then_inc(raw_full[slot], 16)

            for t in range(TT):
                sp.dma_start(x[:, t, :], x_in[0, t * P:(t + 1) * P, :]).then_inc(x_in_full, 16)
            for l, kind in enumerate(KIND):
                w_in = {"swa": swa_w_qkv, "hgrn": hgrn_w_in, "fox": fox_w_in}[kind][l // 3]
                w_o = {"swa": swa_w_o, "hgrn": hgrn_w_o, "fox": fox_w_o}[kind][l // 3]
                w_in = w_in.rearrange("(k p) n -> p k n", p=P)
                w_o = w_o.rearrange("(k p) n -> p k n", p=P)
                for c, chunk in enumerate(CHUNKS[kind]):
                    for u in range(2):
                        load(MIX0[l] + 2 * c + u, w_in[:, 4 * u:4 * u + 4, chunk * HALF:(chunk + 1) * HALF], HALF)
                for u in range(OUT_UNITS):
                    load(OUT0[l] + u, w_o[:, 2 * u:2 * u + 2, :], D)
                up = w_up[l].rearrange("(k p) n -> p k n", p=P)
                down = w_down[l].rearrange("(k p) n -> p k n", p=P)
                with sp.Fori(0, PAIRS) as i:
                    for j in range(8):
                        ab, u = (j // 2) % 2, j % 2
                        if j < 4:
                            src = up[:, 4 * u:4 * u + 4, bass.ds((i * 2 + ab) * HALF, HALF)]
                        else:
                            src = down[:, bass.ds((i * 2 + ab) * 4 + 2 * u, 2), :]
                        slot = (MLP0[l] + j) % RAWS
                        sp.wait_ge(lo_done, i * 8 + (MLP0[l] + j - RAWS + 1))
                        dst = raw[:, slot, :].rearrange("p (k n) -> p k n", n=HALF if j < 4 else D)
                        sp.dma_start(dst, src).then_inc(raw_full[slot], 16)
            for t in range(TT):
                sp.wait_ge(rows_ready, TT * 2 * DEPTH + t + 1)
                sp.dma_start(out[0, t * P:(t + 1) * P, :], rows[:, t, :]).then_inc(out_done, 16)
            sp.wait_ge(out_done, 16 * TT)

        @block.gpsimd
        def _(pool):
            steps = [0]

            def link(ins):
                steps[0] += 1
                ins.then_inc(pool_step, 1)
                pool.wait_ge(pool_step, steps[0])

            nc.gpsimd.memset(qT[:, 0, :], 0.0).then_inc(zeroed, 1)
            link(nc.gpsimd.memset(minus_half[:], -0.5))
            link(nc.gpsimd.memset(ident[:], 0.0))
            nc.gpsimd.affine_select(out=ident[:], in_=ident[:], compare_op=ALU.not_equal, fill=1.0, base=0,
                                    pattern=[[-1, P]], channel_multiplier=1).then_inc(consts, 1)
            pool.wait_ge(consts, 1)
            link(nc.gpsimd.tensor_copy(ident_h[:], ident[:]))
            link(nc.gpsimd.memset(masks[:], 0.0))
            for m in (0, 2, 4):
                link(nc.gpsimd.affine_select(out=masks[:, m, :], in_=masks[:, m, :], compare_op=ALU.is_ge, fill=MASKED,
                                             base=0, pattern=[[-1, P]], channel_multiplier=1))
            nc.gpsimd.affine_select(out=masks[:, 1, :], in_=masks[:, 1, :], compare_op=ALU.is_gt, fill=MASKED, base=0,
                                    pattern=[[1, P]], channel_multiplier=-1).then_inc(consts, 1)

            def norm_root(phase):
                for t in range(TT):
                    pool.wait_ge(sq_ready, TT * phase + t + 1)
                    link(nc.gpsimd.tensor_scalar(mean[:, 0:1], sumsq[:, t:t + 1], 1.0 / D, EPS, ALU.mult, ALU.add))
                    nc.gpsimd.tensor_tensor(rnorm[:, t:t + 1], mean[:, 0:1], minus_half[:, 0:1],
                                            ALU.pow).then_inc(rnorm_ready, 1)
                    pool.wait_ge(rnorm_ready, TT * phase + t + 1)

            norm_root(0)
            link(nc.gpsimd.memset(pick[:], 0.0))
            link(nc.gpsimd.affine_select(out=pick[:], in_=pick[:], compare_op=ALU.not_equal, fill=1.0, base=0,
                                         pattern=[[-1, HEADS], [0, P]], channel_multiplier=1))
            link(nc.gpsimd.memset(level_mask[:], 0.0))
            for j in range(1, LEVELS):
                size = 2 ** (j - 1)
                blocks = P // (2 * size)
                right = level_mask[:, j, :].rearrange("p (b h w) -> p b h w", h=2, w=size)[:, :, 1, :]
                link(nc.gpsimd.memset(right, 1.0))
                link(nc.gpsimd.affine_select(out=right, in_=right, compare_op=ALU.is_ge, fill=0.0, base=0,
                                             pattern=[[-2 * size, blocks], [0, size]], channel_multiplier=1))
                link(nc.gpsimd.affine_select(out=right, in_=right, compare_op=ALU.is_ge, fill=0.0, base=size - 1,
                                             pattern=[[2 * size, blocks], [0, size]], channel_multiplier=-1))
            nc.gpsimd.tensor_copy(level_mask[:, 0, :], ident[:]).then_inc(consts, 1)
            hg_n = 0
            for l, kind in enumerate(KIND):
                if l > 0:
                    norm_root(2 * l)
                if kind == "hgrn":
                    for _ in range(2 * TT):
                        hg_n += 1
                        pool.wait_ge(hg_sum, hg_n)
                        link(nc.gpsimd.tensor_scalar(mean[:], hg_sumsq[:], 1.0 / P, EPS, ALU.mult, ALU.add))
                        nc.gpsimd.tensor_tensor(hg_rnorm[:], mean[:], minus_half[:], ALU.pow).then_inc(hg_rn, 1)
                        pool.wait_ge(hg_rn, hg_n)
                norm_root(2 * l + 1)
            norm_root(2 * DEPTH)

        @block.scalar
        def _(act):
            steps = [0]

            def link(ins):
                steps[0] += 1
                ins.then_inc(act_step, 1)
                act.wait_ge(act_step, steps[0])

            act.wait_ge(zeroed, 1)
            smalls = [(params[ROW_MIX:ROW_MIX + 32, :], norm_mix.rearrange("l (k p) -> (l k) p", p=P)),
                      (params[ROW_MLP:ROW_MLP + 32, :], norm_mlp.rearrange("l (k p) -> (l k) p", p=P)),
                      (params[ROW_LB:ROW_LB + 32, :], hgrn_lb_logits.rearrange("l (k p) -> (l k) p", p=P)),
                      (params[ROW_GN:ROW_GN + 8, :], hgrn_g_norm.rearrange("l (k p) -> (l k) p", p=P)),
                      (params2[0:16, :], fox_b_in[0, 0:2 * D].rearrange("(k p) -> k p", p=P))]
            for a in range(2):
                row = ROW_SWA + SWA_ROWS * a
                src = swa_b_qkv[a, 0:SWA_ROWS * P].rearrange("(k p) -> k p", p=P)
                smalls.append((params[row:row + SWA_ROWS, :], src))
            assert len(smalls) == SMALLS
            for dst, src in smalls:
                act.dma_start(dst, src).then_inc(small_full, 16)
            bcasts = [(v_bias[:], fox_b_in[0, 2 * D:3 * D].partition_broadcast(P)),
                      (gate_bias[:], fox_b_in[0, 3 * D:3 * D + HEADS].partition_broadcast(P)),
                      (gate_w[:], fox_w_in[0, :, 3 * D:3 * D + HEADS].rearrange("(k p) n -> p k n", p=P))]
            for a in range(2):
                bcasts.append((swa_v_bias[:, a, :], swa_b_qkv[a, D + 256:D + 512].partition_broadcast(P)))
                bcasts.append((sinks[:, a, :], swa_sinks[a].partition_broadcast(P)))
            assert len(bcasts) == BCASTS
            for dst, src in bcasts:
                act.dma_start(dst, src).then_inc(bcast_full, 16)

            def round_unit(n):
                nc.scalar.activation(w_hi[:, n % RING, :], raw[:, n % RAWS, :], ACT.Copy).then_inc(hi_done, 1)

            def split_unit(n):
                if n >= RING:
                    wait_unit_used(act, n - RING)
                act.wait_ge(raw_full[n % RAWS], 16 * (n // RAWS + 1))
                round_unit(n)

            def sum_squares(phase):
                for t in range(TT):
                    if phase == 0:
                        act.wait_ge(x_in_full, 16 * TT)
                    else:
                        act.wait_ge(x_ready, TT * (phase - 1) + t + 1)
                    nc.scalar.activation(rows[:, t, :], x[:, t, :], ACT.Square,
                                         accum_out=sumsq[:, t:t + 1]).then_inc(sq_ready, 1)

            def round_actT(name, l, gain_row):
                for b in range(4):
                    key = (name, l, b)
                    wait_full(act, key)
                    if gain_row is None:
                        nc.scalar.activation(actT[:, 2 * b:2 * b + 2, 0, :], bank(key).rearrange("p (k t) -> p k t", k=2),
                                             ACT.Copy).then_inc(actT_hi, 1)
                    else:
                        for e in range(2):
                            k = 2 * b + e
                            last = nc.scalar.activation(actT[:, k, 0, :], bank(key, T, e * T), ACT.Copy,
                                                        scale=cols[:, gain_row + k:gain_row + k + 1])
                        last.then_inc(actT_hi, 1)

            def second_half(key, scale=1.0, bias=None):
                wait_full(act, key)
                src, dst = bank(key, T, T), half[:, bank_of(key) - 4, :]
                if bias is None:
                    nc.scalar.activation(dst, src, ACT.Copy).then_inc(half_ready, 1)
                else:
                    nc.scalar.activation(dst, src, ACT.Identity, bias=bias, scale=scale).then_inc(half_ready, 1)

            def softmax(l, g):
                buf = g % 2
                act.wait_ge(max_ready, group_number(l, g) + 1)
                for b in range(3):
                    key = (l, "score", g, b)
                    for e in range(GROUP if b == 0 else 2):
                        h = e if b == 0 else 2 * (b - 1) + e
                        src = bank(key, P, e * P) if b == 0 else bank(key, T, e * T)
                        dst = probs[:, buf, h, 0:P] if b == 0 else probs[:, buf, h, P:3 * P]
                        c = h if b == 0 else GROUP + h
                        last = nc.scalar.activation(dst, src, ACT.Exp, bias=neg_max[:, buf, c:c + 1],
                                                    accum_out=denom[:, buf, c:c + 1])
                    last.then_inc(exp_ready, 1)
                if KIND[l] == "swa":
                    nc.scalar.activation(sink_exp[:, buf, :], sink_shift[:, buf, :], ACT.Exp).then_inc(sink_ready, 1)

            def turn(l, g):
                for b in (0, 2):
                    key = (l, "turn", g, b)
                    wait_full(act, key)
                    nc.scalar.activation(probsT[:, g % 2, b, :, :], bank(key).rearrange("p (h s) -> p h s", h=GROUP),
                                         ACT.Copy).then_inc(turned_a, 1)

            sum_squares(0)
            for n in range(RING):
                split_unit(n)
            act.wait_ge(lb_shifted, 1)
            nc.scalar.activation(lb[:, 0:DEPTH, :], lb[:, 0:DEPTH, :], ACT.Exp).then_inc(lb_exp, 1)
            act.wait_ge(bias_ready, 1)

            hg_n = 0
            for l, kind in enumerate(KIND):
                if l > 0:
                    sum_squares(2 * l)
                round_actT("normT", 2 * l, ROW_MIX + KT * l)
                for s in STEPS[kind]:
                    key = (l, *s)
                    if s[0] == "use":
                        for u in range(2):
                            split_unit(MIX0[l] + 2 * s[1] + u + RING)
                    elif s[0] == "feat" and kind == "hgrn":
                        second_half(key)
                        slot = bank_of(key) - 4
                        act.wait_ge(wide_ready, plan.order["wide_ready", key])
                        nc.scalar.activation(half[:, slot, :], wide[:, slot, :], ACT.Sigmoid).then_inc(sig_ready, 1)
                    elif s[0] == "feat":
                        which = SWA_LAYERS.index(l) if kind == "swa" else 2
                        if s[1] == "q":
                            second_half(key, Q_SCALE, q_bias[:, which, s[2]:s[2] + 1])
                        elif kind == "swa":
                            c = ROW_SWA + SWA_ROWS * which + 8 + s[2]
                            second_half(key, 1.0, cols[:, c:c + 1])
                        else:
                            second_half(key, 1.0, foxcols[:, 8 + s[2]:9 + s[2]])
                    elif s[0] == "tok" and s[1] == "i":
                        wait_full(act, key)
                        nc.scalar.activation(v[:, s[3], s[2] * HALF:(s[2] + 1) * HALF], bank(key),
                                             ACT.Copy).then_inc(v_ready, 1)
                    elif s[0] == "tok" and s[1] == "g":
                        wait_full(act, key)
                        nc.scalar.activation(gate[:, s[3], s[2] * HALF:(s[2] + 1) * HALF], bank(key),
                                             ACT.Sigmoid).then_inc(sig_ready, 1)
                    elif s[0] == "gate":
                        act.wait_ge(bcast_full, 16 * BCASTS)
                        nc.scalar.activation(gate_whi[:], gate_w[:], ACT.Copy).then_inc(gate_hi_done, 1)
                        act.wait_ge(gateT_ready, 1)
                        z = fox_tmp[:, 1, :]
                        link(nc.scalar.activation(fox_tmp[:, 2, :], z, ACT.Abs))
                        link(nc.scalar.activation(fox_tmp[:, 2, :], fox_tmp[:, 2, :], ACT.Exp, scale=-1.0))
                        nc.scalar.activation(fox_tmp[:, 3, :], fox_tmp[:, 2, :], ACT.Ln, bias=1.0).then_inc(gate_log, 1)
                    elif s[0] == "score":
                        softmax(l, s[1])
                    elif s[0] == "turn":
                        turn(l, s[1])
                    elif s[0] == "mix":
                        wait_full(act, key)
                        if hg_n:
                            act.wait_ge(hg_sum, hg_n)
                        hg_n += 1
                        nc.scalar.activation(wide[:, 0:2, :], bank(key).rearrange("p (a b) -> p a b", a=2),
                                             ACT.Square).then_inc(hg_sq, 1)
                round_actT("outT", l, ROW_GN if kind == "hgrn" else None)
                for u in range(OUT_UNITS):
                    split_unit(OUT0[l] + u + RING)
                sum_squares(2 * l + 1)
                round_actT("normT", 2 * l + 1, ROW_MLP + KT * l)

                def mlp_pair(i, last):
                    def split_in_loop(j):
                        if last and j >= 4:
                            return
                        n = MLP0[l] + j + RING
                        if j < 4:
                            b, full = plan.full["up", l, 3]
                            act.wait_ge(bank_full[b], i * 2 + (full + j // 2))
                        else:
                            act.wait_ge(down_used, i * 4 + (4 * PAIRS * l + j - 3))
                        act.wait_ge(raw_full[n % RAWS], i * (8 // RAWS * 16) + 16 * (n // RAWS + 1))
                        round_unit(n)

                    for ab in range(2):
                        for f in range(4):
                            b, full = plan.full["up", l, f]
                            act.wait_ge(bank_full[b], i * 2 + (full + ab))
                            nc.scalar.activation(half[:, f, :], psum[:, b, T:2 * T], ACT.Copy).then_inc(half_ready, 1)
                            act.wait_ge(wide_ready, i * 8 + (plan.order["wide_ready", (l, "mlp")] + 4 * ab + f + 1))
                            nc.scalar.activation(hidden[:, ab, f, 0, :], wide[:, f, :], ACT.Copy).then_inc(hid_hi, 1)
                            if ab == 1 and f < 2:
                                split_in_loop(f)
                    for j in range(2, 8):
                        split_in_loop(j)

                with act.Fori(0, PAIRS - (l == DEPTH - 1)) as i:
                    mlp_pair(i, False)
                if l == DEPTH - 1:
                    mlp_pair(PAIRS - 1, True)
            act.dma_start(final_gain, norm_final.partition_broadcast(P)).then_inc(gain_full, 16)
            sum_squares(2 * DEPTH)

        @block.vector
        def _(dve):
            steps = [0]

            def link(ins):
                steps[0] += 1
                ins.then_inc(dve_step, 1)
                dve.wait_ge(dve_step, steps[0])

            def f32(ap):
                return ap.bitcast(F32)

            def rest_unit(n):
                nc.vector.tensor_tensor(w_lo[:, n % RING, :], raw[:, n % RAWS, :], f32(w_hi[:, n % RING, :]),
                                        ALU.subtract).then_inc(lo_done, 1)

            def split_unit(n):
                dve.wait_ge(hi_done, n + 1)
                rest_unit(n)

            def add_to_x(name, l, phase):
                for t in range(TT):
                    if name == "mixed":
                        for e in range(2):
                            wait_full(dve, (name, l, 2 * t + e))
                    elif t == 0:
                        dve.wait_ge(down_tile0, PAIRS * (l + 1))
                    else:
                        dve.wait_ge(down_used, 4 * PAIRS * (l + 1))
                    nc.vector.tensor_tensor(x[:, t, :], psum[:, 2 * t:2 * t + 2, :].rearrange("p a b -> p (a b)"),
                                            x[:, t, :], ALU.add).then_inc(x_ready, 1)

            def scale_rows(phase):
                for t in range(TT):
                    dve.wait_ge(rnorm_ready, TT * phase + t + 1)
                    nc.vector.tensor_scalar(rows[:, t, :], x[:, t, :], rnorm[:, t:t + 1], None,
                                            ALU.mult).then_inc(rows_ready, 1)

            def rest_actT(name, l, turned, gain_row):
                for b in range(4):
                    key = (name, 2 * l + turned // 2 if name == "normT" else l, b)
                    dve.wait_ge(actT_hi, turned_number(l, turned, b))
                    if gain_row is None:
                        nc.vector.tensor_tensor(actT[:, 2 * b:2 * b + 2, 1, :],
                                                bank(key).rearrange("p (k t) -> p k t", k=2),
                                                f32(actT[:, 2 * b:2 * b + 2, 0, :]), ALU.subtract).then_inc(actT_lo, 1)
                    else:
                        for e in range(2):
                            k = 2 * b + e
                            last = nc.vector.scalar_tensor_tensor(
                                actT[:, k, 1, :], bank(key, T, e * T), cols[:, gain_row + k:gain_row + k + 1],
                                f32(actT[:, k, 0, :]), ALU.mult, ALU.subtract)
                        last.then_inc(actT_lo, 1)

            for c, (dst, width) in enumerate(((cols, P), (foxcols, 16))):
                wait_full(dve, ("param", c))
                nc.vector.tensor_copy(dst[:], bank(("param", c), width)).then_inc(cols_copied, 1)
            dve.wait_ge(cols_copied, 2)
            for a in range(2):
                row = ROW_SWA + SWA_ROWS * a
                nc.vector.tensor_scalar(q_bias[:, a, :], cols[:, row:row + 8], Q_SCALE, None, ALU.mult)
            nc.vector.tensor_scalar(q_bias[:, 2, :], foxcols[:, 0:8], Q_SCALE, None, ALU.mult).then_inc(bias_ready, 1)
            logits = cols[:, ROW_LB:ROW_LB + 32].rearrange("p (l h) -> p l h", l=DEPTH)
            link(nc.vector.tensor_reduce(lb[:, DEPTH, :], logits.rearrange("p l h -> p h l"), AX.X, ALU.max))
            nc.vector.tensor_tensor(lb[:, 0:DEPTH, :], logits,
                                    lb[:, DEPTH:DEPTH + 1, :].to_broadcast([P, DEPTH, HG_HEADS]),
                                    ALU.subtract).then_inc(lb_shifted, 1)

            scale_rows(0)
            for n in range(RING):
                split_unit(n)
            dve.wait_ge(bcast_full, 16 * BCASTS)
            nc.vector.tensor_scalar(neg_sinks[:], sinks[:], -1.0, None, ALU.mult)
            dve.wait_ge(lb_exp, 1)
            link(nc.vector.tensor_reduce(lb[:, DEPTH, :], lb[:, 0:DEPTH, :].rearrange("p l h -> p h l"), AX.X, ALU.add))
            link(nc.vector.reciprocal(lb[:, DEPTH + 1, :], lb[:, DEPTH, :]))
            link(nc.vector.tensor_tensor(lb[:, 0:DEPTH, :], lb[:, 0:DEPTH, :],
                                         lb[:, DEPTH + 1:DEPTH + 2, :].to_broadcast([P, DEPTH, HG_HEADS]), ALU.mult))
            total = lb[:, 0, :]
            for i in range(1, HG_LAYER + 1):
                link(nc.vector.tensor_tensor(lb[:, DEPTH + 2, :], total, lb[:, i, :], ALU.add))
                total = lb[:, DEPTH + 2, :]
            link(nc.vector.tensor_tensor(lower[:, 0, :], total, lb[:, 0, :], ALU.subtract))
            link(nc.vector.tensor_scalar(lower[:, 1, :], lower[:, 0, :], -1.0, 1.0, ALU.mult, ALU.add))
            dve.sem_inc(up_sum, 4)

            def feature_tile(l, s):
                key = (l, *s)
                slot = bank_of(key) - 4
                dve.wait_ge(half_ready, plan.order["half_ready", key])
                first, other = bank(key, T), half[:, slot, :]
                if KIND[l] != "hgrn":
                    dst = (kT if s[1] == "k" else qT)[:, s[2], :]
                    last = nc.vector.scalar_tensor_tensor(dst, first, Q_SCALE if s[1] == "q" else 1.0, other,
                                                          ALU.mult, ALU.add)
                    if KIND[l] == "swa" and s[1] == "k":
                        link(last)
                        nc.vector.tensor_copy(kT[DH:P, 2 + s[2], :], kT[0:DH, s[2], :])
                        last = nc.vector.tensor_copy(kT[0:DH, 2 + s[2], :], kT[DH:P, s[2], :])
                    last.then_inc(feat_ready, 1)
                    return
                h, z = s[2], wide[:, slot, :]
                nc.vector.tensor_tensor(z, first, other, ALU.add).then_inc(wide_ready, 1)
                dve.wait_ge(sig_ready, plan.order["sig_ready", key])
                if s[1] == "q":
                    nc.vector.tensor_tensor(qT[:, h, :], z, other, ALU.mult).then_inc(feat_ready, 1)
                else:
                    link(nc.vector.tensor_scalar(keep[:, h % GROUP, :], other, lower[:, 1, h:h + 1],
                                                 lower[:, 0, h:h + 1], ALU.mult, ALU.add))
                    nc.vector.tensor_scalar(kT[:, h, :], keep[:, h % GROUP, :], -1.0, 1.0,
                                            ALU.mult, ALU.add).then_inc(feat_ready, 1)

            def span_of(j):
                if j == 0:
                    return keep.rearrange("p h t -> p (h t)")
                start = GROUP * (T - T // 2 ** (j - 1))
                return span[:, start:start + GROUP * (T // 2 ** j)]

            def level(l, g, j):
                heads = slice(GROUP * g, GROUP * g + GROUP)
                for t in range(TT):
                    wait_full(dve, (l, "level", g, j, t))
                if j == 0:
                    nc.vector.tensor_tensor(qT[:, heads, :], qT[:, heads, :], keep, ALU.mult).then_inc(level_ready, 1)
                else:
                    size = 2 ** (j - 1)
                    qv = qT[:, heads, :].rearrange("p h (b e w) -> p (h b) e w", e=2, w=size)
                    kv = kT[:, heads, :].rearrange("p h (b e w) -> p (h b) e w", e=2, w=size)
                    blocks = GROUP * T // (2 * size)
                    sv = span_of(j - 1).rearrange("p (b e) -> p b e", e=2)
                    nc.vector.tensor_tensor(qv[:, :, 1, :], qv[:, :, 1, :],
                                            sv[:, :, 0:1].to_broadcast([P, blocks, size]), ALU.mult)
                    if j < LEVELS - 1:
                        link(nc.vector.tensor_tensor(span_of(j), sv[:, :, 0], sv[:, :, 1], ALU.mult))
                    nc.vector.tensor_tensor(kv[:, :, 0, :], kv[:, :, 0, :],
                                            sv[:, :, 1:2].to_broadcast([P, blocks, size]),
                                            ALU.mult).then_inc(level_ready, 1)
                for t in range(TT):
                    key = (l, "level", g, j, t)
                    if j > 0:
                        wait_free(dve, (l, "level", g, j - 1, t))
                    mask = level_mask[:, j:j + 1, :].bitcast(I16).to_broadcast([P, GROUP, P])
                    nc.vector.copy_predicated(mixT[:, heads, t * P:(t + 1) * P], mask,
                                              bank(key).rearrange("p (h t) -> p h t", h=GROUP)).then_inc(level_out, 1)

            def max_of_scores(l, g):
                buf = g % 2
                for b in range(3):
                    key = (l, "score", g, b)
                    wait_full(dve, key)
                    heads = GROUP if b == 0 else 2
                    c = 0 if b == 0 else GROUP + 2 * (b - 1)
                    last = nc.vector.tensor_reduce(neg_max[:, buf, c:c + heads],
                                                   bank(key).rearrange("p (h s) -> p h s", h=heads),
                                                   AX.X, ALU.max, negate=True)
                if KIND[l] != "swa":
                    last.then_inc(max_ready, 1)
                    return
                link(last)
                a, first = SWA_LAYERS.index(l), 2 * GROUP * (g // 2) + g % 2
                hs = slice(first, first + 2 * GROUP - 1, 2)
                nm = neg_max[:, buf, :].rearrange("p (b h) -> p b h", b=2)
                link(nc.vector.tensor_tensor(nm, nm, neg_sinks[:, a:a + 1, hs].to_broadcast([P, 2, GROUP]), ALU.min))
                nc.vector.tensor_tensor(sink_shift[:, buf, :].rearrange("p (b h) -> p b h", b=2), nm,
                                        sinks[:, a:a + 1, hs].to_broadcast([P, 2, GROUP]), ALU.add).then_inc(max_ready, 1)

            def turn(l, g):
                buf = g % 2
                dve.wait_ge(exp_ready, 3 * (group_number(l, g) + 1))
                if KIND[l] == "swa":
                    which = GROUPS * SWA_LAYERS.index(l) + g
                    dve.wait_ge(sink_ready, which + 1)
                    link(nc.vector.tensor_tensor(denom[:, buf, :], denom[:, buf, :], sink_exp[:, buf, :], ALU.add))
                nc.vector.reciprocal(inv_denom[:, buf, :], denom[:, buf, :])
                key = (l, "turn", g, 1)
                wait_full(dve, key)
                link(nc.vector.tensor_copy(probsT[:, buf, 1, :, :], bank(key).rearrange("p (h s) -> p h s", h=GROUP)))
                dve.sem_inc(turned_v, 1)

            def forget_gates(l):
                dve.wait_ge(gate_hi_done, 1)
                nc.vector.tensor_tensor(gate_wlo[:], gate_w[:], f32(gate_whi[:]), ALU.subtract).then_inc(gate_split, 1)
                link(nc.vector.memset(gate_rows, 0.0))
                key = (l, "gate")
                wait_full(dve, key)
                nc.vector.tensor_tensor(gate_rows[:, :, 0:HEADS],
                                        bank(key, TT * HEADS).rearrange("p (t h) -> p t h", t=TT),
                                        gate_bias[:].unsqueeze(1).to_broadcast([P, TT, HEADS]),
                                        ALU.add).then_inc(gate_rows_ready, 1)
                key = (l, "gateT")
                wait_full(dve, key)
                z = fox_tmp[:, 1, :]
                nc.vector.tensor_copy(z, psum[0:HEADS, bank_of(key), 0:T]).then_inc(gateT_ready, 1)
                dve.wait_ge(gate_log, 1)
                link(nc.vector.tensor_scalar(z, z, 0.0, None, ALU.min))
                link(nc.vector.tensor_tensor(fox_tmp[:, 2, :], z, fox_tmp[:, 3, :], ALU.subtract))
                link(nc.vector.memset(fox_tmp[:, 3, :], 1.0))
                link(nc.vector.tensor_tensor_scan(z, fox_tmp[:, 3, :], fox_tmp[:, 2, :], 0.0, ALU.mult, ALU.add))
                link(nc.vector.tensor_scalar(z, z, -1.0, None, ALU.mult))
                link(nc.vector.tensor_copy(decay[:, 0, :], z))
                link(nc.vector.tensor_tensor(z, z, decay[:, 0, :], ALU.subtract))
                link(nc.vector.tensor_copy(decay[:, 1, :], z))
                link(nc.vector.tensor_tensor(z, z, decay[:, 1, :], ALU.subtract))
                nc.vector.tensor_copy(decay[:, 2, :], z).then_inc(decay_ready, 1)

            hg_n = 0
            for l, kind in enumerate(KIND):
                if l > 0:
                    scale_rows(2 * l)
                rest_actT("normT", l, 0, ROW_MIX + KT * l)
                if kind == "hgrn":
                    link(nc.vector.memset(mixT, 0.0))
                    dve.wait_ge(consts, 3)
                for s in STEPS[kind]:
                    key = (l, *s)
                    if s[0] == "use":
                        for u in range(2):
                            split_unit(MIX0[l] + 2 * s[1] + u + RING)
                    elif s[0] == "feat":
                        feature_tile(l, s)
                    elif s[0] == "tok" and s[1] == "v":
                        wait_full(dve, key)
                        if kind == "swa":
                            dst, src, bias = v[:, s[3], 0:256], bank(key, 256), swa_v_bias[:, SWA_LAYERS.index(l), :]
                        else:
                            cs = slice(s[2] * HALF, (s[2] + 1) * HALF)
                            dst, src, bias = v[:, s[3], cs], bank(key), v_bias[:, cs]
                        nc.vector.tensor_tensor(dst, src, bias, ALU.add).then_inc(v_ready, 1)
                    elif s[0] == "tok" and s[1] == "g":
                        cs = slice(s[2] * HALF, (s[2] + 1) * HALF)
                        dve.wait_ge(sig_ready, plan.order["sig_ready", key])
                        nc.vector.tensor_tensor(gate[:, s[3], cs], bank(key), gate[:, s[3], cs],
                                                ALU.mult).then_inc(gate_ready, 1)
                    elif s[0] == "gate":
                        forget_gates(l)
                    elif s[0] == "score":
                        max_of_scores(l, s[1])
                    elif s[0] == "turn":
                        turn(l, s[1])
                    elif s[0] == "value":
                        g = s[1]
                        wait_full(dve, key)
                        for t in range(TT):
                            pairs = rows[:, t, (g // 2) * HALF:(g // 2 + 1) * HALF]
                            dst = pairs.rearrange("p (h e d) -> p h e d", h=GROUP, e=2)[:, :, g % 2, :]
                            src = bank(key, T, t * T).rearrange("p (h d) -> p h d", h=GROUP)
                            inv = inv_denom[:, g % 2, GROUP * t:GROUP * t + GROUP]
                            last = nc.vector.tensor_tensor(dst, src, inv.unsqueeze(2).to_broadcast([P, GROUP, DH]),
                                                           ALU.mult)
                        last.then_inc(o_ready, 1)
                    elif s[0] == "level":
                        level(l, s[1], s[2])
                    elif s[0] == "cross":
                        heads = slice(GROUP * s[1], GROUP * s[1] + GROUP)
                        wait_full(dve, key)
                        nc.vector.tensor_copy(crossT[:, heads, :],
                                              bank(key).rearrange("p (h t) -> p h t", h=GROUP)).then_inc(mixT_ready, 1)
                    elif s[0] == "mix":
                        g, t = s[1], s[2]
                        hg_n += 1
                        dve.wait_ge(hg_sq, hg_n)
                        nc.vector.tensor_reduce(hg_sumsq[:], wide[:, 0:2, :].rearrange("p a (h n) -> p (a h) n", n=P),
                                                AX.X, ALU.add).then_inc(hg_sum, 1)
                        dve.wait_ge(hg_rn, hg_n)
                        cs = slice(g * HALF, (g + 1) * HALF)
                        nc.vector.tensor_tensor(rows[:, t, cs].rearrange("p (h n) -> p h n", h=GROUP),
                                                bank(key).rearrange("p (h n) -> p h n", h=GROUP),
                                                hg_rnorm[:].unsqueeze(2).to_broadcast([P, GROUP, P]),
                                                ALU.mult).then_inc(hg_scaled, 1)
                        dve.wait_ge(hg_scaled, hg_n)
                        nc.vector.tensor_tensor(rows[:, t, cs], rows[:, t, cs], gate[:, t, cs],
                                                ALU.mult).then_inc(hg_rows, 1)
                rest_actT("outT", l, 1, ROW_GN if kind == "hgrn" else None)
                for u in range(OUT_UNITS):
                    split_unit(OUT0[l] + u + RING)
                add_to_x("mixed", l, 2 * l + 1)
                scale_rows(2 * l + 1)
                rest_actT("normT", l, 2, ROW_MLP + KT * l)

                def mlp_pair(i, last):
                    def split_in_loop(j):
                        if last and j >= 4:
                            return
                        n = MLP0[l] + j + RING
                        dve.wait_ge(hi_done, i * 8 + (n + 1))
                        rest_unit(n)

                    for ab in range(2):
                        for f in range(4):
                            b = bank_of(("up", l, f))
                            n = 4 * ab + f
                            dve.wait_ge(half_ready, i * 8 + (plan.order["half_ready", (l, "mlp")] + n + 1))
                            nc.vector.tensor_tensor(half[:, f, :], psum[:, b, 0:T], half[:, f, :],
                                                    ALU.add).then_inc(up_sum, 1)
                            dve.wait_ge(up_sum, i * 8 + (4 + UP_TILES * l + n + 1))
                            nc.vector.scalar_tensor_tensor(wide[:, f, :], half[:, f, :], 0.0, half[:, f, :],
                                                           ALU.max, ALU.mult).then_inc(wide_ready, 1)
                            dve.wait_ge(hid_hi, i * 8 + (UP_TILES * l + n + 1))
                            nc.vector.tensor_tensor(hidden[:, ab, f, 1, :], wide[:, f, :],
                                                    f32(hidden[:, ab, f, 0, :]), ALU.subtract).then_inc(hid_lo, 1)
                            if ab == 1 and f < 2:
                                split_in_loop(f)
                    for j in range(2, 8):
                        split_in_loop(j)

                with dve.Fori(0, PAIRS - (l == DEPTH - 1)) as i:
                    mlp_pair(i, False)
                if l == DEPTH - 1:
                    mlp_pair(PAIRS - 1, True)
                add_to_x("down", l, 2 * l + 2)
            dve.wait_ge(gain_full, 16)
            for t in range(TT):
                dve.wait_ge(rnorm_ready, TT * 2 * DEPTH + t + 1)
                nc.vector.scalar_tensor_tensor(rows[:, t, :], x[:, t, :], rnorm[:, t:t + 1], final_gain,
                                               ALU.mult, ALU.mult).then_inc(rows_ready, 1)

        @block.tensor
        def _(pe):
            def take_bank(key):
                if plan.before[key]:
                    wait_free(pe, plan.before[key])
                return bank_of(key)

            def weight(ring, n, k, width, start, size):
                return ring[:, n % RING, k * width + start:k * width + start + size]

            def transposes(name, l, wait_rows):
                index = 2 * l if name == "normT" else l
                for t in range(TT):
                    wait_rows(t)
                    for b in range(4):
                        key = (name, int(index), b)
                        if t == 0:
                            take_bank(key)
                        for e in range(2):
                            k = 2 * b + e
                            last = nc.tensor.transpose(bank(key, P, e * T + t * P), rows[:, t, k * P:(k + 1) * P],
                                                       ident[:])
                        if t == TT - 1:
                            last.then_inc(bank_full[bank_of(key)], 1)

            def norm_transposes(phase):
                transposes("normT", phase / 2, lambda t: pe.wait_ge(rows_ready, TT * phase + t + 1))

            def out_transposes(l):
                def wait_rows(t):
                    if KIND[l] == "hgrn":
                        n = 4 * GATES.index(l)
                        pe.wait_ge(hg_rows, n + 3 + t)
                    elif t == 0:
                        wait_free(pe, (l, "value", GROUPS - 1))
                transposes("outT", l, wait_rows)

            def wait_actT(l, turned, k):
                if k % 2 == 0:
                    pe.wait_ge(actT_lo, turned_number(l, turned, k // 2))

            def feature_major(b, cols_of, wait_act, wait_weights):
                for k in range(KT):
                    wait_act(k)
                    if k % 4 == 0:
                        wait_weights(k // 4)
                    hi, lo = cols_of(w_hi, k), cols_of(w_lo, k)
                    both = actT[:, k, :, :].rearrange("p a t -> p (a t)")
                    if k == 0:
                        nc.tensor.matmul(psum[:, b, :], hi, both, start=True, stop=False)
                    last = nc.tensor.matmul(psum[:, b, 0:T], lo, actT[:, k, 0, :], start=False, stop=False)
                    if k > 0:
                        last = nc.tensor.matmul(psum[:, b, :], hi, both, start=False, stop=k == KT - 1)
                return last

            def token_major(dst, lhs, rhs_hi, rhs_lo, start, stop, skip=False):
                nc.tensor.matmul(dst, lhs[0], rhs_hi, start=start, stop=False, skip_group_check=skip)
                nc.tensor.matmul(dst, lhs[0], rhs_lo, start=False, stop=False, skip_group_check=skip)
                return nc.tensor.matmul(dst, lhs[1], rhs_hi, start=False, stop=stop, skip_group_check=skip)

            def act_lhs(k, t):
                return [actT[:, k, a, t * P:(t + 1) * P] for a in range(2)]

            pe.wait_ge(consts, 1)
            pe.wait_ge(small_full, 16 * SMALLS)
            for c, src in enumerate((params, params2)):
                key = ("param", c)
                nc.tensor.transpose(bank(key, P), src, ident[:]).then_inc(bank_full[take_bank(key)], 1)
            pe.wait_ge(consts, 2)

            def score(l, g):
                kind = KIND[l]
                needed = [("feat", c, 4 * (g // 2) + 3) for c in ("q" if kind == "swa" else "qk")]
                for s in needed:
                    wait_free(pe, (l, *s))
                if kind == "fox":
                    pe.wait_ge(decay_ready, 1)
                for b in range(3):
                    key = (l, "score", g, b)
                    take_bank(key)
                    for e in range(GROUP if b == 0 else 2):
                        j = e if b == 0 else 2 * (b - 1) + e
                        keys = P if b == 0 else T
                        dst = bank(key, keys, e * keys)
                        part, qt = slice(DH * (g % 2), DH * (g % 2) + DH), 4 * (g // 2) + j
                        kt = qt
                        if kind == "swa":
                            kv = (2 * qt + g % 2) // (HEADS // KV_HEADS)
                            kt = kv // 2 if kv % 2 == g % 2 else 2 + kv // 2
                        if kind == "fox":
                            for part3 in range(3):
                                nc.tensor.matmul(dst, pick[:, 2 * qt + g % 2, :], decay[:, part3, 0:keys],
                                                 start=e == 0 and part3 == 0, stop=False, skip_group_check=True)
                        t = 0 if b == 0 else 1
                        nc.tensor.matmul(dst, qT[part, qt, t * P:(t + 1) * P], kT[part, kt, 0:keys],
                                         start=e == 0 and kind == "swa", stop=False, skip_group_check=True)
                    mask = masks[:, 0:1, :] if b == 0 else masks[:, 1:3, :] if kind == "swa" else masks[:, 3:5, :]
                    mask = mask.rearrange("p a s -> p (a s)").unsqueeze(1)
                    heads, keys = (GROUP, P) if b == 0 else (2, T)
                    nc.tensor.matmul(bank(key).rearrange("p (h s) -> p h s", h=heads), ident_h[:],
                                     mask.to_broadcast([P, heads, keys]), start=False, stop=True,
                                     skip_group_check=True).then_inc(bank_full[b], 1)

            def turn(l, g):
                pe.wait_ge(exp_ready, 3 * (group_number(l, g) + 1))
                for b in range(3):
                    key = (l, "turn", g, b)
                    take_bank(key)
                    for h in range(GROUP):
                        last = nc.tensor.transpose(bank(key, P, h * P), probs[:, g % 2, h, b * P:(b + 1) * P], ident[:])
                    last.then_inc(bank_full[bank_of(key)], 1)

            def value(l, g):
                for b in range(3):
                    wait_free(pe, (l, "turn", g, b))
                wait_free(pe, (l, "tok", "v", 0 if KIND[l] == "swa" else g // 2, 1))
                key = (l, "value", g)
                take_bank(key)
                for h in range(GROUP):
                    c = 2 * (GROUP * (g // 2) + h) + g % 2
                    if KIND[l] == "swa":
                        c //= HEADS // KV_HEADS
                    vc = [v[:, t, c * DH:(c + 1) * DH] for t in range(TT)]
                    nc.tensor.matmul(bank(key, DH, h * DH), probsT[:, g % 2, 0, h, :], vc[0], start=True, stop=True)
                    dst = bank(key, DH, T + h * DH)
                    nc.tensor.matmul(dst, probsT[:, g % 2, 1, h, :], vc[0], start=True, stop=False)
                    last = nc.tensor.matmul(dst, probsT[:, g % 2, 2, h, :], vc[1], start=False, stop=True)
                last.then_inc(bank_full[bank_of(key)], 1)

            def level(l, g, j):
                if j == 0:
                    wait_free(pe, (l, "feat", "f", GROUP * g + GROUP - 1))
                else:
                    pe.wait_ge(level_ready, plan.order["level_ready", (l, "level", g, j - 1)])
                for t in range(TT if j < LEVELS else 1):
                    key = (l, "level", g, j, t) if j < LEVELS else (l, "cross", g)
                    take_bank(key)
                    s_tile = slice(t * P, (t + 1) * P)
                    t_tile = s_tile if j < LEVELS else slice(P, T)
                    for h in range(GROUP):
                        last = nc.tensor.matmul(bank(key, P, h * P), kT[:, GROUP * g + h, s_tile],
                                                qT[:, GROUP * g + h, t_tile], start=True, stop=True)
                    last.then_inc(bank_full[bank_of(key)], 1)

            def mix(l, g, t):
                key = (l, "mix", g, t)
                take_bank(key)
                wait_free(pe, (l, "level", g, LEVELS - 1, TT - 1))
                wait_free(pe, (l, "cross", g))
                wait_free(pe, (l, "tok", "i", g, 1))
                for h in range(GROUP):
                    head = GROUP * g + h
                    dst = bank(key, P, h * P)
                    vc = [v[:, a, head * P:(head + 1) * P] for a in range(TT)]
                    if t == 1:
                        nc.tensor.matmul(dst, crossT[:, head, :], vc[0], start=True, stop=False)
                    last = nc.tensor.matmul(dst, mixT[:, head, t * P:(t + 1) * P], vc[t], start=t == 0, stop=True)
                last.then_inc(bank_full[bank_of(key)], 1)

            for l, kind in enumerate(KIND):
                norm_transposes(2 * l)
                for s in STEPS[kind]:
                    key = (l, *s)
                    if s[0] in ("feat", "tok"):
                        n = MIX0[l] + 2 * CHUNK_OF[kind](s)
                        b = take_bank(key)
                    if s[0] == "feat":
                        def cols_of(ring, k, n=n, j=s[2] % 4):
                            return weight(ring, n + k // 4, k % 4, HALF, j * P, P)

                        last = feature_major(b, cols_of, lambda k: wait_actT(l, 0, k),
                                             lambda u, n=n: pe.wait_ge(lo_done, n + u + 1))
                        last.then_inc(bank_full[b], 1)
                    elif s[0] == "tok":
                        start, width = (256, 256) if kind == "swa" else (0, HALF)
                        for k in range(KT):
                            if k % 4 == 0:
                                pe.wait_ge(lo_done, n + k // 4 + 1)
                            rhs = [weight(r, n + k // 4, k % 4, HALF, start, width) for r in (w_hi, w_lo)]
                            last = token_major(psum[:, b, 0:width], act_lhs(k, s[3]), *rhs, k == 0, k == KT - 1)
                        last.then_inc(bank_full[b], 1)
                    elif s[0] == "gate":
                        b = take_bank(key)
                        pe.wait_ge(gate_split, 1)
                        for t in range(TT):
                            for k in range(KT):
                                wait_actT(l, 0, k)
                                last = token_major(psum[:, b, t * HEADS:(t + 1) * HEADS], act_lhs(k, t),
                                                   gate_whi[:, k, :], gate_wlo[:, k, :], k == 0, k == KT - 1)
                        last.then_inc(bank_full[b], 1)
                        b = take_bank((l, "gateT"))
                        pe.wait_ge(gate_rows_ready, 1)
                        for t in range(TT):
                            last = nc.tensor.transpose(psum[:, b, t * P:(t + 1) * P], gate_rows[:, t, :], ident[:])
                        last.then_inc(bank_full[b], 1)
                    elif s[0] == "score":
                        score(l, s[1])
                    elif s[0] == "turn":
                        turn(l, s[1])
                    elif s[0] == "value":
                        value(l, s[1])
                    elif s[0] == "level":
                        level(l, s[1], s[2])
                    elif s[0] == "cross":
                        level(l, s[1], LEVELS)
                    elif s[0] == "mix":
                        mix(l, s[1], s[2])
                out_transposes(l)
                for t in range(TT):
                    for e in range(2):
                        take_bank(("mixed", l, 2 * t + e))
                    for u in range(OUT_UNITS):
                        n = OUT0[l] + u
                        pe.wait_ge(lo_done, n + 1)
                        for kk in range(2):
                            k = 2 * u + kk
                            wait_actT(l, 1, k)
                            for e in range(2):
                                rhs = [weight(r, n, kk, D, e * HALF, HALF) for r in (w_hi, w_lo)]
                                last = token_major(psum[:, 2 * t + e, :], act_lhs(k, t), *rhs, k == 0, k == KT - 1)
                                if k == KT - 1:
                                    last.then_inc(bank_full[2 * t + e], 1)
                        if t == TT - 1 and u < OUT_UNITS - 1:
                            last.then_inc(out_used, 1)
                norm_transposes(2 * l + 1)
                for b in range(4):
                    take_bank(("down", l, b))
                    nc.tensor.matmul(psum[:, b, :].rearrange("p (a n) -> p a n", a=4), ident_h[:],
                                     masks[:, 3:4, :].to_broadcast([P, 4, P]), start=True, stop=True)
                with pe.Fori(0, PAIRS) as i:
                    for ab in range(2):
                        n = MLP0[l] + 2 * ab
                        for f in range(4):
                            b = bank_of(("up", l, f))
                            pe.wait_ge(up_sum, i * 8 + (UP_TILES * l + 4 * ab + f + 1))
                            last = feature_major(b, lambda ring, k: weight(ring, n + k // 4, k % 4, HALF, f * P, P),
                                                 lambda k: wait_actT(l, 2, k),
                                                 lambda u: pe.wait_ge(lo_done, i * 8 + (n + u + 1)))
                            last.then_inc(bank_full[b], 1)
                    for ab in range(2):
                        for t in range(TT):
                            for u in range(2):
                                n = MLP0[l] + 4 + 2 * ab + u
                                pe.wait_ge(lo_done, i * 8 + (n + 1))
                                for kk in range(2):
                                    k = 2 * u + kk
                                    if t == 0:
                                        pe.wait_ge(hid_lo, i * 8 + (UP_TILES * l + 4 * ab + k + 1))
                                    lhs = [hidden[:, ab, k, a, t * P:(t + 1) * P] for a in range(2)]
                                    for e in range(2):
                                        rhs = [weight(r, n, kk, D, e * HALF, HALF) for r in (w_hi, w_lo)]
                                        last = token_major(psum[:, 2 * t + e, :], lhs, *rhs, False, True, skip=True)
                                if t == 1:
                                    last.then_inc(down_used, 1)
                                elif ab == 1 and u == 1:
                                    last.then_inc(down_tile0, 1)


_INS = ["x", "norm_mix", "norm_mlp", "norm_final", "w_up", "w_down", "swa_w_qkv", "swa_b_qkv", "swa_sinks", "swa_w_o",
        "hgrn_w_in", "hgrn_lb_logits", "hgrn_g_norm", "hgrn_w_o", "fox_w_in", "fox_b_in", "fox_w_o"]


def kernel(**inputs):
    import numpy as np
    import concourse.bacc as bacc
    from concourse.bass_utils import run_bass_kernel_spmd

    nc = bacc.Bacc("TRN2", target_bir_lowering=False, num_devices=1)
    arrays, args = {}, []
    for name in _INS:
        a = np.ascontiguousarray(inputs[name])
        arrays[f"in_{name}"] = a
        args.append(nc.dram_tensor(f"in_{name}", a.shape, mybir.dt.from_np(a.dtype), kind="ExternalInput").ap())
    args.append(nc.dram_tensor("out", (1, T, D), F32, kind="ExternalOutput").ap())
    build_trunk(nc, *args)
    result = run_bass_kernel_spmd(nc, [arrays], core_ids=[0])
    return result.results[0]["out"]
```

```python
import concourse.bass as bass
from concourse import mybir
from contextlib import ExitStack

F32 = mybir.dt.float32
F32R = mybir.dt.float32r
BF16 = mybir.dt.bfloat16
I16 = mybir.dt.int16
ALU = mybir.AluOpType
ACT = mybir.ActivationFunctionType
AX = mybir.AxisListType

P = 128
D = 1024
T = 256
DEPTH = 4
TT = T // P
KT = D // P
FF = 4 * D
EPS = 1e-6
HALF = 512
UNIT = 2048
RING = 4
RAWS = 2
PAIRS = FF // (2 * HALF)
MASKED = -1.0e30

HEADS = 16
KV_HEADS = 4
DH = 64
GROUP = 4
GROUPS = HEADS // GROUP
Q_SCALE = DH ** -0.5
HG_HEADS = 8
LEVELS = 8

MIXERS = ["swa", "hgrn", "fox"]
KIND = [MIXERS[i % 3] for i in range(DEPTH)]
MIX_UNITS = {"swa": 6, "hgrn": 16, "fox": 12}
OUT_UNITS = 4
MLP_UNITS = 8 * PAIRS


def unit_bases():
    at, mix, out, mlp = 0, [], [], []
    for kind in KIND:
        mix.append(at)
        out.append(at + MIX_UNITS[kind])
        mlp.append(at + MIX_UNITS[kind] + OUT_UNITS)
        at = mlp[-1] + MLP_UNITS
    return mix, out, mlp, at


MIX0, OUT0, MLP0, ALL_UNITS = unit_bases()

CHUNKS = {"swa": [2, 0, 1], "hgrn": [0, 2, 1, 3, 4, 5, 6, 7], "fox": [2, 0, 4, 3, 1, 5]}



def split(*units):
    return [s for n in units for s in (("round", n), ("rest", n))]


def after(n, first, second, third=None):
    return [("round", n), *first, ("rest", n), ("round", n + 1), *second, ("rest", n + 1), *(third or [])]


def projection(n):
    return [("proj", 1, 0), ("round", n), ("rest", n), ("round", n + 1), ("proj", 1, 1), ("rest", n + 1),
            ("proj", 1, 2), ("proj", 1, 3)]


STEPS = {
    "swa": (split(2, 3) + [("spread",), ("feat", "k", 0), ("feat", "k", 1), ("root",), ("tok", "v", 0, 0), ("tok", "v", 0, 1)]
            + after(4, [("feat", "q", 0)], [("feat", "q", 1)], [("feat", "q", 2), ("feat", "q", 3)])
            + after(6, [("score", 0), ("feat", "q", 4)], [("feat", "q", 5)], [("score", 1)])
            + [("feat", "q", 6), ("turn", 0), ("feat", "q", 7), ("value", 0), ("turn", 1), ("score", 2), ("value", 1)]
            + [("outT", 0), ("score", 3), ("turn", 2), ("proj", 0, 3)]
            + after(8, [("value", 2), ("turn", 3)], [("proj", 0, 0), ("value", 3)], [("proj", 0, 1), ("outT", 1)])
            + [("proj", 0, 2)] + projection(10)),
    "fox": (split(2, 3) + [("spread",), ("feat", "k", 0), ("feat", "k", 1), ("root",), ("gate",), ("feat", "k", 2), ("feat", "k", 3)]
            + after(4, [("feat", "q", 0)], [("feat", "q", 1)], [("feat", "q", 2), ("feat", "q", 3)])
            + after(6, [("tok", "v", 0, 0), ("score", 0)], [("tok", "v", 0, 1)])
            + after(8, [("feat", "k", 4)], [("feat", "k", 5)], [("score", 1), ("feat", "k", 6), ("turn", 0)])
            + [("feat", "k", 7), ("value", 0), ("turn", 1)]
            + after(10, [("feat", "q", 4), ("value", 1)], [("feat", "q", 5)], [("feat", "q", 6), ("feat", "q", 7)])
            + after(12, [("score", 2), ("tok", "v", 1, 0)], [("score", 3), ("tok", "v", 1, 1)])
            + [("turn", 2), ("outT", 0), ("turn", 3), ("value", 2)]
            + after(14, [("proj", 0, 3)], [("value", 3), ("proj", 0, 0)], [("outT", 1)])
            + [("proj", 0, 1), ("proj", 0, 2)] + projection(16)),
    "hgrn": (split(2, 3) + [("spread",), ("feat", "q", 0), ("feat", "q", 1), ("root",), ("feat", "q", 2), ("feat", "q", 3)]
             + after(4, [("feat", "f", 0)], [("feat", "f", 1)], [("feat", "f", 2), ("feat", "f", 3)])
             + after(6, [("feat", "q", 4), ("level", 0, 0)], [("feat", "q", 5), ("level", 0, 1)])
             + [("feat", "q", 6), ("level", 0, 2), ("feat", "q", 7), ("level", 0, 3)]
             + after(8, [("feat", "f", 4), ("level", 0, 4)], [("feat", "f", 5), ("level", 0, 5)])
             + [("feat", "f", 6), ("level", 0, 6), ("feat", "f", 7), ("level", 0, 7), ("cross", 0)]
             + after(10, [("tok", "i", 0, 0), ("level", 1, 0)], [("tok", "i", 0, 1), ("level", 1, 1)])
             + after(12, [("tok", "i", 1, 0), ("level", 1, 2)], [("tok", "i", 1, 1), ("level", 1, 3)])
             + after(14, [("tok", "g", 0, 0), ("level", 1, 4)], [("tok", "g", 0, 1), ("level", 1, 5)])
             + [("mix", 0, 0), ("mix", 0, 1)]
             + after(16, [("tok", "g", 1, 0), ("level", 1, 6)], [("tok", "g", 1, 1), ("level", 1, 7)])
             + [("cross", 1), ("outT", 0), ("proj", 0, 1)]
             + after(18, [("mix", 1, 0)], [("mix", 1, 1), ("proj", 0, 0)], [("proj", 0, 2)])
             + [("outT", 1), ("proj", 0, 3)] + projection(20)),
}
IN_BANK_3 = {("swa", "feat", "q", 7), ("fox", "feat", "k", 7), ("fox", "feat", "q", 4), ("fox", "tok", "v", 1, 1)}
OUTT_BANKS = {"swa": (3, 7, 4, 5), "fox": (3, 7, 4, 5), "hgrn": (4, 5, 6, 7)}
CHUNK_OF = {
    "swa": lambda s: 0 if s[1] in "kv" else 1 + s[2] // 4,
    "fox": lambda s: {"k": (0, 3), "q": (1, 4)}[s[1]][s[2] // 4] if s[0] == "feat" else (2, 5)[s[2]],
    "hgrn": lambda s: {"q": (0, 2), "f": (1, 3)}[s[1]][s[2] // 4] if s[0] == "feat" else {"i": 4, "g": 6}[s[1]] + s[2],
}


class Plan:

    def __init__(self):
        self.full, self.free, self.before = {}, {}, {}
        self.order = {}
        self.fills, self.last, self.counts, self.turn = [0] * 8, [None] * 8, {}, 0
        self.walk()

    def take(self, key, bank, signal, times=1, count=1):
        self.before[key] = self.last[bank]
        self.last[bank] = key
        self.fills[bank] += 1
        self.full[key] = (bank, self.fills[bank])
        self.fills[bank] += times - 1
        self.counts[signal] = self.counts.get(signal, 0) + count
        self.free[key] = (signal, self.counts[signal])

    def note(self, key, signal, count=1):
        self.counts[signal] = self.counts.get(signal, 0) + count
        self.order[signal, key] = self.counts[signal]

    def work(self, key, signal):
        if (KIND[key[0]], *key[1:]) in IN_BANK_3:
            self.take(key, 3, signal)
            return
        self.take(key, 4 + self.turn % 4, signal)
        self.turn += 1

    def walk(self):
        for c in range(2):
            self.take(("param", c), 4 + c, "cols_copied")
        for l, kind in enumerate(KIND):
            for b in range(4):
                self.take(("normT", 2 * l, b), 4 + b, "actT_lo")
            self.turn = 0
            for s in STEPS[kind]:
                if s[0] == "feat":
                    self.work((l, *s), "feat_sum")
                    for signal in ("half_ready", "wide_ready", "feat_ready"):
                        self.note((l, *s), signal)
                    if kind == "hgrn":
                        self.note((l, *s), "sig_ready")
                if s[0] == "root":
                    self.work((l, *s), "spread_ready")
                if s[0] == "tok":
                    self.work((l, *s), "gate_ready" if s[1] == "g" else "v_ready")
                    if s[1] == "g":
                        self.note((l, *s), "sig_ready")
                if s[0] == "gate":
                    self.work((l, *s), "gate_rows_ready")
                    self.work((l, "gateT"), "gateT_ready")
                if s[0] == "score":
                    for b in range(3):
                        self.take((l, *s, b), b, "exp_ready")
                if s[0] == "turn":
                    for b in range(3):
                        self.take((l, *s, b), 4 + b, "turned_v" if b == 1 else "turned_a")
                if s[0] == "value":
                    self.take((l, *s), 7, "o_ready")
                if s[0] == "level":
                    for t in range(TT):
                        self.take((l, *s, t), 2 * (s[2] % 2) + t, "level_out")
                    self.note((l, *s), "level_ready")
                if s[0] == "cross":
                    self.take((l, *s), 0, "mixT_ready")
                if s[0] == "mix":
                    self.take((l, *s), 2 + s[2], "hg_scaled")
                if s[0] == "outT":
                    for b in (2 * s[1], 2 * s[1] + 1):
                        self.take(("outT", l, b), OUTT_BANKS[kind][b], "actT_lo")
                if s[0] == "proj" and s[1] == 0:
                    self.take(("mixed", l, s[2]), s[2], "x_ready", times=s[2] < 3, count=0)
            for b in range(4):
                self.note(("mixed", l, b), "x_ready")
                self.free[("mixed", l, b)] = ("x_ready", self.counts["x_ready"])
            for b in range(4):
                self.take(("normT", 2 * l + 1, b), 4 + b, "actT_lo")
            for b in range(4):
                self.take(("up", l, b), 4 + b, "up_sum", 2 * PAIRS)
            self.counts["up_sum"] += 8 * PAIRS - 4
            for signal in ("half_ready", "wide_ready"):
                self.note((l, "mlp"), signal, 0)
                self.counts[signal] += 8 * PAIRS
            for b in range(4):
                self.free[("up", l, b)] = ("up_sum", self.counts["up_sum"] + 4)
            for b in range(4):
                self.take(("down", l, b), b, "x_ready", 0)


ROW_MIX, ROW_MLP, ROW_LB, ROW_GN, ROW_SWA = 0, 32, 64, 96, 104
SWA_ROWS = 10
HG_LAYER = 1
SWA_LAYERS = [l for l in range(DEPTH) if KIND[l] == "swa"]
SMALLS, BCASTS = 7, 7


def build_trunk(nc, x_in, norm_mix, norm_mlp, norm_final, w_up, w_down, swa_w_qkv, swa_b_qkv, swa_sinks, swa_w_o,
                hgrn_w_in, hgrn_lb_logits, hgrn_g_norm, hgrn_w_o, fox_w_in, fox_b_in, fox_w_o, out):
    plan = Plan()
    ctx = ExitStack()
    with ctx:
        def sb(name, shape, dt=F32):
            return ctx.enter_context(nc.sbuf_tensor(name, shape, dt))

        def sem(name):
            return ctx.enter_context(nc.semaphore(name))

        raw = sb("raw", [P, RAWS, UNIT])
        w_hi = sb("w_hi", [P, RING, UNIT], F32R)
        w_lo = sb("w_lo", [P, RING, UNIT], F32R)
        x = sb("x", [P, TT, D])
        rows = sb("rows", [P, TT, D])
        actT = sb("actT", [P, KT, 2, T], F32R)
        hidden = sb("hidden", [P, 2, 4, 2, T], F32R)
        half = sb("half", [P, 4, T])
        wide = sb("wide", [P, 4, T])
        qT = sb("qT", [P, 8, T])
        kT = sb("kT", [P, 8, T])
        v = sb("v", [P, TT, D])
        scratch = sb("scratch", [P, 6144])
        probs = scratch[:, 0:3072].rearrange("p (g h s) -> p g h s", g=2, h=GROUP)
        probsT = scratch[:, 3072:6144].rearrange("p (g b h s) -> p g b h s", g=2, b=3, h=GROUP)
        mixT = scratch[:, 0:2048].rearrange("p (h t) -> p h t", h=HG_HEADS)
        crossT = scratch[:, 2048:3072].rearrange("p (h t) -> p h t", h=HG_HEADS)
        gate = scratch[:, 3072:5120].rearrange("p (t n) -> p t n", t=TT)
        keep = scratch[:, 5120:6144].rearrange("p (h t) -> p h t", h=GROUP)
        span = sb("span", [P, GROUP * 254])
        level_mask = sb("level_mask", [P, LEVELS, P], BF16)
        ident = sb("ident", [P, P])
        ident_h = sb("ident_h", [P, P], BF16)
        masks = sb("masks", [P, 5, P], BF16)
        pick = sb("pick", [HEADS, HEADS, P], BF16)
        decay = sb("decay", [HEADS, 3, T], BF16)
        cols = sb("cols", [P, P])
        foxcols = sb("foxcols", [P, 16])
        q_bias = sb("q_bias", [P, 3, 8])
        v_bias = sb("v_bias", [P, D])
        swa_v_bias = sb("swa_v_bias", [P, 2, 256])
        sinks = sb("sinks", [P, 2, HEADS])
        neg_sinks = sb("neg_sinks", [P, 2, HEADS])
        gate_bias = sb("gate_bias", [P, HEADS])
        gate_w = sb("gate_w", [P, KT, HEADS])
        gate_whi = sb("gate_whi", [P, KT, HEADS], F32R)
        gate_wlo = sb("gate_wlo", [P, KT, HEADS], F32R)
        sumsq = sb("sumsq", [P, TT])
        mean = sb("mean", [P, GROUP])
        rnorm = sb("rnorm", [P, TT])
        spread = sb("spread", [P, T])
        hg_sumsq = sb("hg_sumsq", [P, GROUP])
        hg_rnorm = sb("hg_rnorm", [P, GROUP])
        minus_half = sb("minus_half", [P, GROUP])
        minus_one = sb("minus_one", [P, 1])
        neg_max = sb("neg_max", [P, 2, 2 * GROUP])
        sink_shift = sb("sink_shift", [P, 2, 2 * GROUP])
        sink_exp = sb("sink_exp", [P, 2, 2 * GROUP])
        denom = sb("denom", [P, 2, 2 * GROUP])
        inv_denom = sb("inv_denom", [P, 2, 2 * GROUP])
        lb = sb("lb", [P, DEPTH + 3, HG_HEADS])
        lower = sb("lower", [P, 2, HG_HEADS])

        params = qT[:, 0, 0:P]
        params2 = qT[:, 0, P:2 * P]
        gate_rows = scratch[:, 0:2 * P].rearrange("p (t h) -> p t h", t=TT)
        fox_tmp = scratch[0:HEADS, 2 * P:2 * P + 4 * T].rearrange("p (a t) -> p a t", a=4)
        final_gain = v[:, 0, :]

        psum = ctx.enter_context(nc.psum_tensor("psum", [P, 8, HALF], F32))

        raw_full = [sem(f"raw_full{i}") for i in range(RAWS)]
        hi_done = sem("hi_done")
        lo_done = sem("lo_done")
        out_used = sem("out_used")
        tail_used = sem("tail_used")
        down_tile0 = sem("down_tile0")
        bank_full = [sem(f"bank_full{b}") for b in range(8)]
        x_in_full = sem("x_in_full")
        small_full = sem("small_full")
        bcast_full = sem("bcast_full")
        gain_full = sem("gain_full")
        zeroed = sem("zeroed")
        consts = sem("consts")
        pool_step = sem("pool_step")
        cols_copied = sem("cols_copied")
        bias_ready = sem("bias_ready")
        lb_shifted = sem("lb_shifted")
        lb_exp = sem("lb_exp")
        x_ready = sem("x_ready")
        sq_ready = sem("sq_ready")
        rnorm_ready = sem("rnorm_ready")
        spread_ready = sem("spread_ready")
        rows_ready = sem("rows_ready")
        actT_hi = sem("actT_hi")
        actT_lo = sem("actT_lo")
        half_ready = sem("half_ready")
        wide_ready = sem("wide_ready")
        sig_ready = sem("sig_ready")
        up_sum = sem("up_sum")
        hid_hi = sem("hid_hi")
        hid_lo = sem("hid_lo")
        feat_sum = sem("feat_sum")
        feat_ready = sem("feat_ready")
        v_ready = sem("v_ready")
        gate_ready = sem("gate_ready")
        max_ready = sem("max_ready")
        exp_ready = sem("exp_ready")
        sink_ready = sem("sink_ready")
        turned_a = sem("turned_a")
        turned_v = sem("turned_v")
        o_ready = sem("o_ready")
        level_ready = sem("level_ready")
        level_out = sem("level_out")
        mixT_ready = sem("mixT_ready")
        hg_sq = sem("hg_sq")
        hg_sum = sem("hg_sum")
        hg_rn = sem("hg_rn")
        hg_scaled = sem("hg_scaled")
        hg_rows = sem("hg_rows")
        gate_split = sem("gate_split")
        gate_hi_done = sem("gate_hi_done")
        gate_rows_ready = sem("gate_rows_ready")
        gateT_ready = sem("gateT_ready")
        gate_log = sem("gate_log")
        decay_ready = sem("decay_ready")
        dve_step = sem("dve_step")
        act_step = sem("act_step")
        out_done = sem("out_done")
        signals = {"cols_copied": cols_copied, "actT_lo": actT_lo, "feat_sum": feat_sum, "spread_ready": spread_ready, "v_ready": v_ready,
                   "gate_ready": gate_ready, "gate_rows_ready": gate_rows_ready, "gateT_ready": gateT_ready,
                   "exp_ready": exp_ready, "turned_a": turned_a, "turned_v": turned_v, "o_ready": o_ready,
                   "level_out": level_out, "mixT_ready": mixT_ready, "hg_scaled": hg_scaled, "x_ready": x_ready,
                   "up_sum": up_sum}

        block = ctx.enter_context(nc.Block())

        def bank(key, width=HALF, start=0):
            return psum[:, plan.full[key][0], start:start + width]

        def bank_of(key):
            return plan.full[key][0]

        def wait_full(engine, key):
            b, n = plan.full[key]
            engine.wait_ge(bank_full[b], n)

        def wait_free(engine, key):
            signal, n = plan.free[key]
            engine.wait_ge(signals[signal], n)

        def group_number(l, g):
            return GROUPS * sum(KIND[m] != "hgrn" for m in range(l)) + g

        def turned_number(l, turned, b):
            return 4 * (3 * l + turned) + b + 1

        def x_count(phase, b):
            return 4 * (phase - 1) + b + 1

        UP_TILES = 8 * PAIRS
        TAILS = 2 + 4 * PAIRS
        GATES = [l for l in range(DEPTH) if KIND[l] == "hgrn"]

        def wait_unit_used(engine, n):
            l = max(m for m in range(DEPTH) if MIX0[m] <= n)
            if n < OUT0[l]:
                place = (n - MIX0[l]) // 2
                tiles = [s for s in STEPS[KIND[l]] if s[0] in ("feat", "tok") and CHUNK_OF[KIND[l]](s) == place]
                wait_full(engine, (l, *tiles[-1]))
            elif n < OUT0[l] + 2:
                engine.wait_ge(out_used, 2 * l + n - OUT0[l] + 1)
            elif n < MLP0[l]:
                engine.wait_ge(tail_used, TAILS * l + n - OUT0[l] - 1)
            else:
                assert MLP0[l] + MLP_UNITS - n in (1, 2)
                engine.wait_ge(tail_used, TAILS * (l + 1) - (MLP0[l] + MLP_UNITS - n - 1))

        @block.sync
        def _(sp):
            def load(n, src, columns):
                slot = n % RAWS
                if n >= RAWS:
                    sp.wait_ge(lo_done, n - RAWS + 1)
                dst = raw[:, slot, :].rearrange("p (k n) -> p k n", n=columns)
                sp.dma_start(dst, src).then_inc(raw_full[slot], 16)

            for t in range(TT):
                sp.dma_start(x[:, t, :], x_in[0, t * P:(t + 1) * P, :]).then_inc(x_in_full, 16)
            for l, kind in enumerate(KIND):
                w_in = {"swa": swa_w_qkv, "hgrn": hgrn_w_in, "fox": fox_w_in}[kind][l // 3]
                w_o = {"swa": swa_w_o, "hgrn": hgrn_w_o, "fox": fox_w_o}[kind][l // 3]
                w_in = w_in.rearrange("(k p) n -> p k n", p=P)
                w_o = w_o.rearrange("(k p) n -> p k n", p=P)
                for c, chunk in enumerate(CHUNKS[kind]):
                    for u in range(2):
                        load(MIX0[l] + 2 * c + u, w_in[:, 4 * u:4 * u + 4, chunk * HALF:(chunk + 1) * HALF], HALF)
                for u in range(OUT_UNITS):
                    load(OUT0[l] + u, w_o[:, 2 * u:2 * u + 2, :], D)
                up = w_up[l].rearrange("(k p) n -> p k n", p=P)
                down = w_down[l].rearrange("(k p) n -> p k n", p=P)
                with sp.Fori(0, PAIRS) as i:
                    for j in range(8):
                        ab, u = (j // 2) % 2, j % 2
                        if j < 4:
                            src = up[:, 4 * u:4 * u + 4, bass.ds((i * 2 + ab) * HALF, HALF)]
                        else:
                            src = down[:, bass.ds((i * 2 + ab) * 4 + 2 * u, 2), :]
                        slot = (MLP0[l] + j) % RAWS
                        sp.wait_ge(lo_done, i * 8 + (MLP0[l] + j - RAWS + 1))
                        dst = raw[:, slot, :].rearrange("p (k n) -> p k n", n=HALF if j < 4 else D)
                        sp.dma_start(dst, src).then_inc(raw_full[slot], 16)
            for t in range(TT):
                sp.wait_ge(rows_ready, t + 1)
                sp.dma_start(out[0, t * P:(t + 1) * P, :], rows[:, t, :]).then_inc(out_done, 16)
            sp.wait_ge(out_done, 16 * TT)

        @block.gpsimd
        def _(pool):
            steps = [0]

            def link(ins):
                steps[0] += 1
                ins.then_inc(pool_step, 1)
                pool.wait_ge(pool_step, steps[0])

            nc.gpsimd.memset(qT[:, 0, :], 0.0).then_inc(zeroed, 1)
            link(nc.gpsimd.memset(minus_half[:], -0.5))
            link(nc.gpsimd.memset(minus_one[:], -1.0))
            link(nc.gpsimd.memset(ident[:], 0.0))
            nc.gpsimd.affine_select(out=ident[:], in_=ident[:], compare_op=ALU.not_equal, fill=1.0, base=0,
                                    pattern=[[-1, P]], channel_multiplier=1).then_inc(consts, 1)
            pool.wait_ge(consts, 1)
            link(nc.gpsimd.tensor_copy(ident_h[:], ident[:]))
            link(nc.gpsimd.memset(masks[:], 0.0))
            for m in (0, 2, 4):
                link(nc.gpsimd.affine_select(out=masks[:, m, :], in_=masks[:, m, :], compare_op=ALU.is_ge, fill=MASKED,
                                             base=0, pattern=[[-1, P]], channel_multiplier=1))
            nc.gpsimd.affine_select(out=masks[:, 1, :], in_=masks[:, 1, :], compare_op=ALU.is_gt, fill=MASKED, base=0,
                                    pattern=[[1, P]], channel_multiplier=-1).then_inc(consts, 1)

            def norm_root(phase):
                for t in range(TT):
                    pool.wait_ge(sq_ready, TT * phase + t + 1)
                    link(nc.gpsimd.tensor_scalar(mean[:, 0:1], sumsq[:, t:t + 1], 1.0 / D, EPS, ALU.mult, ALU.add))
                    exponent = minus_one[:] if phase % 2 else minus_half[:, 0:1]
                    nc.gpsimd.tensor_tensor(rnorm[:, t:t + 1], mean[:, 0:1], exponent, ALU.pow).then_inc(rnorm_ready, 1)
                    pool.wait_ge(rnorm_ready, TT * phase + t + 1)

            norm_root(0)
            link(nc.gpsimd.memset(pick[:], 0.0))
            link(nc.gpsimd.affine_select(out=pick[:], in_=pick[:], compare_op=ALU.not_equal, fill=1.0, base=0,
                                         pattern=[[-1, HEADS], [0, P]], channel_multiplier=1))
            link(nc.gpsimd.memset(level_mask[:], 0.0))
            for j in range(1, LEVELS):
                size = 2 ** (j - 1)
                blocks = P // (2 * size)
                right = level_mask[:, j, :].rearrange("p (b h w) -> p b h w", h=2, w=size)[:, :, 1, :]
                link(nc.gpsimd.memset(right, 1.0))
                link(nc.gpsimd.affine_select(out=right, in_=right, compare_op=ALU.is_ge, fill=0.0, base=0,
                                             pattern=[[-2 * size, blocks], [0, size]], channel_multiplier=1))
                link(nc.gpsimd.affine_select(out=right, in_=right, compare_op=ALU.is_ge, fill=0.0, base=size - 1,
                                             pattern=[[2 * size, blocks], [0, size]], channel_multiplier=-1))
            nc.gpsimd.tensor_copy(level_mask[:, 0, :], ident[:]).then_inc(consts, 1)
            hg_n = 0
            for l, kind in enumerate(KIND):
                if l > 0:
                    norm_root(2 * l)
                if kind == "hgrn":
                    for _ in range(2 * TT):
                        hg_n += 1
                        pool.wait_ge(hg_sum, hg_n)
                        link(nc.gpsimd.tensor_scalar(mean[:], hg_sumsq[:], 1.0 / P, EPS, ALU.mult, ALU.add))
                        nc.gpsimd.tensor_tensor(hg_rnorm[:], mean[:], minus_half[:], ALU.pow).then_inc(hg_rn, 1)
                        pool.wait_ge(hg_rn, hg_n)
                norm_root(2 * l + 1)
            norm_root(2 * DEPTH)

        @block.scalar
        def _(act):
            steps = [0]

            def link(ins):
                steps[0] += 1
                ins.then_inc(act_step, 1)
                act.wait_ge(act_step, steps[0])

            act.wait_ge(zeroed, 1)
            smalls = [(params[ROW_MIX:ROW_MIX + 32, :], norm_mix.rearrange("l (k p) -> (l k) p", p=P)),
                      (params[ROW_MLP:ROW_MLP + 32, :], norm_mlp.rearrange("l (k p) -> (l k) p", p=P)),
                      (params[ROW_LB:ROW_LB + 32, :], hgrn_lb_logits.rearrange("l (k p) -> (l k) p", p=P)),
                      (params[ROW_GN:ROW_GN + 8, :], hgrn_g_norm.rearrange("l (k p) -> (l k) p", p=P)),
                      (params2[0:16, :], fox_b_in[0, 0:2 * D].rearrange("(k p) -> k p", p=P))]
            for a in range(2):
                row = ROW_SWA + SWA_ROWS * a
                src = swa_b_qkv[a, 0:SWA_ROWS * P].rearrange("(k p) -> k p", p=P)
                smalls.append((params[row:row + SWA_ROWS, :], src))
            assert len(smalls) == SMALLS
            for dst, src in smalls:
                act.dma_start(dst, src).then_inc(small_full, 16)
            bcasts = [(v_bias[:], fox_b_in[0, 2 * D:3 * D].partition_broadcast(P)),
                      (gate_bias[:], fox_b_in[0, 3 * D:3 * D + HEADS].partition_broadcast(P)),
                      (gate_w[:], fox_w_in[0, :, 3 * D:3 * D + HEADS].rearrange("(k p) n -> p k n", p=P))]
            for a in range(2):
                bcasts.append((swa_v_bias[:, a, :], swa_b_qkv[a, D + 256:D + 512].partition_broadcast(P)))
                bcasts.append((sinks[:, a, :], swa_sinks[a].partition_broadcast(P)))
            assert len(bcasts) == BCASTS
            for dst, src in bcasts:
                act.dma_start(dst, src).then_inc(bcast_full, 16)

            def round_unit(n):
                nc.scalar.activation(w_hi[:, n % RING, :], raw[:, n % RAWS, :], ACT.Copy).then_inc(hi_done, 1)

            def split_unit(n):
                if n >= RING:
                    wait_unit_used(act, n - RING)
                act.wait_ge(raw_full[n % RAWS], 16 * (n // RAWS + 1))
                round_unit(n)

            def sum_squares(phase, t):
                if phase == 0:
                    act.wait_ge(x_in_full, 16 * TT)
                else:
                    act.wait_ge(x_ready, x_count(phase, 2 * t + 1))
                nc.scalar.activation(rows[:, t, :], x[:, t, :], ACT.Square,
                                     accum_out=sumsq[:, t:t + 1]).then_inc(sq_ready, 1)

            def round_actT(name, l, gain_row, banks=range(4)):
                for b in banks:
                    key = (name, l, b)
                    wait_full(act, key)
                    if gain_row is None:
                        nc.scalar.activation(actT[:, 2 * b:2 * b + 2, 0, :], bank(key).rearrange("p (k t) -> p k t", k=2),
                                             ACT.Copy).then_inc(actT_hi, 1)
                    else:
                        for e in range(2):
                            k = 2 * b + e
                            last = nc.scalar.activation(actT[:, k, 0, :], bank(key, T, e * T), ACT.Copy,
                                                        scale=cols[:, gain_row + k:gain_row + k + 1])
                        last.then_inc(actT_hi, 1)

            def feature_tile(l, s):
                key = (l, *s)
                slot = bank_of(key) % 4
                wait_full(act, key)
                nc.scalar.activation(half[:, slot, :], bank(key, T, T), ACT.Copy).then_inc(half_ready, 1)
                act.wait_ge(wide_ready, plan.order["wide_ready", key])
                z = wide[:, slot, :]
                if KIND[l] == "hgrn":
                    nc.scalar.activation(half[:, slot, :], z, ACT.Sigmoid).then_inc(sig_ready, 1)
                elif s[1] == "q":
                    which = SWA_LAYERS.index(l) if KIND[l] == "swa" else 2
                    nc.scalar.activation(qT[:, s[2], :], z, ACT.Identity, bias=q_bias[:, which, s[2]:s[2] + 1],
                                         scale=Q_SCALE).then_inc(feat_ready, 1)
                elif KIND[l] == "fox":
                    nc.scalar.activation(kT[:, s[2], :], z, ACT.Identity,
                                         bias=foxcols[:, 8 + s[2]:9 + s[2]]).then_inc(feat_ready, 1)
                else:
                    c = ROW_SWA + SWA_ROWS * SWA_LAYERS.index(l) + 8 + s[2]
                    nc.scalar.activation(kT[:, s[2], :], z, ACT.Identity, bias=cols[:, c:c + 1])
                    nc.scalar.activation(kT[DH:P, 2 + s[2], :], wide[0:DH, slot, :], ACT.Identity, bias=cols[0:DH, c:c + 1])
                    nc.scalar.activation(kT[0:DH, 2 + s[2], :], wide[DH:P, slot, :], ACT.Identity,
                                         bias=cols[DH:P, c:c + 1]).then_inc(feat_ready, 1)

            def softmax(l, g):
                buf = g % 2
                act.wait_ge(max_ready, group_number(l, g) + 1)
                for b in range(3):
                    key = (l, "score", g, b)
                    for e in range(GROUP if b == 0 else 2):
                        h = e if b == 0 else 2 * (b - 1) + e
                        src = bank(key, P, e * P) if b == 0 else bank(key, T, e * T)
                        dst = probs[:, buf, h, 0:P] if b == 0 else probs[:, buf, h, P:3 * P]
                        c = h if b == 0 else GROUP + h
                        last = nc.scalar.activation(dst, src, ACT.Exp, bias=neg_max[:, buf, c:c + 1],
                                                    accum_out=denom[:, buf, c:c + 1])
                    last.then_inc(exp_ready, 1)
                if KIND[l] == "swa":
                    nc.scalar.activation(sink_exp[:, buf, :], sink_shift[:, buf, :], ACT.Exp).then_inc(sink_ready, 1)

            def turn(l, g):
                for b in (0, 2):
                    key = (l, "turn", g, b)
                    wait_full(act, key)
                    nc.scalar.activation(probsT[:, g % 2, b, :, :], bank(key).rearrange("p (h s) -> p h s", h=GROUP),
                                         ACT.Copy).then_inc(turned_a, 1)

            hg_n = 0
            for l, kind in enumerate(KIND):
                if l == 0:
                    act.wait_ge(cols_copied, 2)
                else:
                    sum_squares(2 * l, 0)
                round_actT("normT", 2 * l, ROW_MIX + KT * l)
                if l == 0:
                    split_unit(0)
                    sum_squares(0, 0)
                    sum_squares(0, 1)
                    split_unit(1)
                    act.wait_ge(lb_shifted, 1)
                    nc.scalar.activation(lb[:, 0:DEPTH, :], lb[:, 0:DEPTH, :], ACT.Exp).then_inc(lb_exp, 1)
                    act.wait_ge(bias_ready, 1)
                else:
                    sum_squares(2 * l, 1)
                for s in STEPS[kind]:
                    key = (l, *s)
                    if s[0] == "round":
                        split_unit(MIX0[l] + s[1])
                    elif s[0] == "feat":
                        feature_tile(l, s)
                    elif s[0] == "root":
                        act.wait_ge(rnorm_ready, TT * (2 * l + 1))
                    elif s[0] == "outT":
                        round_actT("outT", l, ROW_GN if kind == "hgrn" else None, (2 * s[1], 2 * s[1] + 1))
                    elif s[0] == "tok" and s[1] == "i":
                        wait_full(act, key)
                        nc.scalar.activation(v[:, s[3], s[2] * HALF:(s[2] + 1) * HALF], bank(key), ACT.Copy,
                                             scale=rnorm[:, s[3]:s[3] + 1]).then_inc(v_ready, 1)
                    elif s[0] == "tok" and s[1] == "g":
                        wait_full(act, key)
                        nc.scalar.activation(gate[:, s[3], s[2] * HALF:(s[2] + 1) * HALF], bank(key), ACT.Sigmoid,
                                             scale=rnorm[:, s[3]:s[3] + 1]).then_inc(sig_ready, 1)
                    elif s[0] == "gate":
                        act.wait_ge(bcast_full, 16 * BCASTS)
                        nc.scalar.activation(gate_whi[:], gate_w[:], ACT.Copy).then_inc(gate_hi_done, 1)
                        act.wait_ge(gateT_ready, 1)
                        z = fox_tmp[:, 1, :]
                        link(nc.scalar.activation(fox_tmp[:, 2, :], z, ACT.Abs))
                        link(nc.scalar.activation(fox_tmp[:, 2, :], fox_tmp[:, 2, :], ACT.Exp, scale=-1.0))
                        nc.scalar.activation(fox_tmp[:, 3, :], fox_tmp[:, 2, :], ACT.Ln, bias=1.0).then_inc(gate_log, 1)
                    elif s[0] == "score":
                        softmax(l, s[1])
                    elif s[0] == "turn":
                        turn(l, s[1])
                    elif s[0] == "mix":
                        wait_full(act, key)
                        if hg_n:
                            act.wait_ge(hg_sum, hg_n)
                        hg_n += 1
                        nc.scalar.activation(wide[:, 0:2, :], bank(key).rearrange("p (a b) -> p a b", a=2),
                                             ACT.Square).then_inc(hg_sq, 1)
                sum_squares(2 * l + 1, 0)
                round_actT("normT", 2 * l + 1, ROW_MLP + KT * l)
                sum_squares(2 * l + 1, 1)

                def mlp_pair(i, last):
                    def split_in_loop(j):
                        n = MLP0[l] + j
                        if j in (4, 5, 6, 7):
                            b, full = plan.full["up", l, 3]
                            act.wait_ge(bank_full[b], i * 2 + (full + (j - 4) // 2))
                        else:
                            before = j - 1 if j < 4 else j - 5
                            act.wait_ge(tail_used, i * 4 + (TAILS * l + before))
                        act.wait_ge(raw_full[n % RAWS], i * (8 // RAWS * 16) + 16 * (n // RAWS + 1))
                        round_unit(n)

                    split_in_loop(2)
                    split_in_loop(3)
                    for ab in range(2):
                        for f in range(4):
                            b, full = plan.full["up", l, f]
                            act.wait_ge(bank_full[b], i * 2 + (full + ab))
                            nc.scalar.activation(half[:, f, :], psum[:, b, T:2 * T], ACT.Copy).then_inc(half_ready, 1)
                            act.wait_ge(wide_ready, i * 8 + (plan.order["wide_ready", (l, "mlp")] + 4 * ab + f + 1))
                            nc.scalar.activation(hidden[:, ab, f, 0, :], wide[:, f, :], ACT.Copy).then_inc(hid_hi, 1)
                            if (ab, f) == (0, 3):
                                split_in_loop(4)
                            if (ab, f) == (1, 0):
                                split_in_loop(5)
                    for j in range(6, 8 if last else 10):
                        split_in_loop(j)

                with act.Fori(0, PAIRS - (l == DEPTH - 1)) as i:
                    mlp_pair(i, False)
                if l == DEPTH - 1:
                    mlp_pair(PAIRS - 1, True)
            act.dma_start(final_gain, norm_final.partition_broadcast(P)).then_inc(gain_full, 16)
            for t in range(TT):
                sum_squares(2 * DEPTH, t)

        @block.vector
        def _(dve):
            steps = [0]

            def link(ins):
                steps[0] += 1
                ins.then_inc(dve_step, 1)
                dve.wait_ge(dve_step, steps[0])

            def f32(ap):
                return ap.bitcast(F32)

            def rest_unit(n):
                nc.vector.tensor_tensor(w_lo[:, n % RING, :], raw[:, n % RAWS, :], f32(w_hi[:, n % RING, :]),
                                        ALU.subtract).then_inc(lo_done, 1)

            def split_unit(n):
                dve.wait_ge(hi_done, n + 1)
                rest_unit(n)

            def add_to_x(l, name, b):
                t, xs = b // 2, x[:, b // 2, (b % 2) * HALF:(b % 2 + 1) * HALF]
                if name == "mixed":
                    if b < 3:
                        wait_full(dve, (name, l, b))
                    else:
                        dve.wait_ge(tail_used, TAILS * l + 2)
                    nc.vector.tensor_tensor(xs, psum[:, b, :], xs, ALU.add).then_inc(x_ready, 1)
                    return
                if b == 0:
                    dve.wait_ge(rnorm_ready, TT * (2 * l + 2))
                    dve.wait_ge(down_tile0, PAIRS * (l + 1))
                if b == 2:
                    dve.wait_ge(tail_used, TAILS * (l + 1))
                nc.vector.scalar_tensor_tensor(xs, psum[:, b, :], rnorm[:, t:t + 1], xs, ALU.mult,
                                               ALU.add).then_inc(x_ready, 1)

            def rest_actT(name, l, turned, gain_row, banks=range(4)):
                for b in banks:
                    key = (name, 2 * l + turned // 2 if name == "normT" else l, b)
                    dve.wait_ge(actT_hi, turned_number(l, turned, b))
                    if gain_row is None:
                        nc.vector.tensor_tensor(actT[:, 2 * b:2 * b + 2, 1, :],
                                                bank(key).rearrange("p (k t) -> p k t", k=2),
                                                f32(actT[:, 2 * b:2 * b + 2, 0, :]), ALU.subtract).then_inc(actT_lo, 1)
                    else:
                        for e in range(2):
                            k = 2 * b + e
                            last = nc.vector.scalar_tensor_tensor(
                                actT[:, k, 1, :], bank(key, T, e * T), cols[:, gain_row + k:gain_row + k + 1],
                                f32(actT[:, k, 0, :]), ALU.mult, ALU.subtract)
                        last.then_inc(actT_lo, 1)

            for c, (dst, width) in enumerate(((cols, P), (foxcols, 16))):
                wait_full(dve, ("param", c))
                nc.vector.tensor_copy(dst[:], bank(("param", c), width)).then_inc(cols_copied, 1)
            dve.wait_ge(cols_copied, 2)
            for a in range(2):
                row = ROW_SWA + SWA_ROWS * a
                nc.vector.tensor_scalar(q_bias[:, a, :], cols[:, row:row + 8], Q_SCALE, None, ALU.mult)
            nc.vector.tensor_scalar(q_bias[:, 2, :], foxcols[:, 0:8], Q_SCALE, None, ALU.mult).then_inc(bias_ready, 1)
            logits = cols[:, ROW_LB:ROW_LB + 32].rearrange("p (l h) -> p l h", l=DEPTH)
            link(nc.vector.tensor_reduce(lb[:, DEPTH, :], logits.rearrange("p l h -> p h l"), AX.X, ALU.max))
            nc.vector.tensor_tensor(lb[:, 0:DEPTH, :], logits,
                                    lb[:, DEPTH:DEPTH + 1, :].to_broadcast([P, DEPTH, HG_HEADS]),
                                    ALU.subtract).then_inc(lb_shifted, 1)

            rest_actT("normT", 0, 0, ROW_MIX)
            split_unit(0)
            split_unit(1)
            dve.wait_ge(bcast_full, 16 * BCASTS)
            nc.vector.tensor_scalar(neg_sinks[:], sinks[:], -1.0, None, ALU.mult)

            def lower_bounds():
                dve.wait_ge(lb_exp, 1)
                link(nc.vector.tensor_reduce(lb[:, DEPTH, :], lb[:, 0:DEPTH, :].rearrange("p l h -> p h l"), AX.X, ALU.add))
                link(nc.vector.reciprocal(lb[:, DEPTH + 1, :], lb[:, DEPTH, :]))
                link(nc.vector.tensor_tensor(lb[:, 0:DEPTH, :], lb[:, 0:DEPTH, :],
                                             lb[:, DEPTH + 1:DEPTH + 2, :].to_broadcast([P, DEPTH, HG_HEADS]), ALU.mult))
                total = lb[:, 0, :]
                for i in range(1, HG_LAYER + 1):
                    link(nc.vector.tensor_tensor(lb[:, DEPTH + 2, :], total, lb[:, i, :], ALU.add))
                    total = lb[:, DEPTH + 2, :]
                link(nc.vector.tensor_tensor(lower[:, 0, :], total, lb[:, 0, :], ALU.subtract))
                link(nc.vector.tensor_scalar(lower[:, 1, :], lower[:, 0, :], -1.0, 1.0, ALU.mult, ALU.add))

            dve.sem_inc(up_sum, 4)

            def feature_tile(l, s):
                key = (l, *s)
                slot = bank_of(key) % 4
                dve.wait_ge(half_ready, plan.order["half_ready", key])
                z, other = wide[:, slot, :], half[:, slot, :]
                nc.vector.tensor_tensor(z, bank(key, T), other, ALU.add).then_inc(feat_sum, 1)
                dve.wait_ge(feat_sum, plan.free[key][1])
                nc.vector.tensor_tensor(z, z, spread[:], ALU.mult).then_inc(wide_ready, 1)
                if KIND[l] != "hgrn":
                    return
                h = s[2]
                dve.wait_ge(sig_ready, plan.order["sig_ready", key])
                if s[1] == "q":
                    nc.vector.tensor_tensor(qT[:, h, :], z, other, ALU.mult).then_inc(feat_ready, 1)
                else:
                    link(nc.vector.tensor_scalar(keep[:, h % GROUP, :], other, lower[:, 1, h:h + 1],
                                                 lower[:, 0, h:h + 1], ALU.mult, ALU.add))
                    nc.vector.tensor_scalar(kT[:, h, :], keep[:, h % GROUP, :], -1.0, 1.0,
                                            ALU.mult, ALU.add).then_inc(feat_ready, 1)

            def span_of(j):
                if j == 0:
                    return keep.rearrange("p h t -> p (h t)")
                start = GROUP * (T - T // 2 ** (j - 1))
                return span[:, start:start + GROUP * (T // 2 ** j)]

            def level(l, g, j):
                heads = slice(GROUP * g, GROUP * g + GROUP)
                for t in range(TT):
                    wait_full(dve, (l, "level", g, j, t))
                if j == 0:
                    nc.vector.tensor_tensor(qT[:, heads, :], qT[:, heads, :], keep, ALU.mult).then_inc(level_ready, 1)
                else:
                    size = 2 ** (j - 1)
                    qv = qT[:, heads, :].rearrange("p h (b e w) -> p (h b) e w", e=2, w=size)
                    kv = kT[:, heads, :].rearrange("p h (b e w) -> p (h b) e w", e=2, w=size)
                    blocks = GROUP * T // (2 * size)
                    sv = span_of(j - 1).rearrange("p (b e) -> p b e", e=2)
                    nc.vector.tensor_tensor(qv[:, :, 1, :], qv[:, :, 1, :],
                                            sv[:, :, 0:1].to_broadcast([P, blocks, size]), ALU.mult)
                    if j < LEVELS - 1:
                        link(nc.vector.tensor_tensor(span_of(j), sv[:, :, 0], sv[:, :, 1], ALU.mult))
                    nc.vector.tensor_tensor(kv[:, :, 0, :], kv[:, :, 0, :],
                                            sv[:, :, 1:2].to_broadcast([P, blocks, size]),
                                            ALU.mult).then_inc(level_ready, 1)
                for t in range(TT):
                    key = (l, "level", g, j, t)
                    if j > 0:
                        wait_free(dve, (l, "level", g, j - 1, t))
                    mask = level_mask[:, j:j + 1, :].bitcast(I16).to_broadcast([P, GROUP, P])
                    nc.vector.copy_predicated(mixT[:, heads, t * P:(t + 1) * P], mask,
                                              bank(key).rearrange("p (h t) -> p h t", h=GROUP)).then_inc(level_out, 1)

            def max_of_scores(l, g):
                buf = g % 2
                for b in range(3):
                    key = (l, "score", g, b)
                    wait_full(dve, key)
                    heads = GROUP if b == 0 else 2
                    c = 0 if b == 0 else GROUP + 2 * (b - 1)
                    last = nc.vector.tensor_reduce(neg_max[:, buf, c:c + heads],
                                                   bank(key).rearrange("p (h s) -> p h s", h=heads),
                                                   AX.X, ALU.max, negate=True)
                if KIND[l] != "swa":
                    last.then_inc(max_ready, 1)
                    return
                link(last)
                a, first = SWA_LAYERS.index(l), 2 * GROUP * (g // 2) + g % 2
                hs = slice(first, first + 2 * GROUP - 1, 2)
                nm = neg_max[:, buf, :].rearrange("p (b h) -> p b h", b=2)
                link(nc.vector.tensor_tensor(nm, nm, neg_sinks[:, a:a + 1, hs].to_broadcast([P, 2, GROUP]), ALU.min))
                nc.vector.tensor_tensor(sink_shift[:, buf, :].rearrange("p (b h) -> p b h", b=2), nm,
                                        sinks[:, a:a + 1, hs].to_broadcast([P, 2, GROUP]), ALU.add).then_inc(max_ready, 1)

            def turn(l, g):
                buf = g % 2
                dve.wait_ge(exp_ready, 3 * (group_number(l, g) + 1))
                if KIND[l] == "swa":
                    which = GROUPS * SWA_LAYERS.index(l) + g
                    dve.wait_ge(sink_ready, which + 1)
                    link(nc.vector.tensor_tensor(denom[:, buf, :], denom[:, buf, :], sink_exp[:, buf, :], ALU.add))
                nc.vector.reciprocal(inv_denom[:, buf, :], denom[:, buf, :])
                key = (l, "turn", g, 1)
                wait_full(dve, key)
                link(nc.vector.tensor_copy(probsT[:, buf, 1, :, :], bank(key).rearrange("p (h s) -> p h s", h=GROUP)))
                dve.sem_inc(turned_v, 1)

            def forget_gates(l):
                dve.wait_ge(gate_hi_done, 1)
                nc.vector.tensor_tensor(gate_wlo[:], gate_w[:], f32(gate_whi[:]), ALU.subtract).then_inc(gate_split, 1)
                link(nc.vector.memset(gate_rows, 0.0))
                key = (l, "gate")
                wait_full(dve, key)
                for t in range(TT):
                    last = nc.vector.scalar_tensor_tensor(gate_rows[:, t, 0:HEADS], bank(key, HEADS, t * HEADS),
                                                          rnorm[:, t:t + 1], gate_bias[:], ALU.mult, ALU.add)
                last.then_inc(gate_rows_ready, 1)
                key = (l, "gateT")
                wait_full(dve, key)
                z = fox_tmp[:, 1, :]
                nc.vector.tensor_copy(z, psum[0:HEADS, bank_of(key), 0:T]).then_inc(gateT_ready, 1)
                dve.wait_ge(gate_log, 1)
                link(nc.vector.tensor_scalar(z, z, 0.0, None, ALU.min))
                link(nc.vector.tensor_tensor(fox_tmp[:, 2, :], z, fox_tmp[:, 3, :], ALU.subtract))
                link(nc.vector.memset(fox_tmp[:, 3, :], 1.0))
                link(nc.vector.tensor_tensor_scan(z, fox_tmp[:, 3, :], fox_tmp[:, 2, :], 0.0, ALU.mult, ALU.add))
                link(nc.vector.tensor_scalar(z, z, -1.0, None, ALU.mult))
                link(nc.vector.tensor_copy(decay[:, 0, :], z))
                link(nc.vector.tensor_tensor(z, z, decay[:, 0, :], ALU.subtract))
                link(nc.vector.tensor_copy(decay[:, 1, :], z))
                link(nc.vector.tensor_tensor(z, z, decay[:, 1, :], ALU.subtract))
                nc.vector.tensor_copy(decay[:, 2, :], z).then_inc(decay_ready, 1)

            hg_n = 0
            for l, kind in enumerate(KIND):
                if l > 0:
                    rest_actT("normT", l, 0, ROW_MIX + KT * l)
                if kind == "hgrn":
                    link(nc.vector.memset(mixT, 0.0))
                    dve.wait_ge(consts, 3)
                for s in STEPS[kind]:
                    key = (l, *s)
                    if s[0] == "rest":
                        split_unit(MIX0[l] + s[1])
                    elif s[0] == "spread":
                        wait_full(dve, (l, "root"))
                        nc.vector.tensor_copy(spread[:], bank((l, "root"), T)).then_inc(spread_ready, 1)
                        dve.wait_ge(spread_ready, l + 1)
                    elif s[0] == "outT":
                        rest_actT("outT", l, 1, ROW_GN if kind == "hgrn" else None, (2 * s[1], 2 * s[1] + 1))
                    elif s[0] == "proj" and s[1] == 1:
                        add_to_x(l, "mixed", s[2])
                    elif s[0] == "feat":
                        feature_tile(l, s)
                    elif s[0] == "tok" and s[1] == "v":
                        wait_full(dve, key)
                        if kind == "swa":
                            dst, src, bias = v[:, s[3], 0:256], bank(key, 256), swa_v_bias[:, SWA_LAYERS.index(l), :]
                        else:
                            cs = slice(s[2] * HALF, (s[2] + 1) * HALF)
                            dst, src, bias = v[:, s[3], cs], bank(key), v_bias[:, cs]
                        nc.vector.scalar_tensor_tensor(dst, src, rnorm[:, s[3]:s[3] + 1], bias, ALU.mult,
                                                       ALU.add).then_inc(v_ready, 1)
                    elif s[0] == "tok" and s[1] == "g":
                        cs = slice(s[2] * HALF, (s[2] + 1) * HALF)
                        dve.wait_ge(sig_ready, plan.order["sig_ready", key])
                        nc.vector.scalar_tensor_tensor(gate[:, s[3], cs], bank(key), rnorm[:, s[3]:s[3] + 1],
                                                       gate[:, s[3], cs], ALU.mult, ALU.mult).then_inc(gate_ready, 1)
                    elif s[0] == "gate":
                        forget_gates(l)
                    elif s[0] == "score":
                        max_of_scores(l, s[1])
                    elif s[0] == "turn":
                        turn(l, s[1])
                    elif s[0] == "value":
                        g = s[1]
                        wait_full(dve, key)
                        for t in range(TT):
                            pairs = rows[:, t, (g // 2) * HALF:(g // 2 + 1) * HALF]
                            dst = pairs.rearrange("p (h e d) -> p h e d", h=GROUP, e=2)[:, :, g % 2, :]
                            src = bank(key, T, t * T).rearrange("p (h d) -> p h d", h=GROUP)
                            inv = inv_denom[:, g % 2, GROUP * t:GROUP * t + GROUP]
                            last = nc.vector.tensor_tensor(dst, src, inv.unsqueeze(2).to_broadcast([P, GROUP, DH]),
                                                           ALU.mult)
                        last.then_inc(o_ready, 1)
                    elif s[0] == "level":
                        level(l, s[1], s[2])
                    elif s[0] == "cross":
                        heads = slice(GROUP * s[1], GROUP * s[1] + GROUP)
                        wait_full(dve, key)
                        nc.vector.tensor_copy(crossT[:, heads, :],
                                              bank(key).rearrange("p (h t) -> p h t", h=GROUP)).then_inc(mixT_ready, 1)
                    elif s[0] == "mix":
                        g, t = s[1], s[2]
                        hg_n += 1
                        dve.wait_ge(hg_sq, hg_n)
                        nc.vector.tensor_reduce(hg_sumsq[:], wide[:, 0:2, :].rearrange("p a (h n) -> p (a h) n", n=P),
                                                AX.X, ALU.add).then_inc(hg_sum, 1)
                        dve.wait_ge(hg_rn, hg_n)
                        cs = slice(g * HALF, (g + 1) * HALF)
                        nc.vector.tensor_tensor(rows[:, t, cs].rearrange("p (h n) -> p h n", h=GROUP),
                                                bank(key).rearrange("p (h n) -> p h n", h=GROUP),
                                                hg_rnorm[:].unsqueeze(2).to_broadcast([P, GROUP, P]),
                                                ALU.mult).then_inc(hg_scaled, 1)
                        dve.wait_ge(hg_scaled, hg_n)
                        nc.vector.tensor_tensor(rows[:, t, cs], rows[:, t, cs], gate[:, t, cs],
                                                ALU.mult).then_inc(hg_rows, 1)
                if l == 0:
                    lower_bounds()
                rest_actT("normT", l, 2, ROW_MLP + KT * l)

                def mlp_pair(i, last):
                    def split_in_loop(j):
                        n = MLP0[l] + j
                        dve.wait_ge(hi_done, i * 8 + (n + 1))
                        rest_unit(n)

                    split_in_loop(2)
                    for ab in range(2):
                        for f in range(4):
                            b = bank_of(("up", l, f))
                            n = 4 * ab + f
                            dve.wait_ge(half_ready, i * 8 + (plan.order["half_ready", (l, "mlp")] + n + 1))
                            nc.vector.tensor_tensor(half[:, f, :], psum[:, b, 0:T], half[:, f, :],
                                                    ALU.add).then_inc(up_sum, 1)
                            dve.wait_ge(up_sum, i * 8 + (4 + UP_TILES * l + n + 1))
                            nc.vector.scalar_tensor_tensor(wide[:, f, :], half[:, f, :], 0.0, half[:, f, :],
                                                           ALU.max, ALU.mult).then_inc(wide_ready, 1)
                            dve.wait_ge(hid_hi, i * 8 + (UP_TILES * l + n + 1))
                            nc.vector.tensor_tensor(hidden[:, ab, f, 1, :], wide[:, f, :],
                                                    f32(hidden[:, ab, f, 0, :]), ALU.subtract).then_inc(hid_lo, 1)
                            if (ab, f) in ((0, 0), (1, 0), (1, 1)):
                                split_in_loop({(0, 0): 3, (1, 0): 4, (1, 1): 5}[ab, f])
                    for j in range(6, 8 if last else 10):
                        split_in_loop(j)

                with dve.Fori(0, PAIRS - (l == DEPTH - 1)) as i:
                    mlp_pair(i, False)
                if l == DEPTH - 1:
                    mlp_pair(PAIRS - 1, True)
                for b in range(4):
                    add_to_x(l, "down", b)
            dve.wait_ge(gain_full, 16)
            for t in range(TT):
                dve.wait_ge(rnorm_ready, TT * 2 * DEPTH + t + 1)
                nc.vector.scalar_tensor_tensor(rows[:, t, :], x[:, t, :], rnorm[:, t:t + 1], final_gain,
                                               ALU.mult, ALU.mult).then_inc(rows_ready, 1)

        @block.tensor
        def _(pe):
            def take_bank(key):
                if plan.before[key]:
                    wait_free(pe, plan.before[key])
                return bank_of(key)

            def weight(ring, n, k, width, start, size):
                return ring[:, n % RING, k * width + start:k * width + start + size]

            def norm_transposes(phase):
                for t in range(TT):
                    for b in range(4):
                        key = ("normT", phase, b)
                        if phase == 0:
                            pe.wait_ge(x_in_full, 16 * TT)
                        else:
                            pe.wait_ge(x_ready, x_count(phase, 2 * t + b // 2))
                        if t == 0:
                            take_bank(key)
                        for e in range(2):
                            k = 2 * b + e
                            last = nc.tensor.transpose(bank(key, P, e * T + t * P), x[:, t, k * P:(k + 1) * P], ident[:])
                        if t == TT - 1:
                            last.then_inc(bank_full[bank_of(key)], 1)
                    if phase % 2:
                        for b in (2 * t, 2 * t + 1):
                            take_bank(("down", phase // 2, b))
                            nc.tensor.matmul(psum[:, b, :].rearrange("p (a n) -> p a n", a=4), ident_h[:],
                                             masks[:, 3:4, :].to_broadcast([P, 4, P]), start=True, stop=True)

            def out_transposes(l, part):
                if KIND[l] != "hgrn":
                    wait_free(pe, (l, "value", 2 * part + 1))
                for t in range(TT):
                    if KIND[l] == "hgrn":
                        pe.wait_ge(hg_rows, 4 * GATES.index(l) + 2 * part + t + 1)
                    for b in (2 * part, 2 * part + 1):
                        key = ("outT", l, b)
                        if t == 0:
                            take_bank(key)
                        for e in range(2):
                            k = 2 * b + e
                            last = nc.tensor.transpose(bank(key, P, e * T + t * P), rows[:, t, k * P:(k + 1) * P],
                                                       ident[:])
                        if t == TT - 1:
                            last.then_inc(bank_full[bank_of(key)], 1)

            def wait_actT(l, turned, k):
                if k % 2 == 0:
                    pe.wait_ge(actT_lo, turned_number(l, turned, k // 2))

            def feature_major(b, cols_of, wait_act, wait_weights):
                for k in range(KT):
                    wait_act(k)
                    if k % 4 == 0:
                        wait_weights(k // 4)
                    hi, lo = cols_of(w_hi, k), cols_of(w_lo, k)
                    both = actT[:, k, :, :].rearrange("p a t -> p (a t)")
                    if k == 0:
                        nc.tensor.matmul(psum[:, b, :], hi, both, start=True, stop=False)
                    last = nc.tensor.matmul(psum[:, b, 0:T], lo, actT[:, k, 0, :], start=False, stop=False)
                    if k > 0:
                        last = nc.tensor.matmul(psum[:, b, :], hi, both, start=False, stop=k == KT - 1)
                return last

            def token_major(dst, lhs, rhs_hi, rhs_lo, start, stop, skip=False):
                nc.tensor.matmul(dst, lhs[0], rhs_hi, start=start, stop=False, skip_group_check=skip)
                nc.tensor.matmul(dst, lhs[0], rhs_lo, start=False, stop=False, skip_group_check=skip)
                return nc.tensor.matmul(dst, lhs[1], rhs_hi, start=False, stop=stop, skip_group_check=skip)

            def act_lhs(k, t):
                return [actT[:, k, a, t * P:(t + 1) * P] for a in range(2)]

            pe.wait_ge(consts, 1)
            pe.wait_ge(small_full, 16 * SMALLS)
            for c, src in enumerate((params, params2)):
                key = ("param", c)
                nc.tensor.transpose(bank(key, P), src, ident[:]).then_inc(bank_full[take_bank(key)], 1)
            pe.wait_ge(consts, 2)

            def score(l, g):
                kind = KIND[l]
                needed = [("feat", c, 4 * (g // 2) + 3) for c in ("q" if kind == "swa" else "qk")]
                for s in needed:
                    pe.wait_ge(feat_ready, plan.order["feat_ready", (l, *s)])
                if kind == "fox":
                    pe.wait_ge(decay_ready, 1)
                for b in range(3):
                    key = (l, "score", g, b)
                    take_bank(key)
                    for e in range(GROUP if b == 0 else 2):
                        j = e if b == 0 else 2 * (b - 1) + e
                        keys = P if b == 0 else T
                        dst = bank(key, keys, e * keys)
                        part, qt = slice(DH * (g % 2), DH * (g % 2) + DH), 4 * (g // 2) + j
                        kt = qt
                        if kind == "swa":
                            kv = (2 * qt + g % 2) // (HEADS // KV_HEADS)
                            kt = kv // 2 if kv % 2 == g % 2 else 2 + kv // 2
                        if kind == "fox":
                            for part3 in range(3):
                                nc.tensor.matmul(dst, pick[:, 2 * qt + g % 2, :], decay[:, part3, 0:keys],
                                                 start=e == 0 and part3 == 0, stop=False, skip_group_check=True)
                        t = 0 if b == 0 else 1
                        nc.tensor.matmul(dst, qT[part, qt, t * P:(t + 1) * P], kT[part, kt, 0:keys],
                                         start=e == 0 and kind == "swa", stop=False, skip_group_check=True)
                    mask = masks[:, 0:1, :] if b == 0 else masks[:, 1:3, :] if kind == "swa" else masks[:, 3:5, :]
                    mask = mask.rearrange("p a s -> p (a s)").unsqueeze(1)
                    heads, keys = (GROUP, P) if b == 0 else (2, T)
                    nc.tensor.matmul(bank(key).rearrange("p (h s) -> p h s", h=heads), ident_h[:],
                                     mask.to_broadcast([P, heads, keys]), start=False, stop=True,
                                     skip_group_check=True).then_inc(bank_full[b], 1)

            def turn(l, g):
                pe.wait_ge(exp_ready, 3 * (group_number(l, g) + 1))
                for b in range(3):
                    key = (l, "turn", g, b)
                    take_bank(key)
                    for h in range(GROUP):
                        last = nc.tensor.transpose(bank(key, P, h * P), probs[:, g % 2, h, b * P:(b + 1) * P], ident[:])
                    last.then_inc(bank_full[bank_of(key)], 1)

            def value(l, g):
                for b in range(3):
                    wait_free(pe, (l, "turn", g, b))
                wait_free(pe, (l, "tok", "v", 0 if KIND[l] == "swa" else g // 2, 1))
                key = (l, "value", g)
                take_bank(key)
                for h in range(GROUP):
                    c = 2 * (GROUP * (g // 2) + h) + g % 2
                    if KIND[l] == "swa":
                        c //= HEADS // KV_HEADS
                    vc = [v[:, t, c * DH:(c + 1) * DH] for t in range(TT)]
                    nc.tensor.matmul(bank(key, DH, h * DH), probsT[:, g % 2, 0, h, :], vc[0], start=True, stop=True)
                    dst = bank(key, DH, T + h * DH)
                    nc.tensor.matmul(dst, probsT[:, g % 2, 1, h, :], vc[0], start=True, stop=False)
                    last = nc.tensor.matmul(dst, probsT[:, g % 2, 2, h, :], vc[1], start=False, stop=True)
                last.then_inc(bank_full[bank_of(key)], 1)

            def level(l, g, j):
                if j == 0:
                    pe.wait_ge(feat_ready, plan.order["feat_ready", (l, "feat", "f", GROUP * g + GROUP - 1)])
                else:
                    pe.wait_ge(level_ready, plan.order["level_ready", (l, "level", g, j - 1)])
                for t in range(TT if j < LEVELS else 1):
                    key = (l, "level", g, j, t) if j < LEVELS else (l, "cross", g)
                    take_bank(key)
                    s_tile = slice(t * P, (t + 1) * P)
                    t_tile = s_tile if j < LEVELS else slice(P, T)
                    for h in range(GROUP):
                        last = nc.tensor.matmul(bank(key, P, h * P), kT[:, GROUP * g + h, s_tile],
                                                qT[:, GROUP * g + h, t_tile], start=True, stop=True)
                    last.then_inc(bank_full[bank_of(key)], 1)

            def mix(l, g, t):
                key = (l, "mix", g, t)
                take_bank(key)
                wait_free(pe, (l, "level", g, LEVELS - 1, TT - 1))
                wait_free(pe, (l, "cross", g))
                wait_free(pe, (l, "tok", "i", g, 1))
                for h in range(GROUP):
                    head = GROUP * g + h
                    dst = bank(key, P, h * P)
                    vc = [v[:, a, head * P:(head + 1) * P] for a in range(TT)]
                    if t == 1:
                        nc.tensor.matmul(dst, crossT[:, head, :], vc[0], start=True, stop=False)
                    last = nc.tensor.matmul(dst, mixT[:, head, t * P:(t + 1) * P], vc[t], start=t == 0, stop=True)
                last.then_inc(bank_full[bank_of(key)], 1)

            def project(l, part, b, frees):
                t, e = b // 2, b % 2
                if part == 0:
                    take_bank(("mixed", l, b))
                for k in range(4 * part, 4 * part + 4):
                    n = OUT0[l] + k // 2
                    if k % 2 == 0:
                        pe.wait_ge(lo_done, n + 1)
                    wait_actT(l, 1, k)
                    rhs = [weight(r, n, k % 2, D, e * HALF, HALF) for r in (w_hi, w_lo)]
                    last = token_major(psum[:, b, :], act_lhs(k, t), *rhs, k == 0, k == KT - 1)
                    if frees and k % 2 == 1:
                        last.then_inc(out_used, 1)
                    if part == 1 and b == 3 and k % 2 == 1:
                        last.then_inc(tail_used, 1)
                if part == 1 and b < 3:
                    last.then_inc(bank_full[b], 1)

            for l, kind in enumerate(KIND):
                norm_transposes(2 * l)
                parts = [s for s in STEPS[kind] if s[:2] == ("proj", 0)]
                for s in STEPS[kind]:
                    key = (l, *s)
                    if s[0] in ("feat", "tok"):
                        n = MIX0[l] + 2 * CHUNK_OF[kind](s)
                        b = take_bank(key)
                    if s[0] == "feat":
                        def cols_of(ring, k, n=n, j=s[2] % 4):
                            return weight(ring, n + k // 4, k % 4, HALF, j * P, P)

                        last = feature_major(b, cols_of, lambda k: wait_actT(l, 0, k),
                                             lambda u, n=n: pe.wait_ge(lo_done, n + u + 1))
                        last.then_inc(bank_full[b], 1)
                    elif s[0] == "tok":
                        start, width = (256, 256) if kind == "swa" else (0, HALF)
                        for k in range(KT):
                            if k % 4 == 0:
                                pe.wait_ge(lo_done, n + k // 4 + 1)
                            rhs = [weight(r, n + k // 4, k % 4, HALF, start, width) for r in (w_hi, w_lo)]
                            last = token_major(psum[:, b, 0:width], act_lhs(k, s[3]), *rhs, k == 0, k == KT - 1)
                        last.then_inc(bank_full[b], 1)
                    elif s[0] == "gate":
                        b = take_bank(key)
                        pe.wait_ge(gate_split, 1)
                        for t in range(TT):
                            for k in range(KT):
                                wait_actT(l, 0, k)
                                last = token_major(psum[:, b, t * HEADS:(t + 1) * HEADS], act_lhs(k, t),
                                                   gate_whi[:, k, :], gate_wlo[:, k, :], k == 0, k == KT - 1)
                        last.then_inc(bank_full[b], 1)
                        b = take_bank((l, "gateT"))
                        pe.wait_ge(gate_rows_ready, 1)
                        for t in range(TT):
                            last = nc.tensor.transpose(psum[:, b, t * P:(t + 1) * P], gate_rows[:, t, :], ident[:])
                        last.then_inc(bank_full[b], 1)
                    elif s[0] == "root":
                        b = take_bank(key)
                        pe.wait_ge(rnorm_ready, TT * (2 * l + 1))
                        for t in range(TT):
                            last = nc.tensor.matmul(psum[:, b, t * P:(t + 1) * P], rnorm[:, t:t + 1].to_broadcast([P, P]),
                                                    ident[:], start=True, stop=True)
                        last.then_inc(bank_full[b], 1)
                    elif s[0] == "outT":
                        out_transposes(l, s[1])
                    elif s[0] == "proj":
                        project(l, s[1], s[2], s == parts[-1])
                    elif s[0] == "score":
                        score(l, s[1])
                    elif s[0] == "turn":
                        turn(l, s[1])
                    elif s[0] == "value":
                        value(l, s[1])
                    elif s[0] == "level":
                        level(l, s[1], s[2])
                    elif s[0] == "cross":
                        level(l, s[1], LEVELS)
                    elif s[0] == "mix":
                        mix(l, s[1], s[2])
                norm_transposes(2 * l + 1)
                with pe.Fori(0, PAIRS) as i:
                    for ab in range(2):
                        n = MLP0[l] + 2 * ab
                        for f in range(4):
                            b = bank_of(("up", l, f))
                            pe.wait_ge(up_sum, i * 8 + (UP_TILES * l + 4 * ab + f + 1))
                            last = feature_major(b, lambda ring, k: weight(ring, n + k // 4, k % 4, HALF, f * P, P),
                                                 lambda k: wait_actT(l, 2, k),
                                                 lambda u: pe.wait_ge(lo_done, i * 8 + (n + u + 1)))
                            last.then_inc(bank_full[b], 1)
                    for ab in range(2):
                        for t in range(TT):
                            for u in range(2):
                                n = MLP0[l] + 4 + 2 * ab + u
                                pe.wait_ge(lo_done, i * 8 + (n + 1))
                                for kk in range(2):
                                    k = 2 * u + kk
                                    if t == 0:
                                        pe.wait_ge(hid_lo, i * 8 + (UP_TILES * l + 4 * ab + k + 1))
                                    lhs = [hidden[:, ab, k, a, t * P:(t + 1) * P] for a in range(2)]
                                    for e in range(2):
                                        rhs = [weight(r, n, kk, D, e * HALF, HALF) for r in (w_hi, w_lo)]
                                        last = token_major(psum[:, 2 * t + e, :], lhs, *rhs, False, True, skip=True)
                                if t == 1:
                                    last.then_inc(tail_used, 1)
                                elif ab == 1 and u == 1:
                                    last.then_inc(down_tile0, 1)


_INS = ["x", "norm_mix", "norm_mlp", "norm_final", "w_up", "w_down", "swa_w_qkv", "swa_b_qkv", "swa_sinks", "swa_w_o",
        "hgrn_w_in", "hgrn_lb_logits", "hgrn_g_norm", "hgrn_w_o", "fox_w_in", "fox_b_in", "fox_w_o"]


def kernel(**inputs):
    import numpy as np
    import concourse.bacc as bacc
    from concourse.bass_utils import run_bass_kernel_spmd

    nc = bacc.Bacc("TRN2", target_bir_lowering=False, num_devices=1)
    arrays, args = {}, []
    for name in _INS:
        a = np.ascontiguousarray(inputs[name])
        arrays[f"in_{name}"] = a
        args.append(nc.dram_tensor(f"in_{name}", a.shape, mybir.dt.from_np(a.dtype), kind="ExternalInput").ap())
    args.append(nc.dram_tensor("out", (1, T, D), F32, kind="ExternalOutput").ap())
    build_trunk(nc, *args)
    result = run_bass_kernel_spmd(nc, [arrays], core_ids=[0])
    return result.results[0]["out"]
```

```python
import concourse.bass as bass
from concourse import mybir
from contextlib import ExitStack

F32 = mybir.dt.float32
F32R = mybir.dt.float32r
BF16 = mybir.dt.bfloat16
I16 = mybir.dt.int16
ALU = mybir.AluOpType
ACT = mybir.ActivationFunctionType
AX = mybir.AxisListType

P = 128
D = 1024
T = 256
DEPTH = 4
TT = T // P
KT = D // P
FF = 4 * D
EPS = 1e-6
HALF = 512
UNIT = 2048
RING = 4
RAWS = 2
PAIRS = FF // (2 * HALF)
MASKED = -1.0e30
WARM_UP = 30

HEADS = 16
KV_HEADS = 4
DH = 64
GROUP = 4
GROUPS = HEADS // GROUP
Q_SCALE = DH ** -0.5
HG_HEADS = 8
LEVELS = 8

MIXERS = ["swa", "hgrn", "fox"]
KIND = [MIXERS[i % 3] for i in range(DEPTH)]
MIX_UNITS = {"swa": 6, "hgrn": 16, "fox": 12}
OUT_UNITS = 4
MLP_UNITS = 8 * PAIRS


def unit_bases():
    at, mix, out, mlp = 0, [], [], []
    for kind in KIND:
        mix.append(at)
        out.append(at + MIX_UNITS[kind])
        mlp.append(at + MIX_UNITS[kind] + OUT_UNITS)
        at = mlp[-1] + MLP_UNITS
    return mix, out, mlp, at


MIX0, OUT0, MLP0, ALL_UNITS = unit_bases()

CHUNKS = {"swa": [2, 0, 1], "hgrn": [0, 2, 1, 3, 4, 5, 6, 7], "fox": [2, 0, 4, 3, 1, 5]}



def split(*units):
    return [s for n in units for s in (("round", n), ("rest", n))]


def after(n, first, second, third=None):
    return [("round", n), *first, ("rest", n), ("round", n + 1), *second, ("rest", n + 1), *(third or [])]


def projection(n):
    return [("proj", 1, 0), ("round", n), ("rest", n), ("round", n + 1), ("proj", 1, 1), ("rest", n + 1),
            ("proj", 1, 2), ("proj", 1, 3)]


STEPS = {
    "swa": (split(2) + [("round", 3), ("spread",), ("feat", "k", 0), ("feat", "k", 1), ("root",), ("rest", 3)]
            + [("tok", "v", 0, 0), ("tok", "v", 0, 1)]
            + after(4, [("feat", "q", 0)], [("feat", "q", 1)], [("feat", "q", 2), ("feat", "q", 3)])
            + [("feat", "q", 4), ("score", 0), ("max", 0), ("exp", 0), ("feat", "q", 5), ("scale", 0), ("feat", "q", 6)]
            + [("score", 1), ("max", 1), ("turn", 0), ("exp", 1), ("feat", "q", 7), ("scale", 1), ("value", 0)]
            + split(6) + [("round", 7), ("score", 2), ("turn", 1), ("max", 2), ("exp", 2), ("rest", 7), ("value", 1)]
            + [("scale", 2), ("outT", 0), ("score", 3), ("max", 3), ("turn", 2), ("exp", 3), ("proj", 0, 3), ("value", 2)]
            + [("scale", 3)] + after(8, [("proj", 0, 0), ("turn", 3)], [("proj", 0, 1), ("value", 3)], [("outT", 1)])
            + [("proj", 0, 2)] + projection(10)),
    "fox": (split(2) + [("round", 3), ("spread",), ("feat", "k", 0), ("feat", "k", 1), ("root",), ("rest", 3)]
            + [("gate",), ("feat", "k", 2), ("feat", "k", 3)]
            + after(4, [("feat", "q", 0)], [("feat", "q", 1)], [("feat", "q", 2), ("feat", "q", 3)])
            + split(6) + [("round", 7), ("tok", "v", 0, 0), ("rest", 7), ("score", 0), ("max", 0), ("exp", 0), ("tok", "v", 0, 1)]
            + [("scale", 0), ("round", 8), ("feat", "k", 4), ("rest", 8), ("round", 9), ("feat", "k", 5), ("turn", 0)]
            + [("rest", 9), ("score", 1), ("max", 1), ("exp", 1), ("value", 0), ("feat", "k", 6), ("feat", "k", 7), ("scale", 1)]
            + after(10, [("feat", "q", 4)], [("feat", "q", 5)], [("feat", "q", 6), ("feat", "q", 7)])
            + [("round", 12), ("tok", "v", 1, 0), ("rest", 12), ("score", 2), ("turn", 1), ("max", 2), ("exp", 2)]
            + [("round", 13), ("value", 1), ("rest", 13), ("score", 3), ("max", 3), ("scale", 2), ("exp", 3), ("tok", "v", 1, 1)]
            + [("turn", 2), ("scale", 3), ("outT", 0), ("value", 2)]
            + after(14, [("proj", 0, 0), ("turn", 3)], [("proj", 0, 1), ("value", 3)], [("proj", 0, 2), ("outT", 1)])
            + [("proj", 0, 3)] + projection(16)),
    "hgrn": (split(2) + [("round", 3), ("spread",), ("feat", "q", 0), ("feat", "q", 1), ("root",), ("rest", 3)]
             + [("feat", "q", 2), ("feat", "q", 3)]
             + after(4, [("feat", "f", 0)], [("feat", "f", 1)], [("feat", "f", 2), ("feat", "f", 3)])
             + [("feat", "q", 4), ("round", 6), ("feat", "q", 5), ("level", 0, 0), ("rest", 6), ("round", 7), ("feat", "q", 6)]
             + [("rest", 7), ("level", 0, 1), ("feat", "q", 7)]
             + after(8, [("feat", "f", 4), ("level", 0, 2)], [("feat", "f", 5)])
             + [("feat", "f", 6), ("level", 0, 3), ("feat", "f", 7)]
             + split(10, 11) + [("tok", "i", 0, 0), ("level", 0, 4), ("level", 1, 0), ("tok", "i", 0, 1), ("level", 0, 5), ("level", 1, 1)]
             + split(12, 13) + [("tok", "i", 1, 0), ("level", 0, 6), ("level", 1, 2), ("tok", "i", 1, 1), ("level", 0, 7), ("level", 1, 3)]
             + split(14, 15) + [("tok", "g", 0, 0), ("level", 1, 4), ("cross", 0), ("tok", "g", 0, 1), ("level", 1, 5), ("mix", 0, 0)]
             + [("mix", 0, 1), ("tok", "g", 1, 0), ("level", 1, 6)] + split(16, 17)
             + [("tok", "g", 1, 1), ("level", 1, 7), ("cross", 1), ("outT", 0), ("mix", 1, 0), ("mix", 1, 1)]
             + split(18) + [("proj", 0, 0)] + split(19) + [("proj", 0, 1), ("proj", 0, 2)]
             + [("outT", 1), ("proj", 0, 3)] + projection(20)),
}
TILE_BANKS = {("swa", "feat", "q", 6): 3, ("swa", "feat", "q", 7): 7, ("fox", "feat", "k", 4): 3, ("fox", "feat", "k", 5): 7,
              ("fox", "feat", "k", 6): 7, ("fox", "tok", "v", 1, 1): 3}
CHUNK_OF = {
    "swa": lambda s: 0 if s[1] in "kv" else 1 + s[2] // 4,
    "fox": lambda s: {"k": (0, 3), "q": (1, 4)}[s[1]][s[2] // 4] if s[0] == "feat" else (2, 5)[s[2]],
    "hgrn": lambda s: {"q": (0, 2), "f": (1, 3)}[s[1]][s[2] // 4] if s[0] == "feat" else {"i": 4, "g": 6}[s[1]] + s[2],
}


class Plan:

    def __init__(self):
        self.full, self.free, self.before = {}, {}, {}
        self.order = {}
        self.fills, self.last, self.counts, self.turn = [0] * 8, [None] * 8, {}, 0
        self.walk()

    def take(self, key, bank, signal, times=1, count=1):
        self.before[key] = self.last[bank]
        self.last[bank] = key
        self.fills[bank] += 1
        self.full[key] = (bank, self.fills[bank])
        self.fills[bank] += times - 1
        self.counts[signal] = self.counts.get(signal, 0) + count
        self.free[key] = (signal, self.counts[signal])

    def note(self, key, signal, count=1):
        self.counts[signal] = self.counts.get(signal, 0) + count
        self.order[signal, key] = self.counts[signal]

    def slot_before(self, key):
        mine = (self.full[key][0], self.order["feat_ready", key])
        before = [n for (signal, other), n in self.order.items()
                  if signal == "feat_ready" and other[0] == key[0] and self.full[other][0] == mine[0] and n < mine[1]]
        return max(before, default=0)

    def work(self, key, signal):
        bank = TILE_BANKS.get((KIND[key[0]], *key[1:]))
        if bank is not None:
            self.take(key, bank, signal)
            return
        self.take(key, 4 + self.turn % 4, signal)
        self.turn += 1

    def walk(self):
        for c in range(2):
            self.take(("param", c), c, "cols_copied")
        for l, kind in enumerate(KIND):
            for b in range(4):
                self.take(("normT", 2 * l, b), 4 + b, "actT_lo")
            self.turn = 0
            for s in STEPS[kind]:
                if s[0] == "feat":
                    self.work((l, *s), "feat_sum")
                    for signal in ("half_ready", "wide_ready", "feat_ready"):
                        self.note((l, *s), signal)
                    if kind == "hgrn":
                        self.note((l, *s), "sig_ready")
                if s[0] == "root":
                    self.work((l, *s), "spread_ready")
                if s[0] == "tok":
                    self.work((l, *s), "gate_ready" if s[1] == "g" else "v_ready")
                    if s[1] == "g":
                        self.note((l, *s), "sig_ready")
                if s[0] == "gate":
                    self.work((l, *s), "gate_rows_ready")
                    self.work((l, "gateT"), "gateT_ready")
                if s[0] == "score":
                    for b in range(3):
                        self.take((l, *s, b), b, "exp_ready")
                if s[0] == "turn":
                    for b in range(3):
                        self.take((l, *s, b), 4 + b, "turned")
                if s[0] == "value":
                    self.take((l, *s, 0), 4, "o_ready_a")
                    self.take((l, *s, 1), 5, "o_ready_v")
                if s[0] == "level":
                    for t in range(TT):
                        self.take((l, *s, t), 2 * ((s[1] + s[2]) % 2) + t, "level_out")
                    self.note((l, *s), "level_q")
                    if s[2] > 0:
                        self.note((l, *s), "level_k")
                if s[0] == "cross":
                    self.take((l, *s), 0, "mixT_ready")
                if s[0] == "mix":
                    self.take((l, *s), 2 + s[2], "hg_scaled")
                if s[0] == "outT":
                    for b in (2 * s[1], 2 * s[1] + 1):
                        if kind == "hgrn":
                            self.take(("outT", l, b), 4 + b, "actT_lo")
                        else:
                            self.note(("outT", l, b), "actT_lo")
                if s[0] == "proj" and s[1] == 0:
                    self.take(("mixed", l, s[2]), s[2], "x_ready", times=s[2] < 3, count=0)
            for b in range(4):
                self.note(("mixed", l, b), "x_ready")
                self.free[("mixed", l, b)] = ("x_ready", self.counts["x_ready"])
            for b in range(4):
                self.take(("normT", 2 * l + 1, b), 4 + b, "actT_lo")
            for b in range(4):
                self.take(("up", l, b), 4 + b, "up_sum", 2 * PAIRS)
            self.counts["up_sum"] += 8 * PAIRS - 4
            for signal in ("half_ready", "wide_ready"):
                self.note((l, "mlp"), signal, 0)
                self.counts[signal] += 8 * PAIRS
            for b in range(4):
                self.free[("up", l, b)] = ("up_sum", self.counts["up_sum"] + 4)
            for b in range(4):
                self.take(("down", l, b), b, "x_ready", 0)


ROW_MIX, ROW_MLP, ROW_LB, ROW_GN, ROW_SWA = 0, 32, 64, 96, 104
SWA_ROWS = 10
HG_LAYER = 1
SWA_LAYERS = [l for l in range(DEPTH) if KIND[l] == "swa"]
SMALLS, BCASTS = 7, 7


def build_trunk(nc, x_in, norm_mix, norm_mlp, norm_final, w_up, w_down, swa_w_qkv, swa_b_qkv, swa_sinks, swa_w_o,
                hgrn_w_in, hgrn_lb_logits, hgrn_g_norm, hgrn_w_o, fox_w_in, fox_b_in, fox_w_o, out):
    plan = Plan()
    ctx = ExitStack()
    with ctx:
        def sb(name, shape, dt=F32):
            return ctx.enter_context(nc.sbuf_tensor(name, shape, dt))

        def sem(name):
            return ctx.enter_context(nc.semaphore(name))

        raw = sb("raw", [P, RAWS, UNIT])
        w_hi = sb("w_hi", [P, RING, UNIT], F32R)
        w_lo = sb("w_lo", [P, RING, UNIT], F32R)
        x = sb("x", [P, TT, D])
        rows = sb("rows", [P, TT, D])
        actT = sb("actT", [P, KT, 2, T], F32R)
        hidden = sb("hidden", [P, 2, 4, 2, T], F32R)
        half = sb("half", [P, 4, T])
        wide = sb("wide", [P, 4, T])
        qT = sb("qT", [P, 8, T])
        kT = sb("kT", [P, 8, T])
        v = sb("v", [P, TT, D])
        scratch = sb("scratch", [P, 6144])
        o = rows.rearrange("p t n -> p (t n)").rearrange("p (k t) -> p k t", k=KT)
        probs = scratch[:, 0:3072].rearrange("p (g h s) -> p g h s", g=2, h=GROUP)
        probsT = scratch[:, 3072:6144].rearrange("p (g b h s) -> p g b h s", g=2, b=3, h=GROUP)
        mixT = scratch[:, 0:2048].rearrange("p (h t) -> p h t", h=HG_HEADS)
        crossT = scratch[:, 2048:3072].rearrange("p (h t) -> p h t", h=HG_HEADS)
        gate = scratch[:, 3072:5120].rearrange("p (t n) -> p t n", t=TT)
        keep = scratch[:, 5120:6144].rearrange("p (h t) -> p h t", h=GROUP)
        span = sb("span", [P, GROUP * 254])
        level_mask = sb("level_mask", [P, LEVELS, P], BF16)
        ident = sb("ident", [P, P])
        ident_h = sb("ident_h", [P, P], BF16)
        masks = sb("masks", [P, 5, P], BF16)
        decay = sb("decay", [96, T], BF16)
        pick = sb("pick", [96, HEADS, P], BF16)
        cols = sb("cols", [P, P])
        foxcols = sb("foxcols", [P, 16])
        q_bias = sb("q_bias", [P, 3, 8])
        v_bias = sb("v_bias", [P, D])
        swa_v_bias = sb("swa_v_bias", [P, 2, 256])
        sinks = sb("sinks", [P, 2, HEADS])
        neg_sinks = sb("neg_sinks", [P, 2, HEADS])
        gate_bias = sb("gate_bias", [P, HEADS])
        gate_w = sb("gate_w", [P, KT, HEADS])
        gate_whi = sb("gate_whi", [P, KT, HEADS], F32R)
        gate_wlo = sb("gate_wlo", [P, KT, HEADS], F32R)
        sumsq = sb("sumsq", [P, TT])
        mean = sb("mean", [P, GROUP])
        rnorm = sb("rnorm", [P, TT])
        spread = sb("spread", [P, T])
        hg_sumsq = sb("hg_sumsq", [P, GROUP])
        hg_rnorm = sb("hg_rnorm", [P, GROUP])
        minus_half = sb("minus_half", [P, GROUP])
        minus_one = sb("minus_one", [P, 1])
        neg_max = sb("neg_max", [P, 2, 2 * GROUP])
        sink_shift = sb("sink_shift", [P, 2, 2 * GROUP])
        sink_exp = sb("sink_exp", [P, 2, 2 * GROUP])
        denom = sb("denom", [P, 2, 2 * GROUP])
        inv_denom = sb("inv_denom", [P, 2, 2 * GROUP])
        lb = sb("lb", [P, DEPTH + 3, HG_HEADS])
        lower = sb("lower", [P, 2, HG_HEADS])

        params = qT[:, 0, 0:P]
        params2 = qT[:, 0, P:2 * P]
        gate_rows = scratch[:, 0:2 * P].rearrange("p (t h) -> p t h", t=TT)
        part_tmp = scratch[0:HEADS, 2 * P + 4 * T:2 * P + 5 * T].bitcast(BF16)[:, 0:T]
        fox_tmp = scratch[0:HEADS, 2 * P:2 * P + 4 * T].rearrange("p (a t) -> p a t", a=4)
        final_gain = v[:, 0, :]

        psum = ctx.enter_context(nc.psum_tensor("psum", [P, 8, HALF], F32))

        raw_full = [sem(f"raw_full{i}") for i in range(RAWS)]
        hi_done = sem("hi_done")
        lo_done = sem("lo_done")
        out_used = sem("out_used")
        tail_used = sem("tail_used")
        down_tile0 = sem("down_tile0")
        bank_full = [sem(f"bank_full{b}") for b in range(8)]
        x_in_full = sem("x_in_full")
        small_full = sem("small_full")
        small_issued = sem("small_issued")
        bcast_full = sem("bcast_full")
        gain_full = sem("gain_full")
        zeroed = sem("zeroed")
        consts = sem("consts")
        pool_step = sem("pool_step")
        cols_copied = sem("cols_copied")
        bias_ready = sem("bias_ready")
        lb_shifted = sem("lb_shifted")
        lb_exp = sem("lb_exp")
        lower_ready = sem("lower_ready")
        x_ready = sem("x_ready")
        sq_ready = sem("sq_ready")
        rnorm_ready = sem("rnorm_ready")
        spread_ready = sem("spread_ready")
        rows_ready = sem("rows_ready")
        actT_hi = sem("actT_hi")
        actT_lo = sem("actT_lo")
        half_ready = sem("half_ready")
        wide_ready = sem("wide_ready")
        sig_ready = sem("sig_ready")
        up_sum = sem("up_sum")
        hid_hi = sem("hid_hi")
        hid_lo = sem("hid_lo")
        feat_sum = sem("feat_sum")
        feat_ready = sem("feat_ready")
        v_ready = sem("v_ready")
        gate_ready = sem("gate_ready")
        max_ready = sem("max_ready")
        exp_ready = sem("exp_ready")
        sink_ready = sem("sink_ready")
        turned = sem("turned")
        probs_ready = sem("probs_ready")
        o_ready_a = sem("o_ready_a")
        o_ready_v = sem("o_ready_v")
        level_q = sem("level_q")
        level_k = sem("level_k")
        mixT_zeroed = sem("mixT_zeroed")
        level_out = sem("level_out")
        mixT_ready = sem("mixT_ready")
        hg_sq = sem("hg_sq")
        hg_sum = sem("hg_sum")
        hg_rn = sem("hg_rn")
        hg_scaled = sem("hg_scaled")
        hg_rows = sem("hg_rows")
        gate_split = sem("gate_split")
        gate_hi_done = sem("gate_hi_done")
        gate_rows_ready = sem("gate_rows_ready")
        gateT_ready = sem("gateT_ready")
        gate_log = sem("gate_log")
        decay_ready = sem("decay_ready")
        dve_step = sem("dve_step")
        act_step = sem("act_step")
        out_done = sem("out_done")
        signals = {"cols_copied": cols_copied, "actT_lo": actT_lo, "feat_sum": feat_sum,
                   "spread_ready": spread_ready, "v_ready": v_ready,
                   "gate_ready": gate_ready, "gate_rows_ready": gate_rows_ready, "gateT_ready": gateT_ready,
                   "exp_ready": exp_ready, "turned": turned, "o_ready_a": o_ready_a,
                   "o_ready_v": o_ready_v,
                   "level_out": level_out, "mixT_ready": mixT_ready, "hg_scaled": hg_scaled, "x_ready": x_ready,
                   "up_sum": up_sum}

        block = ctx.enter_context(nc.Block())

        def bank(key, width=HALF, start=0):
            return psum[:, plan.full[key][0], start:start + width]

        def bank_of(key):
            return plan.full[key][0]

        def wait_full(engine, key):
            b, n = plan.full[key]
            engine.wait_ge(bank_full[b], n)

        def wait_free(engine, key):
            signal, n = plan.free[key]
            engine.wait_ge(signals[signal], n)

        def group_number(l, g):
            return GROUPS * sum(KIND[m] != "hgrn" for m in range(l)) + g

        def o_of(g, i):
            k = GROUP * (g // 2) + 2 * i
            return o[DH * (g % 2):DH * (g % 2) + DH, k:k + 2, :]

        def o_sums(l, g, i):
            return bank((l, "value", g, i))[DH * (g % 2):DH * (g % 2) + DH, :].rearrange("p (k t) -> p k t", k=2)

        def turned_number(l, turned, b):
            return 4 * (3 * l + turned) + b + 1

        def x_count(phase, b):
            return 4 * (phase - 1) + b + 1

        def span_of(j):
            if j == 0:
                return keep.rearrange("p h t -> p (h t)")
            start = GROUP * (T - T // 2 ** (j - 1))
            return span[:, start:start + GROUP * (T // 2 ** j)]

        UP_TILES = 8 * PAIRS
        TAILS = 2 + 4 * PAIRS
        GATES = [l for l in range(DEPTH) if KIND[l] == "hgrn"]

        def wait_unit_used(engine, n):
            l = max(m for m in range(DEPTH) if MIX0[m] <= n)
            if n < OUT0[l]:
                place = (n - MIX0[l]) // 2
                tiles = [s for s in STEPS[KIND[l]] if s[0] in ("feat", "tok") and CHUNK_OF[KIND[l]](s) == place]
                wait_full(engine, (l, *tiles[-1]))
            elif n < OUT0[l] + 2:
                engine.wait_ge(out_used, 2 * l + n - OUT0[l] + 1)
            elif n < MLP0[l]:
                engine.wait_ge(tail_used, TAILS * l + n - OUT0[l] - 1)
            else:
                assert MLP0[l] + MLP_UNITS - n in (1, 2)
                engine.wait_ge(tail_used, TAILS * (l + 1) - (MLP0[l] + MLP_UNITS - n - 1))

        @block.sync
        def _(sp):
            def load(n, src, columns):
                slot = n % RAWS
                if n >= RAWS:
                    sp.wait_ge(lo_done, n - RAWS + 1)
                dst = raw[:, slot, :].rearrange("p (k n) -> p k n", n=columns)
                sp.dma_start(dst, src).then_inc(raw_full[slot], 16)

            for t in range(TT):
                sp.dma_start(x[:, t, :], x_in[0, t * P:(t + 1) * P, :]).then_inc(x_in_full, 16)
            bcasts = [(v_bias[:], fox_b_in[0, 2 * D:3 * D].partition_broadcast(P)),
                      (gate_bias[:], fox_b_in[0, 3 * D:3 * D + HEADS].partition_broadcast(P)),
                      (gate_w[:], fox_w_in[0, :, 3 * D:3 * D + HEADS].rearrange("(k p) n -> p k n", p=P))]
            for a in range(2):
                bcasts.append((swa_v_bias[:, a, :], swa_b_qkv[a, D + 256:D + 512].partition_broadcast(P)))
                bcasts.append((sinks[:, a, :], swa_sinks[a].partition_broadcast(P)))
            assert len(bcasts) == BCASTS
            sp.wait_ge(small_issued, 1)
            for l, kind in enumerate(KIND):
                w_in = {"swa": swa_w_qkv, "hgrn": hgrn_w_in, "fox": fox_w_in}[kind][l // 3]
                w_o = {"swa": swa_w_o, "hgrn": hgrn_w_o, "fox": fox_w_o}[kind][l // 3]
                w_in = w_in.rearrange("(k p) n -> p k n", p=P)
                w_o = w_o.rearrange("(k p) n -> p k n", p=P)
                for c, chunk in enumerate(CHUNKS[kind]):
                    for u in range(2):
                        load(MIX0[l] + 2 * c + u, w_in[:, 4 * u:4 * u + 4, chunk * HALF:(chunk + 1) * HALF], HALF)
                    if l == 0 and c == 0:
                        for dst, src in bcasts:
                            sp.dma_start(dst, src).then_inc(bcast_full, 16)
                for u in range(OUT_UNITS):
                    load(OUT0[l] + u, w_o[:, 2 * u:2 * u + 2, :], D)
                up = w_up[l].rearrange("(k p) n -> p k n", p=P)
                down = w_down[l].rearrange("(k p) n -> p k n", p=P)
                with sp.Fori(0, PAIRS) as i:
                    for j in range(8):
                        ab, u = (j // 2) % 2, j % 2
                        if j < 4:
                            src = up[:, 4 * u:4 * u + 4, bass.ds((i * 2 + ab) * HALF, HALF)]
                        else:
                            src = down[:, bass.ds((i * 2 + ab) * 4 + 2 * u, 2), :]
                        slot = (MLP0[l] + j) % RAWS
                        sp.wait_ge(lo_done, i * 8 + (MLP0[l] + j - RAWS + 1))
                        dst = raw[:, slot, :].rearrange("p (k n) -> p k n", n=HALF if j < 4 else D)
                        sp.dma_start(dst, src).then_inc(raw_full[slot], 16)
            for t in range(TT):
                sp.wait_ge(rows_ready, t + 1)
                sp.dma_start(out[0, t * P:(t + 1) * P, :], rows[:, t, :]).then_inc(out_done, 16)
            sp.wait_ge(out_done, 16 * TT)

        @block.gpsimd
        def _(pool):
            steps = [0]

            def link(ins):
                steps[0] += 1
                ins.then_inc(pool_step, 1)
                pool.wait_ge(pool_step, steps[0])

            nc.gpsimd.memset(qT[:, 0, :], 0.0).then_inc(zeroed, 1)
            link(nc.gpsimd.memset(minus_half[:], -0.5))
            link(nc.gpsimd.memset(minus_one[:], -1.0))
            link(nc.gpsimd.memset(ident[:], 0.0))
            nc.gpsimd.affine_select(out=ident[:], in_=ident[:], compare_op=ALU.not_equal, fill=1.0, base=0,
                                    pattern=[[-1, P]], channel_multiplier=1).then_inc(consts, 1)
            pool.wait_ge(consts, 1)
            link(nc.gpsimd.tensor_copy(ident_h[:], ident[:]))
            link(nc.gpsimd.memset(masks[:], 0.0))
            for m in (0, 2, 4):
                link(nc.gpsimd.affine_select(out=masks[:, m, :], in_=masks[:, m, :], compare_op=ALU.is_ge, fill=MASKED,
                                             base=0, pattern=[[-1, P]], channel_multiplier=1))
            nc.gpsimd.affine_select(out=masks[:, 1, :], in_=masks[:, 1, :], compare_op=ALU.is_gt, fill=MASKED, base=0,
                                    pattern=[[1, P]], channel_multiplier=-1).then_inc(consts, 1)

            def norm_root(phase):
                for t in range(TT):
                    pool.wait_ge(sq_ready, TT * phase + t + 1)
                    link(nc.gpsimd.tensor_scalar(mean[:, 0:1], sumsq[:, t:t + 1], 1.0 / D, EPS, ALU.mult, ALU.add))
                    exponent = minus_one[:] if phase % 2 else minus_half[:, 0:1]
                    nc.gpsimd.tensor_tensor(rnorm[:, t:t + 1], mean[:, 0:1], exponent, ALU.pow).then_inc(rnorm_ready, 1)
                    pool.wait_ge(rnorm_ready, TT * phase + t + 1)

            norm_root(0)
            link(nc.gpsimd.memset(decay[:], 0.0))
            link(nc.gpsimd.memset(pick[:], 0.0))
            for i in range(3):
                link(nc.gpsimd.affine_select(out=pick[:], in_=pick[:], compare_op=ALU.not_equal, fill=1.0, base=-32 * i,
                                             pattern=[[-1, HEADS], [0, P]], channel_multiplier=1))
            link(nc.gpsimd.memset(level_mask[:], 0.0))
            for j in range(1, LEVELS):
                size = 2 ** (j - 1)
                blocks = P // (2 * size)
                right = level_mask[:, j, :].rearrange("p (b h w) -> p b h w", h=2, w=size)[:, :, 1, :]
                link(nc.gpsimd.memset(right, 1.0))
                link(nc.gpsimd.affine_select(out=right, in_=right, compare_op=ALU.is_ge, fill=0.0, base=0,
                                             pattern=[[-2 * size, blocks], [0, size]], channel_multiplier=1))
                link(nc.gpsimd.affine_select(out=right, in_=right, compare_op=ALU.is_ge, fill=0.0, base=size - 1,
                                             pattern=[[2 * size, blocks], [0, size]], channel_multiplier=-1))
            nc.gpsimd.tensor_copy(level_mask[:, 0, :], ident[:]).then_inc(consts, 1)
            def keys_and_queries(l, s):
                key, h = (l, *s), s[2]
                slot = bank_of(key) % 4
                z, sigmoid = wide[:, slot, :], half[:, slot, :]
                pool.wait_ge(sig_ready, plan.order["sig_ready", key])
                if s[1] == "q":
                    nc.gpsimd.tensor_tensor(qT[:, h, :], z, sigmoid, ALU.mult).then_inc(feat_ready, 1)
                    return
                if h == GROUP:
                    pool.wait_ge(level_q, plan.order["level_q", (l, "level", 0, 1)])
                    pool.wait_ge(level_k, plan.order["level_k", (l, "level", 0, 1)])
                pool.wait_ge(lower_ready, 1)
                link(nc.gpsimd.tensor_scalar(keep[:, h % GROUP, :], sigmoid, lower[:, 1, h:h + 1],
                                             lower[:, 0, h:h + 1], ALU.mult, ALU.add))
                nc.gpsimd.tensor_scalar(kT[:, h, :], keep[:, h % GROUP, :], -1.0, 1.0,
                                        ALU.mult, ALU.add).then_inc(feat_ready, 1)

            def decay_keys(l, g, j):
                for t in range(TT):
                    wait_full(pool, (l, "level", g, j, t))
                if j > 1:
                    pool.wait_ge(level_q, plan.order["level_q", (l, "level", g, j - 1)])
                size = 2 ** (j - 1)
                kv = kT[:, GROUP * g:GROUP * g + GROUP, :].rearrange("p h (b e w) -> p (h b) e w", e=2, w=size)
                sv = span_of(j - 1).rearrange("p (b e) -> p b e", e=2)
                nc.gpsimd.tensor_tensor(kv[:, :, 0, :], kv[:, :, 0, :],
                                        sv[:, :, 1:2].to_broadcast([P, GROUP * T // (2 * size), size]),
                                        ALU.mult).then_inc(level_k, 1)

            hg_n = 0
            for l, kind in enumerate(KIND):
                if l > 0:
                    norm_root(2 * l)
                if kind == "hgrn":
                    nc.gpsimd.memset(mixT, 0.0).then_inc(mixT_zeroed, 1)
                    for s in STEPS[kind]:
                        if s[0] == "feat":
                            keys_and_queries(l, s)
                        if s[0] == "level" and s[2] > 0:
                            decay_keys(l, s[1], s[2])
                        if s[0] != "mix":
                            continue
                        hg_n += 1
                        pool.wait_ge(hg_sum, hg_n)
                        link(nc.gpsimd.tensor_scalar(mean[:], hg_sumsq[:], 1.0 / P, EPS, ALU.mult, ALU.add))
                        nc.gpsimd.tensor_tensor(hg_rnorm[:], mean[:], minus_half[:], ALU.pow).then_inc(hg_rn, 1)
                        pool.wait_ge(hg_rn, hg_n)
                norm_root(2 * l + 1)
            norm_root(2 * DEPTH)

        @block.scalar
        def _(act):
            steps = [0]

            def link(ins):
                steps[0] += 1
                ins.then_inc(act_step, 1)
                act.wait_ge(act_step, steps[0])

            act.wait_ge(zeroed, 1)
            smalls = [(params[ROW_MIX:ROW_MIX + 32, :], norm_mix.rearrange("l (k p) -> (l k) p", p=P)),
                      (params[ROW_MLP:ROW_MLP + 32, :], norm_mlp.rearrange("l (k p) -> (l k) p", p=P)),
                      (params[ROW_LB:ROW_LB + 32, :], hgrn_lb_logits.rearrange("l (k p) -> (l k) p", p=P)),
                      (params[ROW_GN:ROW_GN + 8, :], hgrn_g_norm.rearrange("l (k p) -> (l k) p", p=P)),
                      (params2[0:16, :], fox_b_in[0, 0:2 * D].rearrange("(k p) -> k p", p=P))]
            for a in range(2):
                row = ROW_SWA + SWA_ROWS * a
                src = swa_b_qkv[a, 0:SWA_ROWS * P].rearrange("(k p) -> k p", p=P)
                smalls.append((params[row:row + SWA_ROWS, :], src))
            assert len(smalls) == SMALLS
            for dst, src in smalls:
                act.dma_start(dst, src).then_inc(small_full, 16)
            act.sem_inc(small_issued, 1)

            def round_unit(n):
                nc.scalar.activation(w_hi[:, n % RING, :], raw[:, n % RAWS, :], ACT.Copy).then_inc(hi_done, 1)

            def split_unit(n):
                if n >= RING:
                    wait_unit_used(act, n - RING)
                act.wait_ge(raw_full[n % RAWS], 16 * (n // RAWS + 1))
                round_unit(n)

            def sum_squares(phase, t):
                if phase == 0:
                    act.wait_ge(x_in_full, 16 * TT)
                else:
                    act.wait_ge(x_ready, x_count(phase, 2 * t + 1))
                nc.scalar.activation(rows[:, t, :], x[:, t, :], ACT.Square,
                                     accum_out=sumsq[:, t:t + 1]).then_inc(sq_ready, 1)

            def round_actT(name, l, gain_row, banks=range(4)):
                for b in banks:
                    key = (name, l, b)
                    if name == "outT" and KIND[l] != "hgrn":
                        wait_free(act, (l, "value", b - b % 2 + 1, b % 2))
                        nc.scalar.activation(actT[:, 2 * b:2 * b + 2, 0, :], o[:, 2 * b:2 * b + 2, :],
                                             ACT.Copy).then_inc(actT_hi, 1)
                        continue
                    wait_full(act, key)
                    if gain_row is None:
                        nc.scalar.activation(actT[:, 2 * b:2 * b + 2, 0, :], bank(key).rearrange("p (k t) -> p k t", k=2),
                                             ACT.Copy).then_inc(actT_hi, 1)
                    else:
                        for e in range(2):
                            k = 2 * b + e
                            last = nc.scalar.activation(actT[:, k, 0, :], bank(key, T, e * T), ACT.Copy,
                                                        scale=cols[:, gain_row + k:gain_row + k + 1])
                        last.then_inc(actT_hi, 1)

            def feature_tile(l, s):
                key = (l, *s)
                slot = bank_of(key) % 4
                wait_full(act, key)
                if KIND[l] == "hgrn" and plan.slot_before(key):
                    act.wait_ge(feat_ready, plan.slot_before(key))
                nc.scalar.activation(half[:, slot, :], bank(key, T, T), ACT.Copy).then_inc(half_ready, 1)
                act.wait_ge(wide_ready, plan.order["wide_ready", key])
                z = wide[:, slot, :]
                if KIND[l] == "hgrn":
                    nc.scalar.activation(half[:, slot, :], z, ACT.Sigmoid).then_inc(sig_ready, 1)
                elif s[1] == "q":
                    which = SWA_LAYERS.index(l) if KIND[l] == "swa" else 2
                    nc.scalar.activation(qT[:, s[2], :], z, ACT.Identity, bias=q_bias[:, which, s[2]:s[2] + 1],
                                         scale=Q_SCALE).then_inc(feat_ready, 1)
                elif KIND[l] == "fox":
                    nc.scalar.activation(kT[:, s[2], :], z, ACT.Identity,
                                         bias=foxcols[:, 8 + s[2]:9 + s[2]]).then_inc(feat_ready, 1)
                else:
                    c = ROW_SWA + SWA_ROWS * SWA_LAYERS.index(l) + 8 + s[2]
                    nc.scalar.activation(kT[:, s[2], :], z, ACT.Identity, bias=cols[:, c:c + 1])
                    nc.scalar.activation(kT[DH:P, 2 + s[2], :], wide[0:DH, slot, :], ACT.Identity, bias=cols[0:DH, c:c + 1])
                    nc.scalar.activation(kT[0:DH, 2 + s[2], :], wide[DH:P, slot, :], ACT.Identity,
                                         bias=cols[DH:P, c:c + 1]).then_inc(feat_ready, 1)

            def softmax(l, g):
                buf = g % 2
                act.wait_ge(max_ready, group_number(l, g) + 1)
                for b in range(3):
                    key = (l, "score", g, b)
                    for e in range(GROUP if b == 0 else 2):
                        h = e if b == 0 else 2 * (b - 1) + e
                        src = bank(key, P, e * P) if b == 0 else bank(key, T, e * T)
                        dst = probs[:, buf, h, 0:P] if b == 0 else probs[:, buf, h, P:3 * P]
                        c = h if b == 0 else GROUP + h
                        last = nc.scalar.activation(dst, src, ACT.Exp, bias=neg_max[:, buf, c:c + 1],
                                                    accum_out=denom[:, buf, c:c + 1])
                    last.then_inc(exp_ready, 1)
                if KIND[l] == "swa":
                    nc.scalar.activation(sink_exp[:, buf, :], sink_shift[:, buf, :], ACT.Exp).then_inc(sink_ready, 1)

            def turn(l, g):
                for b in range(3):
                    key = (l, "turn", g, b)
                    wait_full(act, key)
                    nc.scalar.activation(probsT[:, g % 2, b, :, :], bank(key).rearrange("p (h s) -> p h s", h=GROUP),
                                         ACT.Copy).then_inc(turned, 1)

            hg_n = 0
            for l, kind in enumerate(KIND):
                sum_squares(2 * l, 0)
                if l == 0:
                    act.wait_ge(cols_copied, 2)
                round_actT("normT", 2 * l, ROW_MIX + KT * l)
                if l == 0:
                    split_unit(0)
                    sum_squares(0, 1)
                    split_unit(1)
                    act.wait_ge(lb_shifted, 1)
                    nc.scalar.activation(lb[:, 0:DEPTH, :], lb[:, 0:DEPTH, :], ACT.Exp).then_inc(lb_exp, 1)
                    act.wait_ge(bias_ready, 1)
                else:
                    sum_squares(2 * l, 1)
                for s in STEPS[kind]:
                    key = (l, *s)
                    if s[0] == "round":
                        split_unit(MIX0[l] + s[1])
                    elif s[0] == "feat":
                        feature_tile(l, s)
                    elif s[0] == "root":
                        act.wait_ge(rnorm_ready, TT * (2 * l + 1))
                    elif s[0] == "outT":
                        if kind != "hgrn" and s[1] == 0:
                            wait_full(act, (l, *[m for m in STEPS[kind] if m[0] in ("feat", "tok")][-1]))
                        round_actT("outT", l, ROW_GN if kind == "hgrn" else None, (2 * s[1], 2 * s[1] + 1))
                    elif s[0] == "tok" and s[1] == "i":
                        wait_full(act, key)
                        nc.scalar.activation(v[:, s[3], s[2] * HALF:(s[2] + 1) * HALF], bank(key), ACT.Copy,
                                             scale=rnorm[:, s[3]:s[3] + 1]).then_inc(v_ready, 1)
                    elif s[0] == "tok" and s[1] == "g":
                        wait_full(act, key)
                        nc.scalar.activation(gate[:, s[3], s[2] * HALF:(s[2] + 1) * HALF], bank(key), ACT.Sigmoid,
                                             scale=rnorm[:, s[3]:s[3] + 1]).then_inc(sig_ready, 1)
                    elif s[0] == "gate":
                        act.wait_ge(gateT_ready, 1)
                        z = fox_tmp[:, 1, :]
                        link(nc.scalar.activation(fox_tmp[:, 2, :], z, ACT.Abs))
                        link(nc.scalar.activation(fox_tmp[:, 2, :], fox_tmp[:, 2, :], ACT.Exp, scale=-1.0))
                        nc.scalar.activation(fox_tmp[:, 3, :], fox_tmp[:, 2, :], ACT.Ln, bias=1.0).then_inc(gate_log, 1)
                    elif s[0] == "exp":
                        softmax(l, s[1])
                    elif s[0] == "value":
                        wait_full(act, (l, *s, 0))
                        nc.scalar.activation(o_of(s[1], 0), o_sums(l, s[1], 0), ACT.Copy).then_inc(o_ready_a, 1)
                    elif s[0] == "turn":
                        turn(l, s[1])
                    elif s[0] == "mix":
                        wait_full(act, key)
                        if hg_n:
                            act.wait_ge(hg_sum, hg_n)
                        hg_n += 1
                        nc.scalar.activation(wide[:, 0:2, :], bank(key).rearrange("p (a b) -> p a b", a=2),
                                             ACT.Square).then_inc(hg_sq, 1)
                sum_squares(2 * l + 1, 0)
                round_actT("normT", 2 * l + 1, ROW_MLP + KT * l)
                sum_squares(2 * l + 1, 1)
                if l == 0:
                    act.wait_ge(bcast_full, 16 * BCASTS)
                    nc.scalar.activation(gate_whi[:], gate_w[:], ACT.Copy).then_inc(gate_hi_done, 1)

                def mlp_pair(i, last):
                    def split_in_loop(j):
                        n = MLP0[l] + j
                        if j in (4, 5, 6, 7):
                            b, full = plan.full["up", l, 3]
                            act.wait_ge(bank_full[b], i * 2 + (full + (j - 4) // 2))
                        else:
                            before = j - 1 if j < 4 else j - 5
                            act.wait_ge(tail_used, i * 4 + (TAILS * l + before))
                        act.wait_ge(raw_full[n % RAWS], i * (8 // RAWS * 16) + 16 * (n // RAWS + 1))
                        round_unit(n)

                    split_in_loop(2)
                    for n in range(9):
                        if n < 8:
                            b, full = plan.full["up", l, n % 4]
                            act.wait_ge(bank_full[b], i * 2 + (full + n // 4))
                            nc.scalar.activation(half[:, n % 4, :], psum[:, b, T:2 * T], ACT.Copy).then_inc(half_ready, 1)
                        if n > 0:
                            act.wait_ge(wide_ready, i * 8 + (plan.order["wide_ready", (l, "mlp")] + n))
                            nc.scalar.activation(hidden[:, (n - 1) // 4, (n - 1) % 4, 0, :], wide[:, (n - 1) % 4, :],
                                                 ACT.Copy).then_inc(hid_hi, 1)
                        if n in (1, 3, 4):
                            split_in_loop({1: 3, 3: 4, 4: 5}[n])
                    for j in range(6, 8 if last else 10):
                        split_in_loop(j)

                with act.Fori(0, PAIRS - (l == DEPTH - 1)) as i:
                    mlp_pair(i, False)
                if l == DEPTH - 1:
                    mlp_pair(PAIRS - 1, True)
            act.dma_start(final_gain, norm_final.partition_broadcast(P)).then_inc(gain_full, 16)
            for t in range(TT):
                sum_squares(2 * DEPTH, t)

        @block.vector
        def _(dve):
            steps = [0]

            def link(ins):
                steps[0] += 1
                ins.then_inc(dve_step, 1)
                dve.wait_ge(dve_step, steps[0])

            def f32(ap):
                return ap.bitcast(F32)

            def rest_unit(n):
                nc.vector.tensor_tensor(w_lo[:, n % RING, :], raw[:, n % RAWS, :], f32(w_hi[:, n % RING, :]),
                                        ALU.subtract).then_inc(lo_done, 1)

            def split_unit(n):
                dve.wait_ge(hi_done, n + 1)
                rest_unit(n)

            def add_to_x(l, name, b):
                t, xs = b // 2, x[:, b // 2, (b % 2) * HALF:(b % 2 + 1) * HALF]
                if name == "mixed":
                    if b < 3:
                        wait_full(dve, (name, l, b))
                    else:
                        dve.wait_ge(tail_used, TAILS * l + 2)
                    nc.vector.tensor_tensor(xs, psum[:, b, :], xs, ALU.add).then_inc(x_ready, 1)
                    return
                if b == 0:
                    dve.wait_ge(rnorm_ready, TT * (2 * l + 2))
                    dve.wait_ge(down_tile0, PAIRS * (l + 1))
                if b == 2:
                    dve.wait_ge(tail_used, TAILS * (l + 1))
                nc.vector.scalar_tensor_tensor(xs, psum[:, b, :], rnorm[:, t:t + 1], xs, ALU.mult,
                                               ALU.add).then_inc(x_ready, 1)

            def rest_actT(name, l, turned, gain_row, banks=range(4)):
                for b in banks:
                    key = (name, 2 * l + turned // 2 if name == "normT" else l, b)
                    dve.wait_ge(actT_hi, turned_number(l, turned, b))
                    if gain_row is None:
                        nc.vector.tensor_tensor(actT[:, 2 * b:2 * b + 2, 1, :], o[:, 2 * b:2 * b + 2, :],
                                                f32(actT[:, 2 * b:2 * b + 2, 0, :]), ALU.subtract).then_inc(actT_lo, 1)
                    else:
                        for e in range(2):
                            k = 2 * b + e
                            last = nc.vector.scalar_tensor_tensor(
                                actT[:, k, 1, :], bank(key, T, e * T), cols[:, gain_row + k:gain_row + k + 1],
                                f32(actT[:, k, 0, :]), ALU.mult, ALU.subtract)
                        last.then_inc(actT_lo, 1)

            for c, (dst, width) in enumerate(((cols, P), (foxcols, 16))):
                wait_full(dve, ("param", c))
                nc.vector.tensor_copy(dst[:], bank(("param", c), width)).then_inc(cols_copied, 1)
            dve.wait_ge(cols_copied, 2)
            for a in range(2):
                row = ROW_SWA + SWA_ROWS * a
                nc.vector.tensor_scalar(q_bias[:, a, :], cols[:, row:row + 8], Q_SCALE, None, ALU.mult)
            nc.vector.tensor_scalar(q_bias[:, 2, :], foxcols[:, 0:8], Q_SCALE, None, ALU.mult).then_inc(bias_ready, 1)
            logits = cols[:, ROW_LB:ROW_LB + 32].rearrange("p (l h) -> p l h", l=DEPTH)
            link(nc.vector.tensor_reduce(lb[:, DEPTH, :], logits.rearrange("p l h -> p h l"), AX.X, ALU.max))
            nc.vector.tensor_tensor(lb[:, 0:DEPTH, :], logits,
                                    lb[:, DEPTH:DEPTH + 1, :].to_broadcast([P, DEPTH, HG_HEADS]),
                                    ALU.subtract).then_inc(lb_shifted, 1)

            rest_actT("normT", 0, 0, ROW_MIX)
            split_unit(0)
            split_unit(1)
            dve.wait_ge(bcast_full, 16 * BCASTS)
            nc.vector.tensor_scalar(neg_sinks[:], sinks[:], -1.0, None, ALU.mult)

            def lower_bounds():
                dve.wait_ge(lb_exp, 1)
                link(nc.vector.tensor_reduce(lb[:, DEPTH, :], lb[:, 0:DEPTH, :].rearrange("p l h -> p h l"), AX.X, ALU.add))
                link(nc.vector.reciprocal(lb[:, DEPTH + 1, :], lb[:, DEPTH, :]))
                link(nc.vector.tensor_tensor(lb[:, 0:DEPTH, :], lb[:, 0:DEPTH, :],
                                             lb[:, DEPTH + 1:DEPTH + 2, :].to_broadcast([P, DEPTH, HG_HEADS]), ALU.mult))
                total = lb[:, 0, :]
                for i in range(1, HG_LAYER + 1):
                    link(nc.vector.tensor_tensor(lb[:, DEPTH + 2, :], total, lb[:, i, :], ALU.add))
                    total = lb[:, DEPTH + 2, :]
                link(nc.vector.tensor_tensor(lower[:, 0, :], total, lb[:, 0, :], ALU.subtract))
                nc.vector.tensor_scalar(lower[:, 1, :], lower[:, 0, :], -1.0, 1.0, ALU.mult,
                                        ALU.add).then_inc(lower_ready, 1)

            dve.sem_inc(up_sum, 4)

            def feature_tile(l, s):
                key = (l, *s)
                slot = bank_of(key) % 4
                dve.wait_ge(half_ready, plan.order["half_ready", key])
                z, other = wide[:, slot, :], half[:, slot, :]
                nc.vector.tensor_tensor(z, bank(key, T), other, ALU.add).then_inc(feat_sum, 1)
                dve.wait_ge(feat_sum, plan.free[key][1])
                nc.vector.tensor_tensor(z, z, spread[:], ALU.mult).then_inc(wide_ready, 1)

            def level(l, g, j):
                heads = slice(GROUP * g, GROUP * g + GROUP)
                for t in range(TT):
                    wait_full(dve, (l, "level", g, j, t))
                if j == 0:
                    nc.vector.tensor_tensor(qT[:, heads, :], qT[:, heads, :], keep, ALU.mult).then_inc(level_q, 1)
                else:
                    dve.wait_ge(level_q, plan.order["level_q", (l, "level", g, j - 1)])
                    size = 2 ** (j - 1)
                    qv = qT[:, heads, :].rearrange("p h (b e w) -> p (h b) e w", e=2, w=size)
                    sv = span_of(j - 1).rearrange("p (b e) -> p b e", e=2)
                    last = nc.vector.tensor_tensor(qv[:, :, 1, :], qv[:, :, 1, :],
                                                   sv[:, :, 0:1].to_broadcast([P, GROUP * T // (2 * size), size]), ALU.mult)
                    if j < LEVELS - 1:
                        last = nc.vector.tensor_tensor(span_of(j), sv[:, :, 0], sv[:, :, 1], ALU.mult)
                    last.then_inc(level_q, 1)
                for t in range(TT):
                    key = (l, "level", g, j, t)
                    if j > 0:
                        wait_free(dve, (l, "level", g, j - 1, t))
                    mask = level_mask[:, j:j + 1, :].bitcast(I16).to_broadcast([P, GROUP, P])
                    nc.vector.copy_predicated(mixT[:, heads, t * P:(t + 1) * P], mask,
                                              bank(key).rearrange("p (h t) -> p h t", h=GROUP)).then_inc(level_out, 1)

            def max_of_scores(l, g):
                buf = g % 2
                for b in range(3):
                    key = (l, "score", g, b)
                    wait_full(dve, key)
                    heads = GROUP if b == 0 else 2
                    c = 0 if b == 0 else GROUP + 2 * (b - 1)
                    last = nc.vector.tensor_reduce(neg_max[:, buf, c:c + heads],
                                                   bank(key).rearrange("p (h s) -> p h s", h=heads),
                                                   AX.X, ALU.max, negate=True)
                if KIND[l] != "swa":
                    last.then_inc(max_ready, 1)
                    return
                link(last)
                a, first = SWA_LAYERS.index(l), 2 * GROUP * (g // 2) + g % 2
                hs = slice(first, first + 2 * GROUP - 1, 2)
                nm = neg_max[:, buf, :].rearrange("p (b h) -> p b h", b=2)
                link(nc.vector.tensor_tensor(nm, nm, neg_sinks[:, a:a + 1, hs].to_broadcast([P, 2, GROUP]), ALU.min))
                nc.vector.tensor_tensor(sink_shift[:, buf, :].rearrange("p (b h) -> p b h", b=2), nm,
                                        sinks[:, a:a + 1, hs].to_broadcast([P, 2, GROUP]), ALU.add).then_inc(max_ready, 1)

            def scale(l, g):
                buf = g % 2
                dve.wait_ge(exp_ready, 3 * (group_number(l, g) + 1))
                if KIND[l] == "swa":
                    which = GROUPS * SWA_LAYERS.index(l) + g
                    dve.wait_ge(sink_ready, which + 1)
                    link(nc.vector.tensor_tensor(denom[:, buf, :], denom[:, buf, :], sink_exp[:, buf, :], ALU.add))
                link(nc.vector.reciprocal(inv_denom[:, buf, :], denom[:, buf, :]))
                for h in range(GROUP):
                    for t, ks in enumerate((slice(0, P), slice(P, 3 * P))):
                        last = nc.vector.tensor_scalar(probs[:, buf, h, ks], probs[:, buf, h, ks],
                                                       inv_denom[:, buf, GROUP * t + h:GROUP * t + h + 1], None, ALU.mult)
                last.then_inc(probs_ready, 1)

            def forget_gates(l):
                link(nc.vector.memset(gate_rows, 0.0))
                key = (l, "gate")
                wait_full(dve, key)
                for t in range(TT):
                    last = nc.vector.scalar_tensor_tensor(gate_rows[:, t, 0:HEADS], bank(key, HEADS, t * HEADS),
                                                          rnorm[:, t:t + 1], gate_bias[:], ALU.mult, ALU.add)
                last.then_inc(gate_rows_ready, 1)
                key = (l, "gateT")
                wait_full(dve, key)
                z = fox_tmp[:, 1, :]
                nc.vector.tensor_copy(z, psum[0:HEADS, bank_of(key), 0:T]).then_inc(gateT_ready, 1)
                dve.wait_ge(gate_log, 1)
                link(nc.vector.tensor_scalar(z, z, 0.0, None, ALU.min))
                link(nc.vector.tensor_tensor(fox_tmp[:, 2, :], z, fox_tmp[:, 3, :], ALU.subtract))
                link(nc.vector.memset(fox_tmp[:, 3, :], 1.0))
                link(nc.vector.tensor_tensor_scan(z, fox_tmp[:, 3, :], fox_tmp[:, 2, :], 0.0, ALU.mult, ALU.add))
                link(nc.vector.tensor_scalar(z, z, -1.0, None, ALU.mult))
                dve.wait_ge(consts, 3)
                for i in range(3):
                    link(nc.vector.tensor_copy(part_tmp, z))
                    last = nc.vector.tensor_copy(decay[32 * i:32 * i + HEADS, :], part_tmp)
                    if i < 2:
                        link(last)
                        link(nc.vector.tensor_tensor(z, z, part_tmp, ALU.subtract))
                last.then_inc(decay_ready, 1)

            hg_n = 0
            for l, kind in enumerate(KIND):
                if l > 0:
                    rest_actT("normT", l, 0, ROW_MIX + KT * l)
                if kind == "hgrn":
                    dve.wait_ge(mixT_zeroed, 1)
                    dve.wait_ge(consts, 3)
                for s in STEPS[kind]:
                    key = (l, *s)
                    if s[0] == "rest":
                        split_unit(MIX0[l] + s[1])
                    elif s[0] == "spread":
                        wait_full(dve, (l, "root"))
                        nc.vector.tensor_copy(spread[:], bank((l, "root"), T)).then_inc(spread_ready, 1)
                        dve.wait_ge(spread_ready, l + 1)
                    elif s[0] == "outT":
                        rest_actT("outT", l, 1, ROW_GN if kind == "hgrn" else None, (2 * s[1], 2 * s[1] + 1))
                    elif s[0] == "proj" and s[1] == 1:
                        add_to_x(l, "mixed", s[2])
                    elif s[0] == "feat":
                        feature_tile(l, s)
                    elif s[0] == "tok" and s[1] == "v":
                        wait_full(dve, key)
                        if kind == "swa":
                            copies = v[:, s[3], 0:2 * KV_HEADS * DH].rearrange("p (h e n) -> p h e n", h=KV_HEADS, e=2)
                            bias = swa_v_bias[:, SWA_LAYERS.index(l), :].rearrange("p (h n) -> p h n", h=KV_HEADS)
                            src = bank(key, KV_HEADS * DH).rearrange("p (h n) -> p h n", h=KV_HEADS)
                            parts = [(copies[:, :, e, :], src, bias) for e in range(2)]
                        else:
                            cs = slice(s[2] * HALF, (s[2] + 1) * HALF)
                            parts = [(v[:, s[3], cs], bank(key), v_bias[:, cs])]
                        for dst, src, bias in parts:
                            last = nc.vector.scalar_tensor_tensor(dst, src, rnorm[:, s[3]:s[3] + 1], bias, ALU.mult, ALU.add)
                        last.then_inc(v_ready, 1)
                    elif s[0] == "tok" and s[1] == "g":
                        cs = slice(s[2] * HALF, (s[2] + 1) * HALF)
                        dve.wait_ge(sig_ready, plan.order["sig_ready", key])
                        nc.vector.scalar_tensor_tensor(gate[:, s[3], cs], bank(key), rnorm[:, s[3]:s[3] + 1],
                                                       gate[:, s[3], cs], ALU.mult, ALU.mult).then_inc(gate_ready, 1)
                    elif s[0] == "gate":
                        forget_gates(l)
                    elif s[0] == "max":
                        max_of_scores(l, s[1])
                    elif s[0] == "scale":
                        scale(l, s[1])
                    elif s[0] == "value":
                        wait_full(dve, (l, *s, 1))
                        nc.vector.tensor_copy(o_of(s[1], 1), o_sums(l, s[1], 1)).then_inc(o_ready_v, 1)
                    elif s[0] == "level":
                        level(l, s[1], s[2])
                    elif s[0] == "cross":
                        heads = slice(GROUP * s[1], GROUP * s[1] + GROUP)
                        wait_full(dve, key)
                        nc.vector.tensor_copy(crossT[:, heads, :],
                                              bank(key).rearrange("p (h t) -> p h t", h=GROUP)).then_inc(mixT_ready, 1)
                    elif s[0] == "mix":
                        g, t = s[1], s[2]
                        hg_n += 1
                        dve.wait_ge(hg_sq, hg_n)
                        nc.vector.tensor_reduce(hg_sumsq[:], wide[:, 0:2, :].rearrange("p a (h n) -> p (a h) n", n=P),
                                                AX.X, ALU.add).then_inc(hg_sum, 1)
                        dve.wait_ge(hg_rn, hg_n)
                        cs = slice(g * HALF, (g + 1) * HALF)
                        nc.vector.tensor_tensor(rows[:, t, cs].rearrange("p (h n) -> p h n", h=GROUP),
                                                bank(key).rearrange("p (h n) -> p h n", h=GROUP),
                                                hg_rnorm[:].unsqueeze(2).to_broadcast([P, GROUP, P]),
                                                ALU.mult).then_inc(hg_scaled, 1)
                        dve.wait_ge(hg_scaled, hg_n)
                        nc.vector.tensor_tensor(rows[:, t, cs], rows[:, t, cs], gate[:, t, cs],
                                                ALU.mult).then_inc(hg_rows, 1)
                if l == 0:
                    lower_bounds()
                rest_actT("normT", l, 2, ROW_MLP + KT * l)
                if l == 0:
                    dve.wait_ge(gate_hi_done, 1)
                    nc.vector.tensor_tensor(gate_wlo[:], gate_w[:], f32(gate_whi[:]), ALU.subtract).then_inc(gate_split, 1)

                def rest_hidden(i, n):
                    dve.wait_ge(hid_hi, i * 8 + (UP_TILES * l + n + 1))
                    nc.vector.tensor_tensor(hidden[:, n // 4, n % 4, 1, :], wide[:, n % 4, :],
                                            f32(hidden[:, n // 4, n % 4, 0, :]), ALU.subtract).then_inc(hid_lo, 1)

                def mlp_pair(i, last):
                    def split_in_loop(j):
                        n = MLP0[l] + j
                        dve.wait_ge(hi_done, i * 8 + (n + 1))
                        rest_unit(n)

                    split_in_loop(2)
                    for n in range(9):
                        if n < 8:
                            b, f = bank_of(("up", l, n % 4)), n % 4
                            dve.wait_ge(half_ready, i * 8 + (plan.order["half_ready", (l, "mlp")] + n + 1))
                            nc.vector.tensor_tensor(half[:, f, :], psum[:, b, 0:T], half[:, f, :],
                                                    ALU.add).then_inc(up_sum, 1)
                        if n > 0:
                            rest_hidden(i, n - 1)
                        if n < 8:
                            dve.wait_ge(up_sum, i * 8 + (4 + UP_TILES * l + n + 1))
                            nc.vector.scalar_tensor_tensor(wide[:, f, :], half[:, f, :], 0.0, half[:, f, :],
                                                           ALU.max, ALU.mult).then_inc(wide_ready, 1)
                        if n in (1, 3, 4):
                            split_in_loop({1: 3, 3: 4, 4: 5}[n])
                    for j in range(6, 8 if last else 10):
                        split_in_loop(j)

                with dve.Fori(0, PAIRS - (l == DEPTH - 1)) as i:
                    mlp_pair(i, False)
                if l == DEPTH - 1:
                    mlp_pair(PAIRS - 1, True)
                for b in range(4):
                    add_to_x(l, "down", b)
            dve.wait_ge(gain_full, 16)
            for t in range(TT):
                dve.wait_ge(rnorm_ready, TT * 2 * DEPTH + t + 1)
                nc.vector.scalar_tensor_tensor(rows[:, t, :], x[:, t, :], rnorm[:, t:t + 1], final_gain,
                                               ALU.mult, ALU.mult).then_inc(rows_ready, 1)

        @block.tensor
        def _(pe):
            def take_bank(key):
                if plan.before[key]:
                    wait_free(pe, plan.before[key])
                return bank_of(key)

            def weight(ring, n, k, width, start, size):
                return ring[:, n % RING, k * width + start:k * width + start + size]

            def norm_transposes(phase):
                for t in range(TT):
                    for b in range(4):
                        key = ("normT", phase, b)
                        if phase == 0:
                            pe.wait_ge(x_in_full, 16 * TT)
                        else:
                            pe.wait_ge(x_ready, x_count(phase, 2 * t + b // 2))
                        if t == 0:
                            take_bank(key)
                        for e in range(2):
                            k = 2 * b + e
                            last = nc.tensor.transpose(bank(key, P, e * T + t * P), x[:, t, k * P:(k + 1) * P], ident[:])
                        if t == TT - 1:
                            last.then_inc(bank_full[bank_of(key)], 1)
                    if phase % 2:
                        for b in (2 * t, 2 * t + 1):
                            take_bank(("down", phase // 2, b))
                            nc.tensor.matmul(psum[:, b, :].rearrange("p (a n) -> p a n", a=4), ident_h[:],
                                             masks[:, 3:4, :].to_broadcast([P, 4, P]), start=True, stop=True)

            def out_transposes(l, part):
                for t in range(TT):
                    pe.wait_ge(hg_rows, 4 * GATES.index(l) + 2 * part + t + 1)
                    for b in (2 * part, 2 * part + 1):
                        key = ("outT", l, b)
                        if t == 0:
                            take_bank(key)
                        for e in range(2):
                            k = 2 * b + e
                            last = nc.tensor.transpose(bank(key, P, e * T + t * P), rows[:, t, k * P:(k + 1) * P],
                                                       ident[:])
                        if t == TT - 1:
                            last.then_inc(bank_full[bank_of(key)], 1)

            def wait_actT(l, turned, k):
                if k % 2 == 0:
                    pe.wait_ge(actT_lo, turned_number(l, turned, k // 2))

            def feature_major(b, cols_of, wait_act, wait_weights):
                for k in range(KT):
                    wait_act(k)
                    if k % 4 == 0:
                        wait_weights(k // 4)
                    hi, lo = cols_of(w_hi, k), cols_of(w_lo, k)
                    both = actT[:, k, :, :].rearrange("p a t -> p (a t)")
                    if k == 0:
                        nc.tensor.matmul(psum[:, b, :], hi, both, start=True, stop=False)
                    last = nc.tensor.matmul(psum[:, b, 0:T], lo, actT[:, k, 0, :], start=False, stop=False)
                    if k > 0:
                        last = nc.tensor.matmul(psum[:, b, :], hi, both, start=False, stop=k == KT - 1)
                return last

            def token_major(dst, lhs, rhs_hi, rhs_lo, start, stop, skip=False):
                nc.tensor.matmul(dst, lhs[0], rhs_hi, start=start, stop=False, skip_group_check=skip)
                nc.tensor.matmul(dst, lhs[0], rhs_lo, start=False, stop=False, skip_group_check=skip)
                return nc.tensor.matmul(dst, lhs[1], rhs_hi, start=False, stop=stop, skip_group_check=skip)

            def act_lhs(k, t):
                return [actT[:, k, a, t * P:(t + 1) * P] for a in range(2)]

            def score(l, g):
                kind = KIND[l]
                needed = [("feat", c, 4 * (g // 2) + 3) for c in ("q" if kind == "swa" else "qk")]
                for s in needed:
                    pe.wait_ge(feat_ready, plan.order["feat_ready", (l, *s)])
                if kind == "fox":
                    pe.wait_ge(decay_ready, 1)
                for b in range(3):
                    key = (l, "score", g, b)
                    take_bank(key)
                    for e in range(GROUP if b == 0 else 2):
                        j = e if b == 0 else 2 * (b - 1) + e
                        keys = P if b == 0 else T
                        dst = bank(key, keys, e * keys)
                        part, qt = slice(DH * (g % 2), DH * (g % 2) + DH), 4 * (g // 2) + j
                        kt = qt
                        if kind == "swa":
                            kv = (2 * qt + g % 2) // (HEADS // KV_HEADS)
                            kt = kv // 2 if kv % 2 == g % 2 else 2 + kv // 2
                        if kind == "fox":
                            nc.tensor.matmul(dst, pick[:, 2 * qt + g % 2, :], decay[:, 0:keys],
                                             start=e == 0, stop=False, skip_group_check=True)
                        t = 0 if b == 0 else 1
                        nc.tensor.matmul(dst, qT[part, qt, t * P:(t + 1) * P], kT[part, kt, 0:keys],
                                         start=e == 0 and kind == "swa", stop=False, skip_group_check=True)
                    mask = masks[:, 0:1, :] if b == 0 else masks[:, 1:3, :] if kind == "swa" else masks[:, 3:5, :]
                    mask = mask.rearrange("p a s -> p (a s)").unsqueeze(1)
                    heads, keys = (GROUP, P) if b == 0 else (2, T)
                    nc.tensor.matmul(bank(key).rearrange("p (h s) -> p h s", h=heads), ident_h[:],
                                     mask.to_broadcast([P, heads, keys]), start=False, stop=True,
                                     skip_group_check=True).then_inc(bank_full[b], 1)

            def turn(l, g):
                pe.wait_ge(probs_ready, group_number(l, g) + 1)
                for b in range(3):
                    key = (l, "turn", g, b)
                    take_bank(key)
                    for h in range(GROUP):
                        last = nc.tensor.transpose(bank(key, P, h * P), probs[:, g % 2, h, b * P:(b + 1) * P], ident[:])
                    last.then_inc(bank_full[bank_of(key)], 1)

            def value(l, g):
                for b in range(3):
                    wait_free(pe, (l, "turn", g, b))
                wait_free(pe, (l, "tok", "v", 0 if KIND[l] == "swa" else g // 2, 1))
                for i in range(2):
                    key = (l, "value", g, i)
                    take_bank(key)
                    for e in range(2):
                        h = 2 * i + e
                        k = GROUP * (g // 2) + h
                        cs = k // 2 if KIND[l] == "swa" else k
                        vc = [v[:, t, cs * P:(cs + 1) * P] for t in range(TT)]
                        nc.tensor.matmul(bank(key, T, e * T).rearrange("p (b s) -> p b s", b=2), vc[0],
                                         probsT[:, g % 2, 0:2, h, :], start=e == 0, stop=False, skip_group_check=True)
                        last = nc.tensor.matmul(bank(key, P, e * T + P), vc[1], probsT[:, g % 2, 2, h, :],
                                                start=False, stop=True, skip_group_check=True)
                    last.then_inc(bank_full[bank_of(key)], 1)

            def level(l, g, j):
                if j == 0:
                    pe.wait_ge(feat_ready, plan.order["feat_ready", (l, "feat", "f", GROUP * g + GROUP - 1)])
                else:
                    pe.wait_ge(level_q, plan.order["level_q", (l, "level", g, j - 1)])
                    if j > 1:
                        pe.wait_ge(level_k, plan.order["level_k", (l, "level", g, j - 1)])
                for t in range(TT if j < LEVELS else 1):
                    key = (l, "level", g, j, t) if j < LEVELS else (l, "cross", g)
                    take_bank(key)
                    s_tile = slice(t * P, (t + 1) * P)
                    t_tile = s_tile if j < LEVELS else slice(P, T)
                    for h in range(GROUP):
                        last = nc.tensor.matmul(bank(key, P, h * P), kT[:, GROUP * g + h, s_tile],
                                                qT[:, GROUP * g + h, t_tile], start=True, stop=True)
                    last.then_inc(bank_full[bank_of(key)], 1)

            def mix(l, g, t):
                key = (l, "mix", g, t)
                take_bank(key)
                wait_free(pe, (l, "level", g, LEVELS - 1, TT - 1))
                wait_free(pe, (l, "cross", g))
                wait_free(pe, (l, "tok", "i", g, 1))
                for h in range(GROUP):
                    head = GROUP * g + h
                    dst = bank(key, P, h * P)
                    vc = [v[:, a, head * P:(head + 1) * P] for a in range(TT)]
                    if t == 1:
                        nc.tensor.matmul(dst, crossT[:, head, :], vc[0], start=True, stop=False)
                    last = nc.tensor.matmul(dst, mixT[:, head, t * P:(t + 1) * P], vc[t], start=t == 0, stop=True)
                last.then_inc(bank_full[bank_of(key)], 1)

            def project(l, part, b, frees):
                t, e = b // 2, b % 2
                if part == 0:
                    take_bank(("mixed", l, b))
                for k in range(4 * part, 4 * part + 4):
                    n = OUT0[l] + k // 2
                    if k % 2 == 0:
                        pe.wait_ge(lo_done, n + 1)
                    wait_actT(l, 1, k)
                    rhs = [weight(r, n, k % 2, D, e * HALF, HALF) for r in (w_hi, w_lo)]
                    last = token_major(psum[:, b, :], act_lhs(k, t), *rhs, k == 0, k == KT - 1)
                    if frees and k % 2 == 1:
                        last.then_inc(out_used, 1)
                    if part == 1 and b == 3 and k % 2 == 1:
                        last.then_inc(tail_used, 1)
                if part == 1 and b < 3:
                    last.then_inc(bank_full[b], 1)

            pe.wait_ge(consts, 1)
            norm_transposes(0)
            pe.wait_ge(small_full, 16 * SMALLS)
            for c, src in enumerate((params, params2)):
                key = ("param", c)
                nc.tensor.transpose(bank(key, P), src, ident[:]).then_inc(bank_full[take_bank(key)], 1)
            pe.wait_ge(consts, 2)
            for _ in range(WARM_UP):
                nc.tensor.matmul(psum[:, 3, :].rearrange("p (a n) -> p a n", a=4), ident_h[:],
                                 masks[:, 3:4, :].to_broadcast([P, 4, P]), start=True, stop=True)

            for l, kind in enumerate(KIND):
                if l > 0:
                    norm_transposes(2 * l)
                parts = [s for s in STEPS[kind] if s[:2] == ("proj", 0)]
                for s in STEPS[kind]:
                    key = (l, *s)
                    if s[0] in ("feat", "tok"):
                        n = MIX0[l] + 2 * CHUNK_OF[kind](s)
                        b = take_bank(key)
                    if s[0] == "feat":
                        def cols_of(ring, k, n=n, j=s[2] % 4):
                            return weight(ring, n + k // 4, k % 4, HALF, j * P, P)

                        last = feature_major(b, cols_of, lambda k: wait_actT(l, 0, k),
                                             lambda u, n=n: pe.wait_ge(lo_done, n + u + 1))
                        last.then_inc(bank_full[b], 1)
                    elif s[0] == "tok":
                        start, width = (256, 256) if kind == "swa" else (0, HALF)
                        for k in range(KT):
                            if k % 4 == 0:
                                pe.wait_ge(lo_done, n + k // 4 + 1)
                            rhs = [weight(r, n + k // 4, k % 4, HALF, start, width) for r in (w_hi, w_lo)]
                            last = token_major(psum[:, b, 0:width], act_lhs(k, s[3]), *rhs, k == 0, k == KT - 1)
                        last.then_inc(bank_full[b], 1)
                    elif s[0] == "gate":
                        b = take_bank(key)
                        pe.wait_ge(gate_split, 1)
                        for t in range(TT):
                            for k in range(KT):
                                wait_actT(l, 0, k)
                                last = token_major(psum[:, b, t * HEADS:(t + 1) * HEADS], act_lhs(k, t),
                                                   gate_whi[:, k, :], gate_wlo[:, k, :], k == 0, k == KT - 1)
                        last.then_inc(bank_full[b], 1)
                        b = take_bank((l, "gateT"))
                        pe.wait_ge(gate_rows_ready, 1)
                        for t in range(TT):
                            last = nc.tensor.transpose(psum[:, b, t * P:(t + 1) * P], gate_rows[:, t, :], ident[:])
                        last.then_inc(bank_full[b], 1)
                    elif s[0] == "root":
                        b = take_bank(key)
                        pe.wait_ge(rnorm_ready, TT * (2 * l + 1))
                        for t in range(TT):
                            last = nc.tensor.matmul(psum[:, b, t * P:(t + 1) * P], rnorm[:, t:t + 1].to_broadcast([P, P]),
                                                    ident[:], start=True, stop=True)
                        last.then_inc(bank_full[b], 1)
                    elif s[0] == "outT" and kind == "hgrn":
                        out_transposes(l, s[1])
                    elif s[0] == "proj":
                        project(l, s[1], s[2], s == parts[-1])
                    elif s[0] == "score":
                        score(l, s[1])
                    elif s[0] == "turn":
                        turn(l, s[1])
                    elif s[0] == "value":
                        value(l, s[1])
                    elif s[0] == "level":
                        level(l, s[1], s[2])
                    elif s[0] == "cross":
                        level(l, s[1], LEVELS)
                    elif s[0] == "mix":
                        mix(l, s[1], s[2])
                norm_transposes(2 * l + 1)
                with pe.Fori(0, PAIRS) as i:
                    for ab in range(2):
                        n = MLP0[l] + 2 * ab
                        for f in range(4):
                            b = bank_of(("up", l, f))
                            pe.wait_ge(up_sum, i * 8 + (UP_TILES * l + 4 * ab + f + 1))
                            last = feature_major(b, lambda ring, k: weight(ring, n + k // 4, k % 4, HALF, f * P, P),
                                                 lambda k: wait_actT(l, 2, k),
                                                 lambda u: pe.wait_ge(lo_done, i * 8 + (n + u + 1)))
                            last.then_inc(bank_full[b], 1)
                    for ab in range(2):
                        for t in range(TT):
                            for u in range(2):
                                n = MLP0[l] + 4 + 2 * ab + u
                                pe.wait_ge(lo_done, i * 8 + (n + 1))
                                for kk in range(2):
                                    k = 2 * u + kk
                                    if t == 0:
                                        pe.wait_ge(hid_lo, i * 8 + (UP_TILES * l + 4 * ab + k + 1))
                                    lhs = [hidden[:, ab, k, a, t * P:(t + 1) * P] for a in range(2)]
                                    for e in range(2):
                                        rhs = [weight(r, n, kk, D, e * HALF, HALF) for r in (w_hi, w_lo)]
                                        last = token_major(psum[:, 2 * t + e, :], lhs, *rhs, False, True, skip=True)
                                if t == 1:
                                    last.then_inc(tail_used, 1)
                                elif ab == 1 and u == 1:
                                    last.then_inc(down_tile0, 1)


_INS = ["x", "norm_mix", "norm_mlp", "norm_final", "w_up", "w_down", "swa_w_qkv", "swa_b_qkv", "swa_sinks", "swa_w_o",
        "hgrn_w_in", "hgrn_lb_logits", "hgrn_g_norm", "hgrn_w_o", "fox_w_in", "fox_b_in", "fox_w_o"]


def kernel(**inputs):
    import numpy as np
    import concourse.bacc as bacc
    from concourse.bass_utils import run_bass_kernel_spmd

    nc = bacc.Bacc("TRN2", target_bir_lowering=False, num_devices=1)
    arrays, args = {}, []
    for name in _INS:
        a = np.ascontiguousarray(inputs[name])
        arrays[f"in_{name}"] = a
        args.append(nc.dram_tensor(f"in_{name}", a.shape, mybir.dt.from_np(a.dtype), kind="ExternalInput").ap())
    args.append(nc.dram_tensor("out", (1, T, D), F32, kind="ExternalOutput").ap())
    build_trunk(nc, *args)
    result = run_bass_kernel_spmd(nc, [arrays], core_ids=[0])
    return result.results[0]["out"]
```
